# Optimizing a Trainium2 kernel written in Bass

```python
import math
import jax, jax.numpy as jnp
from jax import lax
import numpy as np

D_MODEL = 1024
BATCH = 1
SEQ = 512
DEPTH = 1

MEM_LEN = 256
BLOCK_Q = 128
SB_HEADS = 8
SB_HEAD_DIM = 64
DF_HEADS = 4
DF_HEAD_DIM = 64
MX_HEADS = 4
MX_HEAD_DIM = 128
SB_WIDTH = SB_HEADS * SB_HEAD_DIM
DF_WIDTH = DF_HEADS * 2 * DF_HEAD_DIM
MX_WIDTH = MX_HEADS * MX_HEAD_DIM
IN_WIDTH = 3 * SB_WIDTH + 3 * DF_WIDTH + MX_WIDTH
N_BRANCH = 3
ROPE_THETA = 500000.0
ROPE_DIM = DF_HEAD_DIM // 4
PEER_HEADS = 8
PEER_NKEYS = 128
PEER_EXPERTS = PEER_NKEYS * PEER_NKEYS
PEER_TOPK = 16
PEER_QDIM = 256
PEER_HALF = PEER_QDIM // 2
PEER_CHUNK = 128
LN_EPS = 1e-5
RMS_EPS = 1e-5
DEEPNORM_ALPHA = (2.0 * DEPTH) ** 0.25
DEEPNORM_BETA = (8.0 * DEPTH) ** -0.25

kernel_name = "hybrid_sb_diff_mem_peer_block"

def layer_norm(x, g, b):
    xf = x.astype(jnp.float32)
    mu = jnp.mean(xf, axis=-1, keepdims=True)
    var = jnp.mean(jnp.square(xf - mu), axis=-1, keepdims=True)
    return ((xf - mu) * lax.rsqrt(var + LN_EPS) * g.astype(jnp.float32) + b.astype(jnp.float32)).astype(x.dtype)

def rope_tables(positions):
    inv = ROPE_THETA ** (-jnp.arange(0, ROPE_DIM, 2, dtype=jnp.float32) / ROPE_DIM)
    ang = positions.astype(jnp.float32)[..., None] * inv
    return jnp.cos(ang), jnp.sin(ang)

def apply_partial_rotary(x, cos, sin):
    xr, xp = x[..., :ROPE_DIM], x[..., ROPE_DIM:]
    x1, x2 = xr[..., :ROPE_DIM // 2], xr[..., ROPE_DIM // 2:]
    rot = jnp.concatenate([x1 * cos - x2 * sin, x2 * cos + x1 * sin], axis=-1).astype(x.dtype)
    return jnp.concatenate([rot, xp], axis=-1)

def stick_breaking_attention(q, k, v):
    B, H, S, d = q.shape
    nb = S // BLOCK_Q
    scale = d ** -0.5
    key_pos = jnp.arange(S)
    qb = q.reshape(B, H, nb, BLOCK_Q, d).transpose(2, 0, 1, 3, 4)

    def block(args):
        q_blk, i = args
        qpos = i * BLOCK_Q + jnp.arange(BLOCK_Q)
        z = jnp.einsum('bhqd,bhkd->bhqk', q_blk, k, preferred_element_type=jnp.float32) * scale
        causal = key_pos[None, :] < qpos[:, None]
        log_beta = jax.nn.log_sigmoid(z)
        log_one_minus = jnp.where(causal, jax.nn.log_sigmoid(-z), 0.0)
        rest = lax.cumsum(log_one_minus, axis=log_one_minus.ndim - 1, reverse=True) - log_one_minus
        a = jnp.where(causal, jnp.exp(log_beta + rest), 0.0)
        return jnp.einsum('bhqk,bhkd->bhqd', a.astype(v.dtype), v)

    out = lax.map(block, (qb, jnp.arange(nb)))
    return out.transpose(1, 2, 0, 3, 4).reshape(B, H, S, d)

def differential_attention(q, k, v, lam):
    B, H, _, S, d = q.shape
    nb = S // BLOCK_Q
    scale = d ** -0.5
    key_pos = jnp.arange(S)
    qb = q.reshape(B, H, 2, nb, BLOCK_Q, d).transpose(3, 0, 1, 2, 4, 5)

    def block(args):
        q_blk, i = args
        qpos = i * BLOCK_Q + jnp.arange(BLOCK_Q)
        s = jnp.einsum('bhmqd,bhmkd->bhmqk', q_blk, k, preferred_element_type=jnp.float32) * scale
        s = jnp.where(key_pos[None, :] <= qpos[:, None], s, -jnp.inf)
        p = jax.nn.softmax(s, axis=-1)
        attn = p[:, :, 0] - lam * p[:, :, 1]
        return jnp.einsum('bhqk,bhkd->bhqd', attn.astype(v.dtype), v)

    out = lax.map(block, (qb, jnp.arange(nb)))
    return out.transpose(1, 2, 0, 3, 4).reshape(B, H, S, 2 * d)

def memory_cross_attention(q, k, v):
    scale = q.shape[-1] ** -0.5
    s = jnp.einsum('bshd,bmhd->bhsm', q, k, preferred_element_type=jnp.float32) * scale
    p = jax.nn.softmax(s, axis=-1)
    return jnp.einsum('bhsm,bmhd->bshd', p.astype(v.dtype), v)

def peer_ffn(x, w_query, sub_keys, u_tab, v_tab):
    B, S, D = x.shape
    nc = S // PEER_CHUNK
    xc = x.reshape(B, nc, PEER_CHUNK, D).transpose(1, 0, 2, 3)

    def chunk(xb):
        C = xb.shape[1]
        q = (xb @ w_query).reshape(B, C, PEER_HEADS, 2, PEER_HALF)
        s = jnp.einsum('bchpd,hpnd->bchpn', q, sub_keys, preferred_element_type=jnp.float32)
        top_s, top_i = lax.top_k(s, PEER_TOPK)
        cand_s = top_s[..., 0, :, None] + top_s[..., 1, None, :]
        cand_i = top_i[..., 0, :, None] * PEER_NKEYS + top_i[..., 1, None, :]
        cand_s = cand_s.reshape(B, C, PEER_HEADS, PEER_TOPK * PEER_TOPK)
        cand_i = cand_i.reshape(B, C, PEER_HEADS, PEER_TOPK * PEER_TOPK)
        best_s, best_pos = lax.top_k(cand_s, PEER_TOPK)
        ids = jnp.take_along_axis(cand_i, best_pos, axis=-1)
        g = jax.nn.softmax(best_s, axis=-1)
        ids = ids.reshape(B, C, PEER_HEADS * PEER_TOPK)
        g = g.reshape(B, C, PEER_HEADS * PEER_TOPK)
        u = jnp.take(u_tab, ids, axis=0)
        v = jnp.take(v_tab, ids, axis=0)
        h = jnp.einsum('bcd,bced->bce', xb, u, preferred_element_type=jnp.float32)
        a = jax.nn.gelu(h, approximate=False) * g
        return jnp.einsum('bce,bced->bcd', a.astype(v.dtype), v)

    out = lax.map(chunk, xc)
    return out.transpose(1, 0, 2, 3).reshape(B, S, D)

def setup_inputs(seed: int = 0) -> dict:
    key = jax.random.key(seed)
    ks = jax.random.split(key, 24)
    f32 = jnp.float32
    nrm = lambda k, shape, s: jax.random.normal(k, shape, f32) * s
    D = D_MODEL
    x = nrm(ks[0], (BATCH, SEQ, D), 1.0)
    mem = nrm(ks[1], (BATCH, MEM_LEN, D), 1.0)
    offset = jax.random.randint(ks[2], (BATCH, 1), 0, 1024, dtype=jnp.int32)
    positions = offset + jnp.arange(SEQ, dtype=jnp.int32)[None, :]
    return {
        "x": x,
        "mem": mem,
        "positions": positions,
        "w_in": nrm(ks[3], (DEPTH, D, IN_WIDTH), D ** -0.5),
        "w_mem_kv": nrm(ks[4], (DEPTH, D, 2 * MX_WIDTH), D ** -0.5),
        "df_lambda": nrm(ks[5], (DEPTH, 4, DF_HEAD_DIM), 0.1),
        "df_norm_g": 1.0 + nrm(ks[6], (DEPTH, 2 * DF_HEAD_DIM), 0.02),
        "w_gate": nrm(ks[7], (DEPTH, D, N_BRANCH * D), D ** -0.5),
        "b_gate": nrm(ks[8], (DEPTH, N_BRANCH * D), 0.02),
        "w_br_sb": nrm(ks[9], (DEPTH, SB_WIDTH, D), SB_WIDTH ** -0.5),
        "w_br_df": nrm(ks[10], (DEPTH, DF_WIDTH, D), DF_WIDTH ** -0.5),
        "w_br_mx": nrm(ks[11], (DEPTH, MX_WIDTH, D), MX_WIDTH ** -0.5),
        "w_out": nrm(ks[12], (DEPTH, D, D), DEEPNORM_BETA * D ** -0.5),
        "ln1_g": 1.0 + nrm(ks[13], (DEPTH, D), 0.02),
        "ln1_b": nrm(ks[14], (DEPTH, D), 0.02),
        "w_query": nrm(ks[15], (DEPTH, D, PEER_HEADS * PEER_QDIM), D ** -0.5),
        "sub_keys": nrm(ks[16], (DEPTH, PEER_HEADS, 2, PEER_NKEYS, PEER_HALF), PEER_HALF ** -0.5),
        "u_tab": nrm(ks[17], (DEPTH, PEER_EXPERTS, D), D ** -0.5),
        "v_tab": nrm(ks[18], (DEPTH, PEER_EXPERTS, D), DEEPNORM_BETA),
        "ln2_g": 1.0 + nrm(ks[19], (DEPTH, D), 0.02),
        "ln2_b": nrm(ks[20], (DEPTH, D), 0.02),
    }

def reference(x, mem, positions, w_in, w_mem_kv, df_lambda, df_norm_g, w_gate, b_gate,
              w_br_sb, w_br_df, w_br_mx, w_out, ln1_g, ln1_b, w_query, sub_keys,
              u_tab, v_tab, ln2_g, ln2_b):
    B, S, D = x.shape
    M = mem.shape[1]
    cos, sin = rope_tables(positions)
    cos = cos[:, :, None, None, :]
    sin = sin[:, :, None, None, :]
    for l in range(DEPTH):
        lambda_init = 0.8 - 0.6 * math.exp(-0.3 * l)
        h = x
        proj = h @ w_in[l]
        sb_q, sb_k, sb_v, df_q, df_k, df_v, mx_q = jnp.split(
            proj, [SB_WIDTH, 2 * SB_WIDTH, 3 * SB_WIDTH,
                   3 * SB_WIDTH + DF_WIDTH, 3 * SB_WIDTH + 2 * DF_WIDTH,
                   3 * SB_WIDTH + 3 * DF_WIDTH], axis=-1)
        to_heads = lambda t: t.reshape(B, S, SB_HEADS, SB_HEAD_DIM).transpose(0, 2, 1, 3)
        o_sb = stick_breaking_attention(to_heads(sb_q), to_heads(sb_k), to_heads(sb_v))
        o_sb = o_sb.transpose(0, 2, 1, 3).reshape(B, S, SB_WIDTH)
        df_q = apply_partial_rotary(df_q.reshape(B, S, DF_HEADS, 2, DF_HEAD_DIM), cos, sin)
        df_k = apply_partial_rotary(df_k.reshape(B, S, DF_HEADS, 2, DF_HEAD_DIM), cos, sin)
        df_v = df_v.reshape(B, S, DF_HEADS, 2 * DF_HEAD_DIM).transpose(0, 2, 1, 3)
        lam_p = df_lambda[l].astype(jnp.float32)
        lam = (jnp.exp(jnp.sum(lam_p[0] * lam_p[1])) - jnp.exp(jnp.sum(lam_p[2] * lam_p[3]))
               + lambda_init)
        o_df = differential_attention(df_q.transpose(0, 2, 3, 1, 4), df_k.transpose(0, 2, 3, 1, 4),
                                      df_v, lam)
        o_df_f = o_df.astype(jnp.float32)
        o_df_f = o_df_f * lax.rsqrt(jnp.mean(jnp.square(o_df_f), axis=-1, keepdims=True) + RMS_EPS)
        o_df = (o_df_f * df_norm_g[l].astype(jnp.float32) * (1.0 - lambda_init)).astype(x.dtype)
        o_df = o_df.transpose(0, 2, 1, 3).reshape(B, S, DF_WIDTH)
        mem_k, mem_v = jnp.split(mem @ w_mem_kv[l], 2, axis=-1)
        o_mx = memory_cross_attention(mx_q.reshape(B, S, MX_HEADS, MX_HEAD_DIM),
                                      mem_k.reshape(B, M, MX_HEADS, MX_HEAD_DIM),
                                      mem_v.reshape(B, M, MX_HEADS, MX_HEAD_DIM))
        o_mx = o_mx.reshape(B, S, MX_WIDTH)
        gates = jax.nn.sigmoid(h @ w_gate[l] + b_gate[l]).reshape(B, S, N_BRANCH, D)
        merged = (gates[:, :, 0] * (o_sb @ w_br_sb[l])
                  + gates[:, :, 1] * (o_df @ w_br_df[l])
                  + gates[:, :, 2] * (o_mx @ w_br_mx[l]))
        mix = merged @ w_out[l]
        x = layer_norm(DEEPNORM_ALPHA * x + mix, ln1_g[l], ln1_b[l])
        ffn = peer_ffn(x, w_query[l], sub_keys[l], u_tab[l], v_tab[l])
        x = layer_norm(DEEPNORM_ALPHA * x + ffn, ln2_g[l], ln2_b[l])
    return x


_drawn_inputs = setup_inputs


def setup_inputs(seed=0):
    import zlib

    import numpy as np

    out = dict(_drawn_inputs(seed))
    spreads = {}
    factors = {'df_norm_g': 3.083, 'b_gate': 4.426, 'ln2_g': 2.837, 'ln2_b': 2.949}
    for name, (base, spread) in spreads.items():
        noise = np.random.default_rng([zlib.crc32(name.encode()), seed]).standard_normal(out[name].shape)
        drawn = base * np.exp(spread * noise) if base else spread * noise
        out[name] = __import__('jax').numpy.asarray(drawn.astype(out[name].dtype))
    for name, factor in factors.items():
        out[name] = (out[name] * factor).astype(out[name].dtype)
    return out
```

```python
from contextlib import ExitStack

import concourse.bass as bass
from concourse import mybir

F32 = mybir.dt.float32
BF16 = mybir.dt.bfloat16
U32 = mybir.dt.uint32
I32 = mybir.dt.int32
ALU = mybir.AluOpType
ACT = mybir.ActivationFunctionType
AX_X = mybir.AxisListType.X

P = 128
T = 512
NT = T // P
D = 1024
KD = D // P
M = 256
NM = M // P
HD = 64
ROUNDS = 4
SEGS = 9
SBQ, SBK, SBV, DFQ, DFK, DFV, MXQ, MXK, MXV = range(SEGS)
UNITS = [SBQ, SBK, SBV, DFQ, DFK, "swap_q", "swap_k", DFV, MXQ, MXK, MXV]
NU = len(UNITS)
NB = 3
FT = D // P
HEADS = 8
NK = 128
TOPK = 16
RING = 8
GROUP = 2
LAMBDA_INIT = 0.8 - 0.6
LN_EPS = 1e-5
RMS_EPS = 1e-5
ALPHA = 2.0 ** 0.25
QSCALE = HD ** -0.5
MXSCALE = 128 ** -0.5
SCORES = 5 * NT
CONST_LOADS = 6
REGION_B = 15104
TWO_PI = 6.283185307179586
PI_A = 6.28125
PI_B = 0.0019350051879882812
PI_C = TWO_PI - PI_A - PI_B
ROUND_MAGIC = 12582912.0
PI_TOP = 3.1415925
NEG_BIG = -3.0e38

WIDTH = [T - P * kb for kb in range(NT)]
OFF = [sum(WIDTH[:kb]) for kb in range(NT)]
CAUSAL = sum(WIDTH)

C_IDENT, C_TRI, C_ONES, C_PERM = 0, P, 2 * P, 3 * P
C_INV = 4 * P
C_SIGN = C_INV + 1
C_EPS = C_INV + 2
C_ONE = C_INV + 3
C_IOTA = C_INV + 4
NCONST = C_IOTA + TOPK


class Steps:

    def __init__(self):
        self.base, self.k = 0, 0

    def add(self):
        self.k += 1
        return 1

    def value(self):
        return self.base + self.k

    def enter(self, i, per):
        self.start, self.per = self.base + self.k, per
        self.base, self.k = i * per + self.start, 0

    def leave(self, trips):
        assert self.k == self.per, (self.k, self.per)
        self.base, self.k = self.start + trips * self.per, 0


def build_layer(nc, xT_d, x_d, memT_d, pos_d, w_mix_d, lam_d, df_g_d, w_gate_d, b_gate_d, w_br_d,
                w_out_d, ln_d, w_query_d, keysT_d, uv_d, const_d, masks_d, out_d):
    ctx = ExitStack()
    with ctx:
        def sb(name, shape, dt=F32):
            return ctx.enter_context(nc.sbuf_tensor(name, shape, dt))

        def sem(name):
            return ctx.enter_context(nc.semaphore(name))

        region_a = sb("region_a", [P, RING * 2 * D])
        w_seg = [region_a[:, s * D:(s + 1) * D].rearrange("p (k c) -> p k c", k=KD) for s in range(SEGS)]
        w_out = region_a[:, 0:KD * D].rearrange("p (k n) -> p k n", k=KD)
        rows = region_a[:, :].rearrange("p (r c) -> p r c", r=RING)
        at = SEGS * D
        memT = region_a[:, at:at + KD * M].rearrange("p (k m) -> p k m", k=KD)
        at += KD * M
        rope_cos = region_a[:, at:at + T]
        rope_sin = region_a[:, at + T:at + 2 * T]
        rope_k = region_a[:, at + 2 * T:at + 3 * T]
        rope_r = region_a[:, at + 3 * T:at + 4 * T]
        at += 4 * T
        df_raw = [region_a[:, at + j * T:at + (j + 1) * T] for j in range(2)]
        at += 2 * T
        assert at <= RING * 2 * D

        region_b = sb("region_b", [P, REGION_B])
        at = 0

        def part(n):
            nonlocal at
            at += n
            assert at <= REGION_B
            return region_b[:, at - n:at]

        sb_qT, sb_kT, sb_v, df_v, mx_qT = part(T), part(T), part(T), part(T), part(T)
        mem_kT, mem_v = part(M), part(M)
        softplus = [part(CAUSAL) for _ in range(2)]
        sb_aT = [part(CAUSAL) for _ in range(2)]
        soft_e = [part(T) for _ in range(2)]
        soft_l = [part(T) for _ in range(2)]
        df_p = [[part(T) for _ in range(2)] for _ in range(2)]
        df_pT = part(T)
        mx_pT = part(M)
        df_sq, df_on = part(T), part(T)
        mx_p = [part(M) for _ in range(2)]
        swapped = part(T)
        pos_i = swapped.bitcast(I32)
        at = 0
        x_nat = part(NT * D).rearrange("p (t d) -> p t d", t=NT)
        ln1_gb = part(2 * D).rearrange("p (j d) -> p j d", j=2)
        at = 0
        acc = part(NT * D).rearrange("p (t d) -> p t d", t=NT)
        ln2_gb = part(2 * D).rearrange("p (j d) -> p j d", j=2)
        w_q = part(2 * D).rearrange("p (u k c) -> p u k c", u=2, k=KD)
        keysT = part(2 * NK).rearrange("p (u n) -> p u n", u=2)
        peer_qT = part(2 * T).rearrange("p (u t) -> p u t", u=2)
        score = part(NT * 2 * NK).rearrange("p (t u n) -> p t u n", t=NT, u=2)
        score_cut = part(2 * NK).rearrange("p (u n) -> p u n", u=2)
        cand, cand_cut = part(TOPK * TOPK), part(TOPK * TOPK)
        onehot = part(2 * TOPK * TOPK).rearrange("p (u e i) -> p u e i", u=2, e=TOPK)
        diag = part(RING * P).rearrange("p (e c) -> p e c", e=RING)

        at = 0
        part(NT * D + 2 * D)
        gate = part(NB * T).rearrange("p (b t) -> p b t", b=NB)
        part_sum = part(NB * T).rearrange("p (b t) -> p b t", b=NB)
        xT = sb("xT", [P, KD, T])
        oT = sb("oT", [P, NB * ROUNDS * T])
        o_branch = oT[:, :].rearrange("p (b i t) -> p b i t", b=NB, i=ROUNDS)
        x1T = oT[:, 0:KD * T].rearrange("p (k t) -> p k t", k=KD)
        x1 = xT[:, :, :].rearrange("p k t -> p (k t)").rearrange("p (t d) -> p t d", t=NT)
        mergedT = sb("mergedT", [P, FT, T])
        w_gate = sb("w_gate", [P, NB, KD, P])
        w_br = sb("w_br", [P, NB, ROUNDS, P])
        b_gate = sb("b_gate", [P, NB, FT])
        const = sb("const", [P, NCONST])
        masks = sb("masks", [P, 3, P], BF16)
        df_g = sb("df_g", [P, 1])
        df_g8 = sb("df_g8", [P, 1])
        lam_in = sb("lam_in", [P, 4, HD])
        lam_pr = sb("lam_pr", [P, 2, HD])
        lam_s = sb("lam_s", [P, 2])
        lam_e = sb("lam_e", [P, 2])
        neg_lam = sb("neg_lam", [P, 1])
        neg_max = sb("neg_max", [P, 3 * NT])
        expsum = sb("expsum", [P, 3 * NT])
        exprec = sb("exprec", [P, 3 * NT])
        df_ss = sb("df_ss", [P, NT])
        df_ln = sb("df_ln", [P, NT])
        df_rms = sb("df_rms", [P, NT])
        stats = sb("stats", [P, NT, 2, 6])
        mean_var = sb("mean_var", [P, NT, 2])
        ln_v = sb("ln_v", [P, NT])
        ln_l = sb("ln_l", [P, NT])
        ln_r = sb("ln_r", [P, NT])
        ln_t = sb("ln_t", [P, NT])
        ln_u = sb("ln_u", [P, NT])
        top_v = sb("top_v", [P, 2, TOPK])
        top_i = sb("top_i", [P, 2, TOPK], U32)
        top_f = sb("top_f", [P, 2, TOPK])
        best_v = sb("best_v", [P, TOPK])
        best_i = sb("best_i", [P, TOPK], U32)
        best_ij = sb("best_ij", [P, 2, TOPK], U32)
        best_f = sb("best_f", [P, 2, TOPK])
        chosen = sb("chosen", [P, 2, TOPK])
        neg_best = sb("neg_best", [P, 1])
        best_e = sb("best_e", [P, TOPK])
        best_z = sb("best_z", [P, 1])
        best_r = sb("best_r", [P, 1])
        ids = sb("ids", [P, NT, TOPK], U32)
        weight = sb("weight", [P, NT, TOPK])
        hid = sb("hid", [P, NT, TOPK])
        gel = sb("gel", [P, NT, TOPK])
        act_w = sb("act_w", [P, NT, TOPK])

        ident = const[:, C_IDENT:C_IDENT + P]
        neg_tri = const[:, C_TRI:C_TRI + P]
        neg_ones = const[:, C_ONES:C_ONES + P]
        swap_perm = const[:, C_PERM:C_PERM + P]
        eps = const[:, C_EPS:C_EPS + 1]
        one = const[:, C_ONE:C_ONE + 1]
        iota16 = const[:, C_IOTA:C_IOTA + TOPK]
        inv_freq = const[:, C_INV:C_INV + 1]
        rope_sign = const[:, C_SIGN:C_SIGN + 1]

        bank = [ctx.enter_context(nc.psum_tensor(f"bank{b}", [P, 512], F32)) for b in range(8)]
        PROJ, SOFT, SCORE = bank[0:2], bank[2:4], bank[4:6]
        TURN = [bank[6], bank[3]]
        SUM, MXOUT = bank[7], bank[2]
        GATE, BRANCH = [bank[0], bank[1], bank[4]], [bank[5], bank[2], bank[3]]
        MIX = [[bank[0], bank[1]], [bank[4], bank[5]]]
        XTURN = [bank[2], bank[3]]
        VSUM = [[bank[0], bank[1]], [bank[4], bank[5]]]
        QUERY = [bank[2], bank[3]]
        KEYSCORE = [bank[6], bank[7]]

        const_loaded, xT_loaded, memT_loaded = sem("const_loaded"), sem("xT_loaded"), sem("memT_loaded")
        w_loaded = [sem(f"w_loaded{s}") for s in range(SEGS)]
        unit_done, unit_used = sem("unit_done"), sem("unit_used")
        z_ready, softlog_ready, softplus_ready = sem("z_ready"), sem("softlog_ready"), sem("softplus_ready")
        score_ready, score_used = sem("score_ready"), sem("score_used")
        negmax_ready, probs_ready = sem("negmax_ready"), sem("probs_ready")
        turned, turned_copied = sem("turned"), sem("turned_copied")
        sb_out_done, sb_out_copied = sem("sb_out_done"), sem("sb_out_copied")
        df_out_done, rms_ready, normed_ready = sem("df_out_done"), sem("rms_ready"), sem("normed_ready")
        mx_out_done, mx_out_used = sem("mx_out_done"), sem("mx_out_used")
        dve_step, act_step, choose_step = sem("dve_step"), sem("act_step"), sem("choose_step")
        angle_ready, sines_ready, lam_ready, lam_exp = (sem("angle_ready"), sem("sines_ready"),
                                                        sem("lam_ready"), sem("lam_exp"))
        wg_loaded = [sem(f"wg_loaded{b}") for b in range(NB)]
        wb_loaded = [sem(f"wb_loaded{b}") for b in range(NB)]
        gate_done, gate_ready = sem("gate_done"), sem("gate_ready")
        branch_done, branch_used = sem("branch_done"), sem("branch_used")
        merged_ready = sem("merged_ready")
        wout_loaded, xnat_loaded, ln1_loaded, ln2_loaded = (sem("wout_loaded"), sem("xnat_loaded"),
                                                            sem("ln1_loaded"), sem("ln2_loaded"))
        mix_done, mix_used = sem("mix_done"), sem("mix_used")
        var_ready, rstd_ready, x1_ready = sem("var_ready"), sem("rstd_ready"), sem("x1_ready")
        x1_turned, x1T_ready, acc_ready = sem("x1_turned"), sem("x1T_ready"), sem("acc_ready")
        wq_loaded, keys_loaded = sem("wq_loaded"), sem("keys_loaded")
        query_done, query_copied = sem("query_done"), sem("query_copied")
        keyscore_done, keyscore_copied = sem("keyscore_done"), sem("keyscore_copied")
        negbest_ready, bestexp_ready, chosen_ready = sem("negbest_ready"), sem("bestexp_ready"), sem("chosen_ready")
        row_loaded = [sem(f"row_loaded{r}") for r in range(RING)]
        row_used = sem("row_used")
        hid_ready, gelu_ready, actw_ready, diag_ready = (sem("hid_ready"), sem("gelu_ready"),
                                                         sem("actw_ready"), sem("diag_ready"))
        vsum_used = sem("vsum_used")
        gathers_begun, choices_begun = sem("gathers_begun"), sem("choices_begun")
        out_ready, out_stored = sem("out_ready"), sem("out_stored")

        block = ctx.enter_context(nc.Block())

        @block.sync
        def _(sp):
            def load_seg(i, s):
                sp.dma_start(w_seg[s], w_mix_d[i, s]).then_inc(w_loaded[s], 16)

            sp.dma_start(const[:, :], const_d).then_inc(const_loaded, 16)
            sp.dma_start(pos_i, pos_d.partition_broadcast(P)).then_inc(const_loaded, 16)
            load_seg(0, SBQ)
            for k in range(KD):
                sp.dma_start(xT[:, k, :], xT_d[k * P:(k + 1) * P, :]).then_inc(xT_loaded, 16)
            sp.dma_start(masks[:, :, :], masks_d).then_inc(const_loaded, 16)
            load_seg(0, SBK)
            sp.dma_start(lam_in[:, :, :].rearrange("p a b -> p (a b)"),
                         lam_d.partition_broadcast(P)).then_inc(const_loaded, 16)
            sp.dma_start(df_g[:, :], df_g_d).then_inc(const_loaded, 16)
            sp.dma_start(b_gate[:, :, :], b_gate_d).then_inc(const_loaded, 16)
            for s in range(SBV, SEGS):
                load_seg(0, s)
            sp.dma_start(memT, memT_d).then_inc(memT_loaded, 16)
            for b in range(NB):
                sp.dma_start(w_gate[:, b], w_gate_d[0, b]).then_inc(wg_loaded[b], 16)
                sp.dma_start(w_br[:, b], w_br_d[0, b]).then_inc(wb_loaded[b], 16)
            with sp.Fori(1, ROUNDS) as i:
                for s in range(SEGS):
                    sp.wait_ge(unit_done, i * NU - NU + UNITS.index(s) + 1)
                    load_seg(i, s)
            sp.wait_ge(unit_done, ROUNDS * NU)
            sp.dma_start(w_out, w_out_d).then_inc(wout_loaded, 16)
            sp.wait_ge(mx_out_used, ROUNDS + 1)
            sp.dma_start(x_nat, x_d).then_inc(xnat_loaded, 16)
            for j in range(2):
                sp.dma_start(ln1_gb[:, j, :], ln_d[j].partition_broadcast(P)).then_inc(ln1_loaded, 16)
            with sp.Fori(1, FT) as f:
                for b in range(NB):
                    sp.wait_ge(gate_done, f * NB - NB + b + 1)
                    sp.dma_start(w_gate[:, b], w_gate_d[f, b]).then_inc(wg_loaded[b], 16)
                    sp.wait_ge(branch_done, f * NB - NB + b + 1)
                    sp.dma_start(w_br[:, b], w_br_d[f, b]).then_inc(wb_loaded[b], 16)
            sp.wait_ge(merged_ready, FT)
            sp.dma_start(w_q, w_query_d[0]).then_inc(wq_loaded, 16)
            sp.dma_start(keysT, keysT_d[0]).then_inc(keys_loaded, 16)
            sp.wait_ge(x1_ready, NT)
            for j in range(2):
                sp.dma_start(ln2_gb[:, j, :], ln_d[2 + j].partition_broadcast(P)).then_inc(ln2_loaded, 16)
            with sp.Fori(1, HEADS) as h:
                sp.wait_ge(keyscore_done, h * 2)
                sp.dma_start(w_q, w_query_d[h]).then_inc(wq_loaded, 16)
                sp.dma_start(keysT, keysT_d[h]).then_inc(keys_loaded, 16)
            for t in range(NT):
                sp.wait_ge(out_ready, t + 1)
                sp.dma_start(out_d[:, t, :], acc[:, t, :]).then_inc(out_stored, 16)
            sp.wait_ge(out_stored, 16 * NT)

        @block.gpsimd
        def _(pool):
            def gather_tile(h, t):
                pool.wait_ge(chosen_ready, h * NT + t + 1)
                for e in range(TOPK):
                    n = (h * NT + t) * TOPK + e
                    pool.wait_ge(row_used, n + 1)
                    pool.sem_inc(gathers_begun, 1)
                    pool.indirect_dma_start(rows[:, e % RING, :], None, uv_d,
                                            bass.IndirectOffsetOnAxis(ap=ids[:, t, e:e + 1], axis=0)
                                            ).then_inc(row_loaded[e % RING], 16)

            pool.wait_ge(mix_done, NT)
            with pool.Fori(0, HEADS) as h:
                for t in range(NT):
                    gather_tile(h, t)

        @block.tensor
        def _(pe):
            def project(i, u):
                seg = UNITS[u]
                out = PROJ[u % 2]
                pe.wait_ge(unit_used, i * NU + (u + 2 if u == 0 else u + 1))
                if seg in ("swap_q", "swap_k"):
                    raw = UNITS.index(DFQ if seg == "swap_q" else DFK)
                    pe.wait_ge(unit_used, i * NU + raw + 1 + 2)
                    mm = pe.matmul(out[:, :], swap_perm, df_raw[seg == "swap_k"], start=True, stop=True)
                    mm.then_inc(unit_done, 1)
                    return
                pe.wait_ge(w_loaded[seg], i * 16 + 16)
                w = w_seg[seg]
                if seg in (SBV, DFV):
                    for t in range(NT):
                        for k in range(KD):
                            mm = pe.matmul(out[:, t * P:(t + 1) * P], xT[:, k, t * P:(t + 1) * P], w[:, k, :],
                                           start=(k == 0), stop=(k == KD - 1))
                elif seg == MXV:
                    for t in range(NM):
                        for k in range(KD):
                            mm = pe.matmul(out[:, t * P:(t + 1) * P], memT[:, k, t * P:(t + 1) * P], w[:, k, :],
                                           start=(k == 0), stop=(k == KD - 1))
                elif seg == MXK:
                    pe.wait_ge(memT_loaded, 16)
                    for k in range(KD):
                        mm = pe.matmul(out[:, 0:M], w[:, k, :], memT[:, k, :], start=(k == 0), stop=(k == KD - 1))
                else:
                    for k in range(KD):
                        mm = pe.matmul(out[:, :], w[:, k, :], xT[:, k, :], start=(k == 0), stop=(k == KD - 1))
                mm.then_inc(unit_done, 1)

            def head_scores(out, a, kb, stop):
                r = slice(a * HD, (a + 1) * HD)
                pe.matmul(out[:, 0:WIDTH[kb]], sb_kT[r, kb * P:(kb + 1) * P], sb_qT[r, kb * P:T],
                          start=True, stop=False)
                return pe.matmul(out[:, 0:P], masks[:, 0, :], masks[:, 1, :], start=False, stop=stop)

            def z_block(i, a, kb):
                n = a * NT + kb
                if n == 0:
                    pe.wait_ge(unit_used, i * NU + 2 + 2)
                    pe.wait_ge(mx_out_used, i + 1)
                pe.wait_ge(softplus_ready, i * 2 * NT + n + 1)
                head_scores(SOFT[n % 2], a, kb, True).then_inc(z_ready, 1)

            def stick_block(i, a, kb):
                n = a * NT + kb
                pe.wait_ge(softplus_ready, i * 2 * NT + (a + 1) * NT + 2)
                pe.wait_ge(score_used, i * SCORES + n + 1)
                out = SCORE[n % 2]
                head_scores(out, a, kb, False)
                mm = pe.matmul(out[:, 0:WIDTH[kb]], neg_tri, softplus[a][:, OFF[kb]:OFF[kb] + WIDTH[kb]],
                               start=False, stop=(kb == NT - 1))
                for later in range(kb + 1, NT):
                    mm = pe.matmul(out[:, (later - kb) * P:WIDTH[kb]], neg_ones,
                                   softplus[a][:, OFF[later]:OFF[later] + WIDTH[later]],
                                   start=False, stop=(later == NT - 1))
                mm.then_inc(score_ready, 1)

            def stick_sum(i):
                pe.wait_ge(score_used, i * SCORES + 2 * NT + 2)
                for a in range(2):
                    for kb in range(NT):
                        mm = pe.matmul(SUM[a * HD:(a + 1) * HD, kb * P:T], sb_v[:, kb * P + a * HD:kb * P + (a + 1) * HD],
                                       sb_aT[a][:, OFF[kb]:OFF[kb] + WIDTH[kb]], start=(kb == 0), stop=(kb == NT - 1))
                mm.then_inc(sb_out_done, 1)

            def df_scores(i, t, m):
                n = 2 * NT + 3 * t + m
                pe.wait_ge(score_used, i * SCORES + n + 1)
                r = slice(m * HD, (m + 1) * HD)
                w = (t + 1) * P
                pe.matmul(SCORE[n % 2][:, 0:w], df_raw[0][r, t * P:w], df_raw[1][r, 0:w], start=True, stop=False)
                pe.matmul(SCORE[n % 2][:, t * P:w], masks[:, 0, :], masks[:, 2, :],
                          start=False, stop=True).then_inc(score_ready, 1)

            def mx_scores(i, t):
                n = 2 * NT + 3 * t + 2
                pe.wait_ge(score_used, i * SCORES + n + 1)
                pe.matmul(SCORE[n % 2][:, 0:M], mx_qT[:, t * P:(t + 1) * P], mem_kT, start=True,
                          stop=True).then_inc(score_ready, 1)

            def tile_scores(i, t):
                df_scores(i, t, 0)
                df_scores(i, t, 1)
                mx_scores(i, t)

            def turn_and_sum(i, t):
                pe.wait_ge(probs_ready, i * 2 * NT + 2 * t + 1)
                for kb in range(t + 1):
                    mm = pe.transpose(TURN[0][:, kb * P:(kb + 1) * P], df_p[t % 2][0][:, kb * P:(kb + 1) * P], ident)
                mm.then_inc(turned, 1)
                pe.wait_ge(probs_ready, i * 2 * NT + 2 * t + 2)
                for kb in range(NM):
                    mm = pe.transpose(TURN[1][:, kb * P:(kb + 1) * P], mx_p[t % 2][:, kb * P:(kb + 1) * P], ident)
                mm.then_inc(turned, 1)
                if t == 0:
                    pe.wait_ge(sb_out_copied, i + 1)
                pe.wait_ge(turned_copied, i * (2 * NT + 1) + 2 * t + 1)
                for kb in range(t + 1):
                    mm = pe.matmul(SUM[:, t * P:(t + 1) * P], df_pT[:, kb * P:(kb + 1) * P],
                                   df_v[:, kb * P:(kb + 1) * P], start=(kb == 0), stop=(kb == t))
                mm.then_inc(df_out_done, 1)
                pe.wait_ge(turned_copied, i * (2 * NT + 1) + 2 * t + 2)
                for kb in range(NM):
                    mm = pe.matmul(MXOUT[:, t * P:(t + 1) * P], mem_v[:, kb * P:(kb + 1) * P],
                                   mx_pT[:, kb * P:(kb + 1) * P], start=(kb == 0), stop=(kb == NM - 1))
                if t == NT - 1:
                    mm.then_inc(mx_out_done, 1)

            pe.wait_ge(const_loaded, 16 * CONST_LOADS)
            pe.wait_ge(xT_loaded, 16 * KD)
            with pe.Fori(0, ROUNDS) as i:
                project(i, 0)
                project(i, 1)
                project(i, 2)
                z_block(i, 0, 0)
                z_block(i, 0, 1)
                project(i, 3)
                z_block(i, 0, 2)
                z_block(i, 0, 3)
                project(i, 4)
                z_block(i, 1, 0)
                z_block(i, 1, 1)
                project(i, 5)
                project(i, 6)
                project(i, 7)
                z_block(i, 1, 2)
                z_block(i, 1, 3)
                stick_block(i, 0, 0)
                stick_block(i, 0, 1)
                project(i, 8)
                stick_block(i, 0, 2)
                stick_block(i, 0, 3)
                project(i, 9)
                stick_block(i, 1, 0)
                stick_block(i, 1, 1)
                project(i, 10)
                stick_block(i, 1, 2)
                stick_block(i, 1, 3)
                tile_scores(i, 0)
                stick_sum(i)
                for t in range(1, NT):
                    tile_scores(i, t)
                    turn_and_sum(i, t - 1)
                turn_and_sum(i, NT - 1)
                pe.wait_ge(normed_ready, i + 1)
                for t in range(NT):
                    mm = pe.transpose(TURN[0][:, t * P:(t + 1) * P], df_on[:, t * P:(t + 1) * P], ident)
                mm.then_inc(turned, 1)

            pe.wait_ge(mx_out_used, ROUNDS + 1)
            with pe.Fori(0, FT) as f:
                for b in range(NB):
                    pe.wait_ge(wg_loaded[b], f * 16 + 16)
                    pe.wait_ge(gate_ready, f * NB + b + 1)
                    for k in range(KD):
                        mm = pe.matmul(GATE[b][:, :], w_gate[:, b, k, :], xT[:, k, :], start=(k == 0), stop=(k == KD - 1))
                    mm.then_inc(gate_done, 1)
                    pe.wait_ge(wb_loaded[b], f * 16 + 16)
                    pe.wait_ge(branch_used, f * NB + b + 1)
                    for k in range(ROUNDS):
                        mm = pe.matmul(BRANCH[b][:, :], w_br[:, b, k, :], o_branch[:, b, k, :],
                                       start=(k == 0), stop=(k == ROUNDS - 1))
                    mm.then_inc(branch_done, 1)

            pe.wait_ge(wout_loaded, 16)
            pe.wait_ge(merged_ready, FT)

            def turn_x1(t):
                pe.wait_ge(x1_ready, t + 1)
                pe.wait_ge(x1T_ready, 2 * t + 1)
                for k in range(KD):
                    mm = pe.transpose(XTURN[k // 4][:, (k % 4) * P:(k % 4 + 1) * P], x1[:, t, k * P:(k + 1) * P], ident)
                    if k % 4 == 3:
                        mm.then_inc(x1_turned, 1)

            for t in range(NT):
                pe.wait_ge(mix_used, t + 1)
                for n in range(2):
                    for f in range(FT):
                        mm = pe.matmul(MIX[t % 2][n][:, :], mergedT[:, f, t * P:(t + 1) * P],
                                       w_out[:, f, n * 512:(n + 1) * 512], start=(f == 0), stop=(f == FT - 1))
                mm.then_inc(mix_done, 1)
                if t >= 1:
                    turn_x1(t - 1)
            turn_x1(NT - 1)

            def query_matmuls(h, first, n):
                for j in range(first, first + n):
                    u, k = j // KD, j % KD
                    if j == 0:
                        pe.wait_ge(wq_loaded, h * 16 + 16)
                    mm = pe.matmul(QUERY[u][:, :], w_q[:, u, k, :], x1T[:, k, :], start=(k == 0), stop=(k == KD - 1))
                    if k == KD - 1:
                        mm.then_inc(query_done, 1)

            def key_scores(h, half, head=1):
                if half == 0:
                    pe.wait_ge(keys_loaded, h * 16 + 16)
                    pe.wait_ge(query_copied, h * 2 + 2)
                    if head > 0:
                        pe.wait_ge(keyscore_copied, h * 2)
                for t in (2 * half, 2 * half + 1):
                    for u in range(2):
                        c = (t % 2) * 2 * NK + u * NK
                        mm = pe.matmul(KEYSCORE[half][:, c:c + NK], peer_qT[:, u, t * P:(t + 1) * P], keysT[:, u, :],
                                       start=True, stop=True)
                mm.then_inc(keyscore_done, 1)

            def sum_rows(h, t, e):
                pe.wait_ge(diag_ready, (h * NT + t) * TOPK + e + 1)
                if e == 0:
                    pe.wait_ge(vsum_used, h * NT + t + 1)
                for n in range(2):
                    mm = pe.matmul(VSUM[t % 2][n][:, :], diag[:, e % RING, :],
                                   rows[:, e % RING, D + n * 512:D + (n + 1) * 512],
                                   start=(e == 0), stop=(e == TOPK - 1))
                mm.then_inc(row_used, 1)

            def experts(h, ahead):
                for t in range(NT):
                    for e in range(TOPK):
                        sum_rows(h, t, e)
                        if ahead and t == 0 and e < 8:
                            query_matmuls(h + 1, 2 * e, 2)
                        if ahead and t == 0 and e in (9, 10):
                            key_scores(h + 1, e - 9)

            pe.sem_inc(row_used, RING)
            pe.wait_ge(x1T_ready, 2 * NT + 1)
            pe.wait_ge(mix_used, NT + 2)
            query_matmuls(0, 0, 2 * KD)
            key_scores(0, 0, head=0)
            key_scores(0, 1, head=0)
            with pe.Fori(0, HEADS - 1) as h:
                experts(h, True)
            experts(HEADS - 1, False)

        @block.scalar
        def _(act):
            steps = Steps()
            act.wait_ge(const_loaded, 16 * CONST_LOADS)
            act.wait_ge(angle_ready, 1)
            act.activation(rope_sin, rope_r, ACT.Sin).then_inc(sines_ready, 1)
            act.wait_ge(angle_ready, 2)
            act.activation(rope_cos, rope_k, ACT.Sin).then_inc(sines_ready, 1)
            act.wait_ge(lam_ready, 1)
            act.activation(lam_e[:, :], lam_s[:, :], ACT.Exp).then_inc(lam_exp, 1)
            act.sem_inc(score_used, 2)

            def softlog(i, a, kb):
                n = a * NT + kb
                w = WIDTH[kb]
                act.wait_ge(z_ready, i * 2 * NT + n + 1)
                act.wait_ge(softplus_ready, i * 2 * NT + n + 1)
                act.activation(soft_e[n % 2][:, 0:w], SOFT[n % 2][:, 0:w], ACT.Abs).then_inc(act_step, steps.add())
                act.wait_ge(act_step, steps.value())
                act.activation(soft_l[n % 2][:, 0:w], soft_e[n % 2][:, 0:w], ACT.Exp,
                               scale=-1.0).then_inc(act_step, steps.add())
                act.wait_ge(act_step, steps.value())
                act.activation(soft_e[n % 2][:, 0:w], soft_l[n % 2][:, 0:w], ACT.Ln,
                               bias=one).then_inc(softlog_ready, 1)

            def stick_weights(i, a, kb):
                n = a * NT + kb
                act.wait_ge(score_ready, i * SCORES + n + 1)
                act.activation(sb_aT[a][:, OFF[kb]:OFF[kb] + WIDTH[kb]], SCORE[n % 2][:, 0:WIDTH[kb]],
                               ACT.Exp).then_inc(score_used, 1)

            def softmax_exp(i, t, j):
                n = 2 * NT + 3 * t + j
                w = (t + 1) * P if j < 2 else M
                dst = df_p[t % 2][j] if j < 2 else mx_p[t % 2]
                act.wait_ge(negmax_ready, i * 3 * NT + 3 * t + j + 1)
                c = 3 * t + j
                act.activation(dst[:, 0:w], SCORE[n % 2][:, 0:w], ACT.Exp, bias=neg_max[:, c:c + 1],
                               accum_out=expsum[:, c:c + 1]).then_inc(score_used, 1)

            with act.Fori(0, ROUNDS) as i:
                steps.enter(i, 2 * 2 * NT + 2)
                for a in range(2):
                    for kb in range(NT):
                        softlog(i, a, kb)
                for a in range(2):
                    for kb in range(NT):
                        stick_weights(i, a, kb)
                for t in range(NT):
                    for j in range(3):
                        softmax_exp(i, t, j)
                act.wait_ge(df_out_done, i * NT + NT)
                for t in range(NT):
                    ins = act.activation(df_sq[:, t * P:(t + 1) * P], SUM[:, t * P:(t + 1) * P], ACT.Square,
                                         accum_out=df_ss[:, t:t + 1])
                ins.then_inc(act_step, steps.add())
                act.wait_ge(act_step, steps.value())
                act.activation(df_ln[:, :], df_ss[:, :], ACT.Ln, bias=eps, scale=1.0 / P).then_inc(act_step, steps.add())
                act.wait_ge(act_step, steps.value())
                act.activation(df_rms[:, :], df_ln[:, :], ACT.Exp, scale=-0.5).then_inc(rms_ready, 1)
                steps.leave(ROUNDS)

            act.sem_inc(gate_ready, NB)
            with act.Fori(0, FT) as f:
                for b in range(NB):
                    act.wait_ge(gate_done, f * NB + b + 1)
                    act.wait_ge(branch_used, f * NB + b + 1)
                    act.activation(gate[:, b, :], GATE[b][:, :], ACT.Sigmoid,
                                   bias=b_gate[:, b, bass.ds(f, 1)]).then_inc(gate_ready, 1)

            def rough_rstd(n):
                act.wait_ge(var_ready, n + 1)
                t = n % NT
                act.activation(ln_l[:, t:t + 1], ln_v[:, t:t + 1], ACT.Ln).then_inc(act_step, steps.add())
                act.wait_ge(act_step, steps.value())
                act.activation(ln_r[:, t:t + 1], ln_l[:, t:t + 1], ACT.Exp, scale=-0.5).then_inc(rstd_ready, 1)

            def copy_x1T(t):
                for half in range(2):
                    act.wait_ge(x1_turned, 2 * t + half + 1)
                    act.activation(x1T[:, 4 * half:4 * half + 4, t * P:(t + 1) * P],
                                   XTURN[half][:, :].rearrange("p (k c) -> p k c", k=4), ACT.Copy
                                   ).then_inc(x1T_ready, 1)

            act.sem_inc(x1T_ready, 1)
            for t in range(NT):
                rough_rstd(t)
                if t >= 1:
                    copy_x1T(t - 1)
            copy_x1T(NT - 1)

            def copy_queries(h, u):
                act.wait_ge(query_done, h * 2 + u + 1)
                act.activation(peer_qT[:, u, :], QUERY[u][:, :], ACT.Copy).then_inc(query_copied, 1)

            def copy_keyscores(h, half):
                act.wait_ge(keyscore_done, h * 2 + half + 1)
                act.activation(score[:, 2 * half:2 * half + 2],
                               KEYSCORE[half][:, :].rearrange("p (t u n) -> p t u n", t=2, u=2),
                               ACT.Copy).then_inc(keyscore_copied, 1)

            def best_exp(h, t):
                act.wait_ge(negbest_ready, h * NT + t + 1)
                act.activation(best_e[:, :], best_v[:, :], ACT.Exp, bias=neg_best[:, :],
                               accum_out=best_z[:, :]).then_inc(bestexp_ready, 1)

            def gelu_group(h, t, g):
                n = (h * NT + t) * (TOPK // GROUP) + g
                act.wait_ge(hid_ready, n + 1)
                c = slice(g * GROUP, (g + 1) * GROUP)
                act.activation(gel[:, t, c], hid[:, t, c], ACT.Gelu).then_inc(gelu_ready, 1)
                act.wait_ge(actw_ready, n + 1)
                for e in range(g * GROUP, (g + 1) * GROUP):
                    if e % GROUP == 0:
                        act.wait_ge(row_used, n * GROUP + GROUP)
                    act.activation(diag[:, e % RING, :], ident, ACT.Copy,
                                   scale=act_w[:, t, e:e + 1]).then_inc(diag_ready, 1)

            def experts(h, ahead):
                for t in range(NT):
                    for g in range(TOPK // GROUP):
                        gelu_group(h, t, g)
                        if ahead and t == 0 and g in (3, 5):
                            copy_queries(h + 1, (g - 3) // 2)
                    if ahead and t == 0:
                        act.wait_ge(chosen_ready, (h + 1) * NT)
                        copy_keyscores(h + 1, 0)
                        copy_keyscores(h + 1, 1)
                    if ahead:
                        best_exp(h + 1, t)

            copy_queries(0, 0)
            copy_queries(0, 1)
            copy_keyscores(0, 0)
            copy_keyscores(0, 1)
            for t in range(NT):
                best_exp(0, t)
            with act.Fori(0, HEADS - 1) as h:
                experts(h, True)
            experts(HEADS - 1, False)
            for t in range(NT):
                rough_rstd(NT + t)

        @block.vector
        def _(dve):
            steps = Steps()

            def then(ins):
                ins.then_inc(dve_step, steps.add())
                dve.wait_ge(dve_step, steps.value())

            dve.sem_inc(unit_used, 2)
            dve.sem_inc(softplus_ready, 2)
            dve.sem_inc(mx_out_used, 1)
            dve.wait_ge(const_loaded, 16 * CONST_LOADS)
            pos_f, angle = df_raw[0], df_raw[1]
            then(dve.tensor_copy(pos_f, pos_i))
            then(dve.tensor_scalar(angle, pos_f, inv_freq, None, ALU.mult))
            for j in range(2):
                k, r = (rope_cos, rope_r) if j == 0 else (rope_cos, rope_k)
                then(dve.tensor_scalar(k, angle, 1.0 / TWO_PI, 0.25 * j, ALU.mult, ALU.add))
                then(dve.tensor_scalar(k, k, ROUND_MAGIC, None, ALU.add))
                then(dve.tensor_scalar(k, k, -ROUND_MAGIC, None, ALU.add))
                then(dve.scalar_tensor_tensor(r, k, -PI_A, angle, ALU.mult, ALU.add))
                then(dve.scalar_tensor_tensor(r, k, -PI_B, r, ALU.mult, ALU.add))
                then(dve.scalar_tensor_tensor(r, k, -PI_C, r, ALU.mult, ALU.add))
                if j == 1:
                    then(dve.tensor_scalar(r, r, TWO_PI / 4, None, ALU.add))
                dve.tensor_scalar(r, r, PI_TOP, -PI_TOP, ALU.min, ALU.max).then_inc(angle_ready, 1)
            then(dve.tensor_tensor(lam_pr[:, :, :], lam_in[:, 0:4:2, :], lam_in[:, 1:4:2, :], ALU.mult))
            dve.tensor_reduce(lam_s[:, :], lam_pr[:, :, :], AX_X, ALU.add).then_inc(lam_ready, 1)
            then(dve.tensor_scalar(df_g8[:, :], df_g[:, :], 1.0 - LAMBDA_INIT, None, ALU.mult))
            dve.wait_ge(sines_ready, 2)
            then(dve.tensor_scalar(rope_sin, rope_sin, rope_sign, None, ALU.mult))
            dve.wait_ge(lam_exp, 1)
            then(dve.scalar_tensor_tensor(neg_lam[:, :], lam_e[:, 1:2], -LAMBDA_INIT, lam_e[:, 0:1],
                                          ALU.add, ALU.subtract))

            def unit(i, u):
                seg, src = UNITS[u], PROJ[u % 2]
                dve.wait_ge(unit_done, i * NU + u + 1)
                if seg in (SBQ, DFQ):
                    dst = sb_qT if seg == SBQ else df_raw[0]
                    dve.tensor_scalar(dst, src[:, :], QSCALE, None, ALU.mult).then_inc(unit_used, 1)
                elif seg == MXQ:
                    dve.tensor_scalar(mx_qT, src[:, :], MXSCALE, None, ALU.mult).then_inc(unit_used, 1)
                elif seg in ("swap_q", "swap_k"):
                    raw = df_raw[seg == "swap_k"]
                    dve.tensor_tensor(swapped, src[:, :], rope_sin, ALU.mult).then_inc(unit_used, 1)
                    then(dve.tensor_tensor(raw, raw, rope_cos, ALU.mult))
                    dve.wait_ge(unit_used, i * NU + u + 1 + 2)
                    then(dve.tensor_tensor(raw, raw, swapped, ALU.add))
                elif seg in (MXK, MXV):
                    dve.tensor_copy(mem_kT if seg == MXK else mem_v, src[:, 0:M]).then_inc(unit_used, 1)
                else:
                    dst = {SBK: sb_kT, SBV: sb_v, DFK: df_raw[1], DFV: df_v}[seg]
                    dve.tensor_copy(dst, src[:, :]).then_inc(unit_used, 1)

            def take_softplus(i, a, kb):
                n = a * NT + kb
                w = WIDTH[kb]
                dve.wait_ge(softlog_ready, i * 2 * NT + n + 1)
                dve.scalar_tensor_tensor(softplus[a][:, OFF[kb]:OFF[kb] + w], SOFT[n % 2][:, 0:w], 0.0,
                                         soft_e[n % 2][:, 0:w], ALU.max, ALU.add).then_inc(softplus_ready, 1)

            def neg_maxima(i, t):
                for j in range(3):
                    n = 2 * NT + 3 * t + j
                    w = (t + 1) * P if j < 2 else M
                    dve.wait_ge(score_ready, i * SCORES + n + 1)
                    dve.tensor_reduce(neg_max[:, 3 * t + j:3 * t + j + 1], SCORE[n % 2][:, 0:w], AX_X, ALU.max,
                                      negate=True).then_inc(negmax_ready, 1)

            def probabilities(i, t):
                c = 3 * t
                dve.wait_ge(score_used, i * SCORES + 2 * NT + c + 3 + 2)
                w = (t + 1) * P
                p0, p1 = df_p[t % 2][0][:, 0:w], df_p[t % 2][1][:, 0:w]
                then(dve.reciprocal(exprec[:, c:c + 3], expsum[:, c:c + 3]))
                then(dve.tensor_scalar(p1, p1, exprec[:, c + 1:c + 2], neg_lam[:, :], ALU.mult, ALU.mult))
                dve.scalar_tensor_tensor(p0, p0, exprec[:, c:c + 1], p1, ALU.mult, ALU.add).then_inc(probs_ready, 1)
                dve.tensor_scalar(mx_p[t % 2], mx_p[t % 2], exprec[:, c + 2:c + 3], None,
                                  ALU.mult).then_inc(probs_ready, 1)

            def copy_turned(i, t):
                dve.wait_ge(turned, i * (2 * NT + 1) + 2 * t + 1)
                dve.tensor_copy(df_pT[:, 0:(t + 1) * P], TURN[0][:, 0:(t + 1) * P]).then_inc(turned_copied, 1)
                dve.wait_ge(turned, i * (2 * NT + 1) + 2 * t + 2)
                dve.tensor_copy(mx_pT, TURN[1][:, 0:M]).then_inc(turned_copied, 1)

            with dve.Fori(0, ROUNDS) as i:
                steps.enter(i, 2 * 2 + 2 * NT)
                unit(i, 0)
                unit(i, 1)
                unit(i, 2)
                take_softplus(i, 0, 0)
                take_softplus(i, 0, 1)
                unit(i, 3)
                take_softplus(i, 0, 2)
                take_softplus(i, 0, 3)
                unit(i, 4)
                take_softplus(i, 1, 0)
                take_softplus(i, 1, 1)
                unit(i, 5)
                unit(i, 6)
                unit(i, 7)
                take_softplus(i, 1, 2)
                take_softplus(i, 1, 3)
                unit(i, 8)
                unit(i, 9)
                unit(i, 10)
                neg_maxima(i, 0)
                dve.wait_ge(sb_out_done, i + 1)
                dve.tensor_copy(o_branch[:, 0, bass.ds(i, 1), :], SUM[:, :].rearrange("p (o t) -> p o t", o=1)
                                ).then_inc(sb_out_copied, 1)
                for t in range(1, NT):
                    neg_maxima(i, t)
                    probabilities(i, t - 1)
                    copy_turned(i, t - 1)
                probabilities(i, NT - 1)
                copy_turned(i, NT - 1)
                dve.wait_ge(rms_ready, i + 1)
                dve.tensor_tensor(df_on.rearrange("p (t d) -> p t d", t=NT),
                                  SUM[:, :].rearrange("p (t d) -> p t d", t=NT),
                                  df_rms[:, :].unsqueeze(2).to_broadcast([P, NT, P]), ALU.mult).then_inc(normed_ready, 1)
                dve.wait_ge(turned, (i + 1) * (2 * NT + 1))
                dve.tensor_scalar(o_branch[:, 1, bass.ds(i, 1), :], TURN[0][:, :].rearrange("p (o t) -> p o t", o=1),
                                  df_g8[:, :], None, ALU.mult).then_inc(turned_copied, 1)
                dve.wait_ge(mx_out_done, i + 1)
                dve.tensor_copy(o_branch[:, 2, bass.ds(i, 1), :], MXOUT[:, :].rearrange("p (o t) -> p o t", o=1)
                                ).then_inc(mx_out_used, 1)
                steps.leave(ROUNDS)

            dve.sem_inc(branch_used, NB)
            with dve.Fori(0, FT) as f:
                steps.enter(f, 1)
                for b in range(NB):
                    dve.wait_ge(gate_ready, f * NB + b + 1 + NB)
                    dve.wait_ge(branch_done, f * NB + b + 1)
                    dve.tensor_tensor(part_sum[:, b, :], gate[:, b, :], BRANCH[b][:, :],
                                      ALU.mult).then_inc(branch_used, 1)
                    dve.wait_ge(branch_used, f * NB + b + 1 + NB)
                    if b == 1:
                        then(dve.tensor_tensor(part_sum[:, 0, :], part_sum[:, 0, :], part_sum[:, 1, :], ALU.add))
                dve.tensor_tensor(mergedT[:, bass.ds(f, 1), :], part_sum[:, 0:1, :], part_sum[:, 2:3, :],
                                  ALU.add).then_inc(merged_ready, 1)
                dve.wait_ge(merged_ready, f + 1)
                steps.leave(FT)

            def variance(src, t):
                for n in range(2):
                    ins = dve.bn_stats(stats[:, t, n, :], src[:, n * 512:(n + 1) * 512])
                then(ins)
                then(dve.bn_aggr(mean_var[:, t, :], stats[:, t, :, :].rearrange("p n c -> p (n c)")))
                dve.tensor_scalar(ln_v[:, t:t + 1], mean_var[:, t, 1:2], LN_EPS, None, ALU.add).then_inc(var_ready, 1)

            def normalise(src, t, n, gb):
                dve.wait_ge(rstd_ready, n + 1)
                r, v = ln_r[:, t:t + 1], ln_v[:, t:t + 1]
                then(dve.tensor_scalar(ln_t[:, t:t + 1], r, r, v, ALU.mult, ALU.mult))
                then(dve.tensor_scalar(ln_t[:, t:t + 1], ln_t[:, t:t + 1], -0.5, 1.5, ALU.mult, ALU.add))
                then(dve.tensor_tensor(ln_u[:, t:t + 1], ln_t[:, t:t + 1], r, ALU.mult))
                then(dve.tensor_scalar(src, src, mean_var[:, t, 0:1], ln_u[:, t:t + 1], ALU.subtract, ALU.mult))
                then(dve.tensor_tensor(src, src, gb[:, 0, :], ALU.mult))
                return dve.tensor_tensor(src, src, gb[:, 1, :], ALU.add)

            dve.sem_inc(mix_used, 2)
            dve.wait_ge(xnat_loaded, 16)
            dve.wait_ge(ln1_loaded, 32)
            for t in range(NT):
                dve.wait_ge(mix_done, t + 1)
                for n in range(2):
                    c = slice(n * 512, (n + 1) * 512)
                    ins = dve.scalar_tensor_tensor(x1[:, t, c], x_nat[:, t, c], ALPHA, MIX[t % 2][n][:, :],
                                                   ALU.mult, ALU.add)
                ins.then_inc(mix_used, 1)
                dve.wait_ge(mix_used, t + 1 + 2)
                variance(x1[:, t, :], t)
                normalise(x1[:, t, :], t, t, ln1_gb).then_inc(x1_ready, 1)
                dve.wait_ge(x1_ready, t + 1)
                dve.tensor_scalar(acc[:, t, :], x1[:, t, :], ALPHA, None, ALU.mult).then_inc(acc_ready, 1)

            def choose(h, t):
                dve.sem_clear(choose_step)
                chain = Steps()

                def chosen_then(ins):
                    ins.then_inc(choose_step, chain.add())
                    dve.wait_ge(choose_step, chain.value())

                dve.wait_ge(keyscore_copied, h * 2 + t // 2 + 1)
                dve.sem_inc(choices_begun, 1)
                first, rest = slice(0, 8), slice(8, TOPK)
                s = score[:, t]
                for u in range(2):
                    ins = dve.max(top_v[:, u, first], s[:, u, :])
                chosen_then(ins)
                for u in range(2):
                    dve.max_index(top_i[:, u, first], top_v[:, u, first], s[:, u, :])
                    ins = dve.match_replace(score_cut[:, u, :], top_v[:, u, first], s[:, u, :], NEG_BIG)
                chosen_then(ins)
                for u in range(2):
                    ins = dve.max(top_v[:, u, rest], score_cut[:, u, :])
                chosen_then(ins)
                for u in range(2):
                    ins = dve.max_index(top_i[:, u, rest], top_v[:, u, rest], score_cut[:, u, :])
                ins = dve.tensor_tensor(cand.rearrange("p (i j) -> p i j", i=TOPK),
                                        top_v[:, 0, :].unsqueeze(2).to_broadcast([P, TOPK, TOPK]),
                                        top_v[:, 1, :].unsqueeze(1).to_broadcast([P, TOPK, TOPK]), ALU.add)
                chosen_then(ins)
                dve.tensor_copy(top_f[:, :, :], top_i[:, :, :])
                chosen_then(dve.max(best_v[:, first], cand))
                chosen_then(dve.tensor_scalar(neg_best[:, :], best_v[:, 0:1], -1.0, None, ALU.mult))
                dve.max_index(best_i[:, first], best_v[:, first], cand)
                chosen_then(dve.match_replace(cand_cut, best_v[:, first], cand, NEG_BIG))
                chosen_then(dve.max(best_v[:, rest], cand_cut))
                dve.sem_inc(negbest_ready, 1)
                chosen_then(dve.max_index(best_i[:, rest], best_v[:, rest], cand_cut))
                dve.tensor_scalar(best_ij[:, 0, :], best_i[:, :], 4, None, ALU.logical_shift_right)
                chosen_then(dve.tensor_scalar(best_ij[:, 1, :], best_i[:, :], TOPK - 1, None, ALU.bitwise_and))
                chosen_then(dve.tensor_copy(best_f[:, :, :], best_ij[:, :, :]))
                for u in range(2):
                    ins = dve.tensor_tensor(onehot[:, u], iota16.unsqueeze(1).to_broadcast([P, TOPK, TOPK]),
                                            best_f[:, u, :].unsqueeze(2).to_broadcast([P, TOPK, TOPK]), ALU.is_equal)
                chosen_then(ins)
                for u in range(2):
                    ins = dve.tensor_tensor(onehot[:, u], onehot[:, u],
                                            top_f[:, u, :].unsqueeze(1).to_broadcast([P, TOPK, TOPK]), ALU.mult)
                chosen_then(ins)
                chosen_then(dve.tensor_reduce(chosen[:, :, :], onehot, AX_X, ALU.add))
                dve.wait_ge(bestexp_ready, h * NT + t + 1)
                chosen_then(dve.reciprocal(best_r[:, :], best_z[:, :]))
                chosen_then(dve.tensor_scalar(weight[:, t, :], best_e[:, :], best_r[:, :], None, ALU.mult))
                dve.scalar_tensor_tensor(ids[:, t, :], chosen[:, 0, :], float(NK), chosen[:, 1, :],
                                         ALU.mult, ALU.add).then_inc(chosen_ready, 1)

            def weigh(h, t, g):
                n = (h * NT + t) * (TOPK // GROUP) + g
                dve.wait_ge(gelu_ready, n + 1)
                c = slice(g * GROUP, (g + 1) * GROUP)
                dve.tensor_tensor(act_w[:, t, c], gel[:, t, c], weight[:, t, c], ALU.mult).then_inc(actw_ready, 1)

            def experts(h, ahead):
                for t in range(NT):
                    for g in range(TOPK // GROUP):
                        for e in range(g * GROUP, (g + 1) * GROUP):
                            dve.wait_ge(row_loaded[e % RING], ((h * NT + t) * (TOPK // RING) + e // RING) * 16 + 16)
                            ins = dve.tensor_tensor_reduce(rows[:, e % RING, 0:D], rows[:, e % RING, 0:D], x1[:, t, :],
                                                           1.0, 0.0, ALU.mult, ALU.add, hid[:, t, e:e + 1])
                        ins.then_inc(hid_ready, 1)
                        if g >= 1:
                            weigh(h, t, g - 1)
                    weigh(h, t, TOPK // GROUP - 1)
                    if ahead:
                        choose(h + 1, t)
                    dve.wait_ge(row_used, (h * NT + t + 1) * TOPK + RING)
                    for n in range(2):
                        c = slice(n * 512, (n + 1) * 512)
                        ins = dve.tensor_tensor(acc[:, t, c], acc[:, t, c], VSUM[t % 2][n][:, :], ALU.add)
                    ins.then_inc(vsum_used, 1)

            dve.sem_inc(vsum_used, 2)
            dve.wait_ge(acc_ready, NT)
            for t in range(NT):
                choose(0, t)
            with dve.Fori(0, HEADS - 1) as h:
                experts(h, True)
            experts(HEADS - 1, False)
            dve.wait_ge(ln2_loaded, 32)
            for t in range(NT):
                dve.wait_ge(vsum_used, (HEADS - 1) * NT + t + 1 + 2)
                variance(acc[:, t, :], t)
                normalise(acc[:, t, :], t, NT + t, ln2_gb).then_inc(out_ready, 1)


def kernel(**inputs):
    import ml_dtypes
    import numpy as np
    import concourse.bacc as bacc
    from concourse import mybir as mb
    from concourse.bass_utils import run_bass_kernel_spmd

    a = {k: np.asarray(v) for k, v in inputs.items()}
    cols = ROUNDS * P
    w_in = a["w_in"][0].reshape(KD, P, 7, ROUNDS, P).transpose(3, 2, 1, 0, 4)
    w_kv = a["w_mem_kv"][0].reshape(KD, P, 2, ROUNDS, P).transpose(3, 2, 1, 0, 4)
    w_gate = a["w_gate"][0].reshape(KD, P, NB, FT, P).transpose(3, 2, 1, 0, 4)
    w_br = np.stack([a["w_br_sb"][0], a["w_br_df"][0], a["w_br_mx"][0]])
    w_br = w_br.reshape(NB, ROUNDS, P, FT, P).transpose(3, 0, 2, 1, 4)
    arrays = {
        "xT": a["x"][0].T,
        "x": a["x"][0].reshape(NT, P, D).transpose(1, 0, 2),
        "memT": a["mem"][0].T.reshape(KD, P, M).transpose(1, 0, 2),
        "pos": a["positions"][0],
        "w_mix": np.concatenate([w_in, w_kv], axis=1),
        "lam": a["df_lambda"][0].reshape(-1),
        "df_g": a["df_norm_g"][0].reshape(P, 1),
        "w_gate": w_gate,
        "b_gate": a["b_gate"][0].reshape(NB, FT, P).transpose(2, 0, 1),
        "w_br": w_br,
        "w_out": a["w_out"][0].reshape(KD, P, D).transpose(1, 0, 2),
        "ln": np.stack([a["ln1_g"][0], a["ln1_b"][0], a["ln2_g"][0], a["ln2_b"][0]]),
        "w_query": a["w_query"][0].reshape(KD, P, HEADS, 2, P).transpose(2, 1, 3, 0, 4),
        "keysT": a["sub_keys"][0].transpose(0, 3, 1, 2),
        "uv": np.concatenate([a["u_tab"][0], a["v_tab"][0]], axis=1),
    }
    row, col = np.arange(P)[:, None], np.arange(P)[None, :]
    rope, half = HD // 4, HD // 8
    c = np.zeros((P, NCONST), np.float32)
    c[:, C_IDENT:C_IDENT + P] = row == col
    c[:, C_TRI:C_TRI + P] = -1.0 * (row >= col)
    c[:, C_ONES:C_ONES + P] = -1.0
    d = np.arange(P) % HD
    partner = np.where(d < half, np.arange(P) + half, np.arange(P) - half)
    c[:, C_PERM:C_PERM + P] = (row == partner[None, :]) & (d < rope)[None, :]
    freq = (500000.0 ** (-np.arange(0, rope, 2, dtype=np.float32) / rope)).astype(np.float32)
    c[:, C_INV] = np.where(d < rope, freq[d % half], 0.0)
    c[:, C_SIGN] = np.where(d < half, -1.0, np.where(d < rope, 1.0, 0.0))
    c[:, C_EPS] = RMS_EPS
    c[:, C_ONE] = 1.0
    c[:, C_IOTA:C_IOTA + TOPK] = np.arange(TOPK)
    arrays["const"] = c
    m = np.zeros((P, 3, P), np.float32)
    m[:, 0] = row == col
    m[:, 1] = -1e30 * (row >= col)
    m[:, 2] = -1e30 * (col > row)
    arrays["masks"] = m.astype(ml_dtypes.bfloat16)
    arrays = {f"in_{k}": np.ascontiguousarray(v) for k, v in arrays.items()}

    nc = bacc.Bacc("TRN2", target_bir_lowering=False, num_devices=1)
    args = [nc.dram_tensor(k, v.shape, mb.dt.from_np(v.dtype), kind="ExternalInput").ap() for k, v in arrays.items()]
    out = nc.dram_tensor("out", (P, NT, D), F32, kind="ExternalOutput").ap()
    build_layer(nc, *args, out)
    r = run_bass_kernel_spmd(nc, [arrays], core_ids=[0])
    return r.results[0]["out"].transpose(1, 0, 2).reshape(1, T, D)
```

```python
from contextlib import ExitStack

import concourse.bass as bass
from concourse import mybir

F32 = mybir.dt.float32
F32R = mybir.dt.float32r
BF16 = mybir.dt.bfloat16
U32 = mybir.dt.uint32
I32 = mybir.dt.int32
ALU = mybir.AluOpType
ACT = mybir.ActivationFunctionType
AX_X = mybir.AxisListType.X

P = 128
T = 512
NT = T // P
D = 1024
KD = D // P
M = 256
NM = M // P
HD = 64
ROUNDS = 4
SEGS = 9
SBQ, SBK, SBV, DFQ, DFK, DFV, MXQ, MXK, MXV = range(SEGS)
UNITS = [SBQ, SBK, SBV, DFQ, "turn_sb", DFK, "swap_q", "swap_k", DFV, MXQ, "turn_df", MXK, MXV, "turn_mx"]
NU = len(UNITS)
TURNED = {"turn_sb": (SBV, 512), "turn_df": (DFV, 512), "turn_mx": (MXV, 256)}
NB = 3
FT = D // P
HEADS = 8
NK = 128
TOPK = 16
WRING = 3
WBLOCKS = ROUNDS * SEGS
RING = 8
GROUP = 2
LAMBDA_INIT = 0.8 - 0.6
LN_EPS = 1e-5
RMS_EPS = 1e-5
ALPHA = 2.0 ** 0.25
QSCALE = HD ** -0.5
MXSCALE = 128 ** -0.5
SCORES = 5 * NT
CONST_LOADS = 6
REGION_B = 15104
TWO_PI = 6.283185307179586
PI_A = 6.28125
PI_B = 0.0019350051879882812
PI_C = TWO_PI - PI_A - PI_B
ROUND_MAGIC = 12582912.0
PI_TOP = 3.1415925
NEG_BIG = -3.0e38

WIDTH = [T - P * kb for kb in range(NT)]
OFF = [sum(WIDTH[:kb]) for kb in range(NT)]
CAUSAL = sum(WIDTH)

C_IDENT, C_TRI, C_ONES, C_PERM = 0, P, 2 * P, 3 * P
C_INV = 4 * P
C_SIGN = C_INV + 1
C_EPS = C_INV + 2
C_ONE = C_INV + 3
C_IOTA = C_INV + 4
NCONST = C_IOTA + TOPK


class Steps:

    def __init__(self):
        self.base, self.k = 0, 0

    def add(self):
        self.k += 1
        return 1

    def value(self):
        return self.base + self.k

    def enter(self, i, per):
        self.start, self.per = self.base + self.k, per
        self.base, self.k = i * per + self.start, 0

    def leave(self, trips):
        assert self.k == self.per, (self.k, self.per)
        self.base, self.k = self.start + trips * self.per, 0


def build_layer(nc, xT_d, x_d, memT_d, pos_d, w_mix_d, lam_d, df_g_d, w_gate_d, b_gate_d, w_br_d,
                w_out_d, ln_d, w_query_d, keysT_d, uv_d, const_d, masks_d, out_d):
    ctx = ExitStack()
    with ctx:
        def sb(name, shape, dt=F32):
            return ctx.enter_context(nc.sbuf_tensor(name, shape, dt))

        def sem(name):
            return ctx.enter_context(nc.semaphore(name))

        region_a_at = (nc.sbuf_base + 63) // 64 * 64
        region_b_at = region_a_at + 4 * RING * 2 * D
        sb("slab", [P, RING * 2 * D + REGION_B + 16])

        def at_offset(name, shape, dt, offset):
            return nc.alloc_sbuf_tensor_at(name, shape, dt, offset=offset)

        region_a = at_offset("region_a", [P, RING * 2 * D], F32, region_a_at)
        rows = region_a[:, :].rearrange("p (r c) -> p r c", r=RING)
        w_raw = region_a[:, 0:WRING * D].rearrange("p (j c) -> p j c", j=WRING)
        w_hi = at_offset("w_hi", [P, WRING, D], F32R, region_a_at + 4 * WRING * D)
        w_lo = at_offset("w_lo", [P, WRING, D], F32R, region_a_at + 8 * WRING * D)
        at = 3 * WRING * D
        rope_cos = region_a[:, at:at + T]
        rope_sin = region_a[:, at + T:at + 2 * T]
        rope_k = region_a[:, at + 2 * T:at + 3 * T]
        rope_r = region_a[:, at + 3 * T:at + 4 * T]
        at += 4 * T
        df_raw = [region_a[:, at + j * T:at + (j + 1) * T] for j in range(2)]
        at += 2 * T
        x_nat = region_a[:, at:at + NT * D].rearrange("p (t d) -> p t d", t=NT)
        assert at + NT * D <= RING * 2 * D

        region_b = at_offset("region_b", [P, REGION_B], F32, region_b_at)
        at = 0

        def part(n):
            nonlocal at
            at += n
            assert at <= REGION_B
            return region_b[:, at - n:at]

        xT_raw = part(KD * T).rearrange("p (k t) -> p k t", k=KD)
        memT_raw = part(KD * M).rearrange("p (k m) -> p k m", k=KD)
        at = 0
        sb_qT, sb_kT, sb_v, df_v, mx_qT = part(T), part(T), part(T), part(T), part(T)
        mem_kT, mem_v = part(M), part(M)
        softplus = [part(CAUSAL) for _ in range(2)]
        sb_aT = [part(CAUSAL) for _ in range(2)]
        soft_log = [part(CAUSAL) for _ in range(2)]
        df_p = [[part(T) for _ in range(2)] for _ in range(2)]
        df_pT = part(T)
        mx_pT = part(M)
        df_on = part(T)
        df_sq = df_pT
        mx_p = [part(M) for _ in range(2)]
        swapped = part(T)
        pos_i = swapped.bitcast(I32)
        mergedT_hi = at_offset("mergedT_hi", [P, FT, T], F32R, region_b_at)
        mergedT_lo = at_offset("mergedT_lo", [P, FT, T], F32R, region_b_at + 4 * FT * T)
        at = 2 * FT * T
        ln1_gb = part(2 * D).rearrange("p (j d) -> p j d", j=2)
        gate = part(NB * T).rearrange("p (b t) -> p b t", b=NB)
        part_sum = part(NB * T).rearrange("p (b t) -> p b t", b=NB)
        w_br = part(NB * ROUNDS * P).rearrange("p (b k c) -> p b k c", b=NB, k=ROUNDS)
        at = 0
        acc = part(NT * D).rearrange("p (t d) -> p t d", t=NT)
        w_q = part(2 * D).rearrange("p (u k c) -> p u k c", u=2, k=KD)
        keysT = part(2 * NK).rearrange("p (u n) -> p u n", u=2)
        peer_qT = part(2 * T).rearrange("p (u t) -> p u t", u=2)
        score_cut = part(2 * NK).rearrange("p (u n) -> p u n", u=2)
        cand, cand_cut = part(TOPK * TOPK), part(TOPK * TOPK)
        assert at <= 2 * FT * T
        at = 2 * FT * T
        ln2_gb = part(2 * D).rearrange("p (j d) -> p j d", j=2)
        score = part(NT * 2 * NK).rearrange("p (t u n) -> p t u n", t=NT, u=2)
        onehot = part(2 * TOPK * TOPK).rearrange("p (u e i) -> p u e i", u=2, e=TOPK)
        diag = part(RING * P).rearrange("p (e c) -> p e c", e=RING)

        xT_hi = sb("xT_hi", [P, KD, T], F32R)
        xT_lo = sb("xT_lo", [P, KD, T], F32R)
        memT_hi = sb("memT_hi", [P, KD * M], F32R)
        memT_lo = sb("memT_lo", [P, KD * M], F32R)
        memTs = [m[:, :].rearrange("p (k m) -> p k m", k=KD) for m in (memT_hi, memT_lo)]
        wqs = [m[:, :].rearrange("p (u k c) -> p u k c", u=2, k=KD) for m in (memT_hi, memT_lo)]
        oT = sb("oT", [P, NB * ROUNDS * T])
        o_branch = oT[:, :].rearrange("p (b i t) -> p b i t", b=NB, i=ROUNDS)
        x1 = oT[:, 0:NT * D].rearrange("p (t d) -> p t d", t=NT)
        b_gate = sb("b_gate", [P, NB, FT])
        const = sb("const", [P, NCONST])
        masks = sb("masks", [P, 3, P], BF16)
        df_g = sb("df_g", [P, 1])
        df_g8 = sb("df_g8", [P, 1])
        lam_in = sb("lam_in", [P, 4, HD])
        lam_pr = sb("lam_pr", [P, 2, HD])
        lam_s = sb("lam_s", [P, 2])
        lam_e = sb("lam_e", [P, 2])
        neg_lam = sb("neg_lam", [P, 1])
        neg_max = sb("neg_max", [P, 3 * NT])
        expsum = sb("expsum", [P, 3 * NT])
        exprec = sb("exprec", [P, 3 * NT])
        df_ss = sb("df_ss", [P, NT])
        df_ln = sb("df_ln", [P, NT])
        df_rms = sb("df_rms", [P, NT])
        stats = sb("stats", [P, NT, 2, 6])
        mean_var = sb("mean_var", [P, NT, 2])
        ln_v = sb("ln_v", [P, NT])
        ln_l = sb("ln_l", [P, NT])
        ln_r = sb("ln_r", [P, NT])
        ln_t = sb("ln_t", [P, NT])
        ln_u = sb("ln_u", [P, NT])
        ln_b = sb("ln_b", [P, NT])
        top_v = sb("top_v", [P, 2, TOPK])
        top_i = sb("top_i", [P, 2, TOPK], U32)
        top_f = sb("top_f", [P, 2, TOPK])
        best_v = sb("best_v", [P, TOPK])
        best_i = sb("best_i", [P, TOPK], U32)
        best_ij = sb("best_ij", [P, 2, TOPK], U32)
        best_f = sb("best_f", [P, 2, TOPK])
        chosen = sb("chosen", [P, 2, TOPK])
        neg_best = sb("neg_best", [P, 1])
        best_e = sb("best_e", [P, TOPK])
        best_z = sb("best_z", [P, 1])
        best_r = sb("best_r", [P, 1])
        ids = sb("ids", [P, NT, TOPK], U32)
        weight = sb("weight", [P, NT, TOPK])
        hid = sb("hid", [P, NT, TOPK])
        gel = sb("gel", [P, NT, TOPK])
        act_w = sb("act_w", [P, NT, TOPK])

        ident = const[:, C_IDENT:C_IDENT + P]
        neg_tri = const[:, C_TRI:C_TRI + P]
        neg_ones = const[:, C_ONES:C_ONES + P]
        swap_perm = const[:, C_PERM:C_PERM + P]
        eps = const[:, C_EPS:C_EPS + 1]
        one = const[:, C_ONE:C_ONE + 1]
        iota16 = const[:, C_IOTA:C_IOTA + TOPK]
        inv_freq = const[:, C_INV:C_INV + 1]
        rope_sign = const[:, C_SIGN:C_SIGN + 1]

        bank = [ctx.enter_context(nc.psum_tensor(f"bank{b}", [P, 512], F32)) for b in range(8)]
        PROJ, SOFT, SCORE = bank[0:2], bank[2:4], bank[4:6]
        TURN = [bank[6], bank[3]]
        SUM, MXOUT = bank[7], bank[2]
        GATE, BRANCH = [bank[0], bank[1], bank[4]], [bank[5], bank[2], bank[3]]
        MIX = [[bank[0], bank[1]], [bank[4], bank[5]], [bank[2], bank[3]], [bank[6], bank[7]]]
        VSUM = [[bank[0], bank[1]], [bank[4], bank[5]]]
        QUERY = [bank[2], bank[3]]
        KEYSCORE = [bank[6], bank[7]]

        const_loaded, memT_loaded = sem("const_loaded"), sem("memT_loaded")
        xT_loaded = [sem(f"xT_loaded{k}") for k in range(KD)]
        w_loaded = [sem(f"w_loaded{j}") for j in range(WRING)]
        w_rounded, w_split = sem("w_rounded"), sem("w_split")
        wq_rounded, wq_split = sem("wq_rounded"), sem("wq_split")
        xT_rounded, xT_split, memT_rounded, memT_split = (sem("xT_rounded"), sem("xT_split"),
                                                          sem("memT_rounded"), sem("memT_split"))
        unit_done, unit_used = sem("unit_done"), sem("unit_used")
        z_ready, abs_ready, softlog_ready, softplus_ready = sem("z_ready"), sem("abs_ready"), sem("softlog_ready"), sem("softplus_ready")
        score_ready, score_used = sem("score_ready"), sem("score_used")
        negmax_ready, probs_ready = sem("negmax_ready"), sem("probs_ready")
        turned, turned_copied = sem("turned"), sem("turned_copied")
        sb_out_done, sb_out_copied = sem("sb_out_done"), sem("sb_out_copied")
        df_out_done, rms_ready, normed_ready = sem("df_out_done"), sem("rms_ready"), sem("normed_ready")
        mx_out_done, mx_out_used = sem("mx_out_done"), sem("mx_out_used")
        dve_step, act_step, choose_step = sem("dve_step"), sem("act_step"), sem("choose_step")
        angle_ready, sines_ready, lam_ready, lam_exp = (sem("angle_ready"), sem("sines_ready"),
                                                        sem("lam_ready"), sem("lam_exp"))
        wb_loaded = [sem(f"wb_loaded{b}") for b in range(NB)]
        gate_done, gate_ready = sem("gate_done"), sem("gate_ready")
        branch_done, branch_used = sem("branch_done"), sem("branch_used")
        merged_ready = sem("merged_ready")
        mix_block_done, xnat_loaded, ln1_loaded, ln2_loaded = (sem("mix_block_done"), sem("xnat_loaded"),
                                                            sem("ln1_loaded"), sem("ln2_loaded"))
        mix_done, mix_used = sem("mix_done"), sem("mix_used")
        var_ready, rstd_ready, scale_ready, scaled = (sem("var_ready"), sem("rstd_ready"),
                                                      sem("scale_ready"), sem("scaled"))
        x1_ready = sem("x1_ready")
        x1_turned, x1T_rounded, x1T_split, acc_ready = (sem("x1_turned"), sem("x1T_rounded"),
                                                        sem("x1T_split"), sem("acc_ready"))
        wq_loaded, keys_loaded = sem("wq_loaded"), sem("keys_loaded")
        query_done, query_copied = sem("query_done"), sem("query_copied")
        keyscore_done, keyscore_copied = sem("keyscore_done"), sem("keyscore_copied")
        negbest_ready, bestexp_ready, chosen_ready = sem("negbest_ready"), sem("bestexp_ready"), sem("chosen_ready")
        row_loaded = [sem(f"row_loaded{r}") for r in range(RING)]
        row_used = sem("row_used")
        hid_ready, gelu_ready, actw_ready, diag_ready = (sem("hid_ready"), sem("gelu_ready"),
                                                         sem("actw_ready"), sem("diag_ready"))
        vsum_used = sem("vsum_used")
        pool_begun, choices_begun = sem("pool_begun"), sem("choices_begun")
        out_ready, out_stored = sem("out_ready"), sem("out_stored")

        block = ctx.enter_context(nc.Block())

        @block.sync
        def _(sp):
            def load_block(n, slot, src):
                sp.dma_start(w_raw[:, slot, :], src).then_inc(w_loaded[slot], 16)

            load_block(0, 0, w_mix_d[0, 0])
            for k in range(KD):
                sp.dma_start(xT_raw[:, k, :], xT_d[k * P:(k + 1) * P, :]).then_inc(xT_loaded[k], 16)
            sp.dma_start(const[:, :], const_d).then_inc(const_loaded, 16)
            sp.dma_start(pos_i, pos_d.partition_broadcast(P)).then_inc(const_loaded, 16)
            load_block(1, 1, w_mix_d[0, 1])
            sp.dma_start(masks[:, :, :], masks_d).then_inc(const_loaded, 16)
            load_block(2, 2, w_mix_d[0, 2])
            sp.dma_start(lam_in[:, :, :].rearrange("p a b -> p (a b)"),
                         lam_d.partition_broadcast(P)).then_inc(const_loaded, 16)
            sp.dma_start(df_g[:, :], df_g_d).then_inc(const_loaded, 16)
            sp.dma_start(b_gate[:, :, :], b_gate_d).then_inc(const_loaded, 16)
            sp.dma_start(memT_raw, memT_d).then_inc(memT_loaded, 16)
            for s in range(WRING, SEGS):
                sp.wait_ge(w_split, s - WRING + 1)
                load_block(s, s % WRING, w_mix_d[0, s])
            sp.dma_start(x_nat, x_d).then_inc(xnat_loaded, 16)
            with sp.Fori(1, ROUNDS) as i:
                for s in range(SEGS):
                    sp.wait_ge(w_split, i * SEGS + s - WRING + 1)
                    load_block(i * SEGS + s, s % WRING, w_mix_d[i, s])

            def load_gate(f, b):
                sp.wait_ge(w_split, f * NB + b + WBLOCKS - WRING + 1)
                load_block(0, b, w_gate_d[f, b])

            for b in range(NB):
                load_gate(0, b)
            sp.wait_ge(turned_copied, ROUNDS * (2 * NT + 1))
            for j in range(2):
                sp.dma_start(ln1_gb[:, j, :], ln_d[j].partition_broadcast(P)).then_inc(ln1_loaded, 16)
            for b in range(NB):
                sp.dma_start(w_br[:, b], w_br_d[0, b]).then_inc(wb_loaded[b], 16)
            with sp.Fori(1, FT) as f:
                for b in range(NB):
                    load_gate(f, b)
                    sp.wait_ge(branch_done, f * NB - NB + b + 1)
                    sp.dma_start(w_br[:, b], w_br_d[f, b]).then_inc(wb_loaded[b], 16)
            for f in range(FT):
                n = WBLOCKS + FT * NB + f
                sp.wait_ge(w_split, n - WRING + 1)
                load_block(n, n % WRING, w_out_d[f])
            sp.wait_ge(mix_done, NT)
            sp.dma_start(w_q, w_query_d[0]).then_inc(wq_loaded, 16)
            sp.dma_start(keysT, keysT_d[0]).then_inc(keys_loaded, 16)
            sp.wait_ge(x1_ready, NT)
            for j in range(2):
                sp.dma_start(ln2_gb[:, j, :], ln_d[2 + j].partition_broadcast(P)).then_inc(ln2_loaded, 16)
            with sp.Fori(1, HEADS) as h:
                sp.wait_ge(wq_split, h * 2)
                sp.dma_start(w_q, w_query_d[h]).then_inc(wq_loaded, 16)
                sp.wait_ge(keyscore_done, h * 2)
                sp.dma_start(keysT, keysT_d[h]).then_inc(keys_loaded, 16)
            for t in range(NT):
                sp.wait_ge(out_ready, t + 1)
                sp.dma_start(out_d[:, t, :], acc[:, t, :]).then_inc(out_stored, 16)
            sp.wait_ge(out_stored, 16 * NT)

        @block.gpsimd
        def _(pool):
            def split_block(n, slot, uses):
                pool.wait_ge(w_loaded[slot], uses * 16)
                pool.sem_inc(pool_begun, 1)
                pool.tensor_scalar(w_hi[:, slot, :], w_raw[:, slot, :], 1.0, 0.0, ALU.mult,
                                   ALU.add).then_inc(w_rounded, 1)
                pool.wait_ge(w_rounded, n + 1)
                pool.tensor_tensor(w_lo[:, slot, :], w_raw[:, slot, :], w_hi[:, slot, :].bitcast(F32),
                                   ALU.subtract).then_inc(w_split, 1)

            def split_query(h, u):
                hi, lo = (m[:, u].rearrange("p k c -> p (k c)") for m in wqs)
                raw = w_q[:, u].rearrange("p k c -> p (k c)")
                pool.wait_ge(wq_loaded, h * 16 + 16)
                pool.sem_inc(pool_begun, 1)
                pool.tensor_scalar(hi, raw, 1.0, 0.0, ALU.mult, ALU.add).then_inc(wq_rounded, 1)
                pool.wait_ge(wq_rounded, h * 2 + u + 1)
                pool.tensor_tensor(lo, raw, hi.bitcast(F32), ALU.subtract).then_inc(wq_split, 1)

            def gather_tile(h, t, ahead):
                pool.wait_ge(chosen_ready, h * NT + t + 1)
                for e in range(TOPK):
                    n = (h * NT + t) * TOPK + e
                    pool.wait_ge(row_used, n + 1)
                    pool.sem_inc(pool_begun, 1)
                    pool.indirect_dma_start(rows[:, e % RING, :], None, uv_d,
                                            bass.IndirectOffsetOnAxis(ap=ids[:, t, e:e + 1], axis=0)
                                            ).then_inc(row_loaded[e % RING], 16)
                    if ahead and t == 0 and e in (3, 5):
                        pool.wait_ge(query_done, h * 2 + (e - 3) // 2 + 1)
                        split_query(h + 1, (e - 3) // 2)

            for s in range(SEGS):
                if s >= WRING:
                    pool.wait_ge(unit_done, UNITS.index(s - WRING) + 1)
                split_block(s, s % WRING, s // WRING + 1)
            with pool.Fori(1, ROUNDS) as i:
                for s in range(SEGS):
                    before = UNITS.index(s - WRING) if s >= WRING else UNITS.index(s - WRING + SEGS) - NU
                    pool.wait_ge(unit_done, i * NU + before + 1)
                    split_block(i * SEGS + s, s % WRING, i * (SEGS // WRING) + s // WRING + 1)
            for b in range(NB):
                pool.wait_ge(unit_done, (ROUNDS - 1) * NU + UNITS.index(MXQ + b) + 1)
                split_block(WBLOCKS + b, b, WBLOCKS // WRING + 1)
            with pool.Fori(1, FT) as f:
                for b in range(NB):
                    pool.wait_ge(gate_done, f * NB - NB + b + 1)
                    split_block(f * NB + WBLOCKS + b, b, f + WBLOCKS // WRING + 1)
            for f in range(FT):
                n = WBLOCKS + FT * NB + f
                if f < WRING:
                    pool.wait_ge(gate_done, FT * NB - WRING + f + 1)
                else:
                    pool.wait_ge(mix_block_done, f - WRING + 1)
                split_block(n, n % WRING, n // WRING + 1)
            split_query(0, 0)
            split_query(0, 1)
            for t in range(NT):
                pool.wait_ge(x1_ready, t + 1)
                pool.tensor_scalar(acc[:, t, :], x1[:, t, :], ALPHA, 0.0, ALU.mult, ALU.add).then_inc(acc_ready, 1)
            pool.wait_ge(mix_used, NT)

            with pool.Fori(0, HEADS - 1) as h:
                for t in range(NT):
                    gather_tile(h, t, True)
            for t in range(NT):
                gather_tile(HEADS - 1, t, False)

        @block.tensor
        def _(pe):
            xTs = (xT_hi, xT_lo)

            def triple(out, left, right, start, stop):
                pe.matmul(out, left[0], right[0], start=start, stop=False)
                pe.matmul(out, left[0], right[1], start=False, stop=False)
                return pe.matmul(out, left[1], right[0], start=False, stop=stop)

            def w_parts(slot, k, n=P):
                return [w[:, slot, k * n:(k + 1) * n] for w in (w_hi, w_lo)]

            def project(i, u, half=None):
                seg = UNITS[u]
                out = PROJ[u % 2]
                ks = range(KD) if half is None else range(half * KD // 2, (half + 1) * KD // 2)
                pe.wait_ge(unit_used, i * NU + u + 1)
                if seg in ("swap_q", "swap_k"):
                    raw = UNITS.index(DFQ if seg == "swap_q" else DFK)
                    pe.wait_ge(unit_used, i * NU + raw + 1 + 2)
                    mm = pe.matmul(out[:, :], swap_perm, df_raw[seg == "swap_k"], start=True, stop=True)
                    mm.then_inc(unit_done, 1)
                    return
                if seg in TURNED:
                    v, n = TURNED[seg]
                    pe.wait_ge(unit_used, i * NU + UNITS.index(v) + 1 + 2)
                    for t in range(n // P):
                        mm = pe.transpose(out[:, t * P:(t + 1) * P], swapped[:, t * P:(t + 1) * P], ident)
                    mm.then_inc(unit_done, 1)
                    return
                pe.wait_ge(w_split, i * SEGS + seg + 1)
                slot = seg % WRING
                n = M if seg in (MXK, MXV) else T
                if seg == MXK:
                    pe.wait_ge(memT_split, 1)
                for k in ks:
                    if isinstance(i, int) and i == 0 and u == 0:
                        pe.wait_ge(xT_split, k + 1)
                    mm = triple(out[:, 0:n], w_parts(slot, k), [x[:, k, :] for x in (memTs if n == M else xTs)],
                                start=(k == 0), stop=(k == KD - 1))
                if KD - 1 in ks:
                    mm.then_inc(unit_done, 1)

            def head_scores(out, a, kb, stop):
                r = slice(a * HD, (a + 1) * HD)
                pe.matmul(out[:, 0:WIDTH[kb]], sb_kT[r, kb * P:(kb + 1) * P], sb_qT[r, kb * P:T],
                          start=True, stop=False)
                return pe.matmul(out[:, 0:P], masks[:, 0, :], masks[:, 1, :], start=False, stop=stop)

            def z_block(i, a, kb):
                n = a * NT + kb
                if n == 0:
                    pe.wait_ge(unit_used, i * NU + 2 + 2)
                    pe.wait_ge(mx_out_used, i + 1)
                pe.wait_ge(abs_ready, i * 2 * NT + n + 1)
                head_scores(SOFT[n % 2], a, kb, True).then_inc(z_ready, 1)

            def stick_block(i, a, kb):
                n = a * NT + kb
                pe.wait_ge(softplus_ready, i * 2 + a + 1)
                pe.wait_ge(score_used, i * SCORES + n + 1)
                out = SCORE[n % 2]
                head_scores(out, a, kb, False)
                mm = pe.matmul(out[:, 0:WIDTH[kb]], neg_tri, softplus[a][:, OFF[kb]:OFF[kb] + WIDTH[kb]],
                               start=False, stop=(kb == NT - 1))
                for later in range(kb + 1, NT):
                    mm = pe.matmul(out[:, (later - kb) * P:WIDTH[kb]], neg_ones,
                                   softplus[a][:, OFF[later]:OFF[later] + WIDTH[later]],
                                   start=False, stop=(later == NT - 1))
                mm.then_inc(score_ready, 1)

            def stick_sum(i):
                pe.wait_ge(score_used, i * SCORES + 2 * NT + 2)
                for a in range(2):
                    for kb in range(NT):
                        mm = pe.matmul(SUM[a * HD:(a + 1) * HD, kb * P:T], sb_v[:, kb * P + a * HD:kb * P + (a + 1) * HD],
                                       sb_aT[a][:, OFF[kb]:OFF[kb] + WIDTH[kb]], start=(kb == 0), stop=(kb == NT - 1))
                mm.then_inc(sb_out_done, 1)

            def df_scores(i, t, m):
                n = 2 * NT + 3 * t + m
                pe.wait_ge(score_used, i * SCORES + n + 1)
                r = slice(m * HD, (m + 1) * HD)
                w = (t + 1) * P
                pe.matmul(SCORE[n % 2][:, 0:w], df_raw[0][r, t * P:w], df_raw[1][r, 0:w], start=True, stop=False)
                pe.matmul(SCORE[n % 2][:, t * P:w], masks[:, 0, :], masks[:, 2, :],
                          start=False, stop=True).then_inc(score_ready, 1)

            def mx_scores(i, t):
                n = 2 * NT + 3 * t + 2
                pe.wait_ge(score_used, i * SCORES + n + 1)
                pe.matmul(SCORE[n % 2][:, 0:M], mx_qT[:, t * P:(t + 1) * P], mem_kT, start=True,
                          stop=True).then_inc(score_ready, 1)

            def tile_scores(i, t):
                df_scores(i, t, 0)
                df_scores(i, t, 1)
                mx_scores(i, t)

            def turn(i, t):
                pe.wait_ge(probs_ready, i * 2 * NT + 2 * t + 1)
                for kb in range(t + 1):
                    mm = pe.transpose(TURN[0][:, kb * P:(kb + 1) * P], df_p[t % 2][0][:, kb * P:(kb + 1) * P], ident)
                mm.then_inc(turned, 1)
                pe.wait_ge(probs_ready, i * 2 * NT + 2 * t + 2)
                for kb in range(NM):
                    mm = pe.transpose(TURN[1][:, kb * P:(kb + 1) * P], mx_p[t % 2][:, kb * P:(kb + 1) * P], ident)
                mm.then_inc(turned, 1)

            def weigh_values(i, t):
                if t == 0:
                    pe.wait_ge(sb_out_copied, i + 1)
                pe.wait_ge(turned_copied, i * (2 * NT + 1) + 2 * t + 1)
                for kb in range(t + 1):
                    mm = pe.matmul(SUM[:, t * P:(t + 1) * P], df_pT[:, kb * P:(kb + 1) * P],
                                   df_v[:, kb * P:(kb + 1) * P], start=(kb == 0), stop=(kb == t))
                mm.then_inc(df_out_done, 1)
                pe.wait_ge(turned_copied, i * (2 * NT + 1) + 2 * t + 2)
                for kb in range(NM):
                    mm = pe.matmul(MXOUT[:, t * P:(t + 1) * P], mem_v[:, kb * P:(kb + 1) * P],
                                   mx_pT[:, kb * P:(kb + 1) * P], start=(kb == 0), stop=(kb == NM - 1))
                if t == NT - 1:
                    mm.then_inc(mx_out_done, 1)

            def softmax_part(i, ahead):
                def fill(u, half=None):
                    if ahead:
                        project(i + 1, u, half)

                tile_scores(i, 0)
                fill(0)
                tile_scores(i, 1)
                turn(i, 0)
                fill(1, 0)
                weigh_values(i, 0)
                tile_scores(i, 2)
                fill(1, 1)
                turn(i, 1)
                weigh_values(i, 1)
                tile_scores(i, 3)
                fill(2, 0)
                turn(i, 2)
                fill(2, 1)
                weigh_values(i, 2)
                turn(i, 3)
                fill(3, 0)
                weigh_values(i, 3)
                fill(3, 1)
                if ahead:
                    z_block(i + 1, 0, 0)
                    z_block(i + 1, 0, 1)
                pe.wait_ge(normed_ready, i + 1)
                for t in range(NT):
                    mm = pe.transpose(TURN[0][:, t * P:(t + 1) * P], df_on[:, t * P:(t + 1) * P], ident)
                mm.then_inc(turned, 1)

            def stick_part(i):
                z_block(i, 0, 2)
                project(i, 4)
                z_block(i, 0, 3)
                project(i, 5)
                z_block(i, 1, 0)
                z_block(i, 1, 1)
                project(i, 6)
                z_block(i, 1, 2)
                project(i, 7)
                z_block(i, 1, 3)
                project(i, 8)
                stick_block(i, 0, 0)
                stick_block(i, 0, 1)
                project(i, 9)
                project(i, 10)
                stick_block(i, 0, 2)
                stick_block(i, 0, 3)
                project(i, 11)
                stick_block(i, 1, 0)
                project(i, 12)
                stick_block(i, 1, 1)
                stick_block(i, 1, 2)
                project(i, 13)
                stick_block(i, 1, 3)
                stick_sum(i)

            for u in range(4):
                project(0, u)
            pe.wait_ge(const_loaded, 16 * CONST_LOADS)
            z_block(0, 0, 0)
            z_block(0, 0, 1)
            with pe.Fori(0, ROUNDS - 1) as i:
                stick_part(i)
                softmax_part(i, True)
            stick_part(ROUNDS - 1)
            softmax_part(ROUNDS - 1, False)

            pe.wait_ge(turned_copied, ROUNDS * (2 * NT + 1))
            with pe.Fori(0, FT) as f:
                for b in range(NB):
                    pe.wait_ge(w_split, f * NB + b + WBLOCKS + 1)
                    pe.wait_ge(gate_ready, f * NB + b + 1)
                    for k in range(KD):
                        mm = triple(GATE[b][:, :], w_parts(b, k), [xT_hi[:, k, :], xT_lo[:, k, :]],
                                    start=(k == 0), stop=(k == KD - 1))
                    mm.then_inc(gate_done, 1)
                    pe.wait_ge(wb_loaded[b], f * 16 + 16)
                    pe.wait_ge(branch_used, f * NB + b + 1)
                    for k in range(ROUNDS):
                        mm = pe.matmul(BRANCH[b][:, :], w_br[:, b, k, :], o_branch[:, b, k, :],
                                       start=(k == 0), stop=(k == ROUNDS - 1))
                    mm.then_inc(branch_done, 1)

            pe.wait_ge(merged_ready, FT)
            pe.wait_ge(gate_ready, FT * NB + NB)
            for f in range(FT):
                n = WBLOCKS + FT * NB + f
                pe.wait_ge(w_split, n + 1)
                for t in range(NT):
                    for c in range(2):
                        mm = triple(MIX[t][c][:, :], [m[:, f, t * P:(t + 1) * P] for m in (mergedT_hi, mergedT_lo)],
                                    w_parts(n % WRING, c, 512), start=(f == 0), stop=(f == FT - 1))
                    if f == FT - 1:
                        mm.then_inc(mix_done, 1)
                if f < FT - 1:
                    mm.then_inc(mix_block_done, 1)
            for t in range(NT):
                pe.wait_ge(x1_ready, t + 1)
                for k in range(KD):
                    mm = pe.transpose(MIX[t][k // 4][:, (k % 4) * P:(k % 4 + 1) * P], x1[:, t, k * P:(k + 1) * P], ident)
                    if k % 4 == 3:
                        mm.then_inc(x1_turned, 1)

            def query_matmuls(h, first, n):
                for j in range(first, first + n):
                    u, k = j // KD, j % KD
                    if k == 0:
                        pe.wait_ge(wq_split, h * 2 + u + 1)
                    mm = triple(QUERY[u][:, :], [w[:, u, k, :] for w in wqs], [xT_hi[:, k, :], xT_lo[:, k, :]],
                                start=(k == 0), stop=(k == KD - 1))
                    if k == KD - 1:
                        mm.then_inc(query_done, 1)

            def key_scores(h, half, head=1):
                if half == 0:
                    pe.wait_ge(keys_loaded, h * 16 + 16)
                    pe.wait_ge(query_copied, h * 2 + 2)
                    if head > 0:
                        pe.wait_ge(keyscore_copied, h * 2)
                for t in (2 * half, 2 * half + 1):
                    for u in range(2):
                        c = (t % 2) * 2 * NK + u * NK
                        mm = pe.matmul(KEYSCORE[half][:, c:c + NK], peer_qT[:, u, t * P:(t + 1) * P], keysT[:, u, :],
                                       start=True, stop=True)
                mm.then_inc(keyscore_done, 1)

            def sum_rows(h, t, e):
                pe.wait_ge(diag_ready, (h * NT + t) * TOPK + e + 1)
                if e == 0:
                    pe.wait_ge(vsum_used, h * NT + t + 1)
                for n in range(2):
                    mm = pe.matmul(VSUM[t % 2][n][:, :], diag[:, e % RING, :],
                                   rows[:, e % RING, D + n * 512:D + (n + 1) * 512],
                                   start=(e == 0), stop=(e == TOPK - 1))
                mm.then_inc(row_used, 1)

            def experts(h, ahead):
                for t in range(NT):
                    for e in range(TOPK):
                        sum_rows(h, t, e)
                        if ahead and t == 0 and 2 <= e < 10:
                            query_matmuls(h + 1, 2 * (e - 2), 2)
                        if ahead and t == 0 and e in (12, 13):
                            key_scores(h + 1, e - 12)

            pe.sem_inc(row_used, RING)
            pe.wait_ge(x1T_split, 2 * NT)
            query_matmuls(0, 0, 2 * KD)
            key_scores(0, 0, head=0)
            key_scores(0, 1, head=0)
            with pe.Fori(0, HEADS - 1) as h:
                experts(h, True)
            experts(HEADS - 1, False)

        @block.scalar
        def _(act):
            steps = Steps()
            act.wait_ge(const_loaded, 16 * CONST_LOADS)
            act.wait_ge(angle_ready, 1)
            act.activation(rope_sin, rope_r, ACT.Sin).then_inc(sines_ready, 1)
            act.wait_ge(angle_ready, 2)
            act.activation(rope_cos, rope_k, ACT.Sin).then_inc(sines_ready, 1)
            act.wait_ge(lam_ready, 1)
            act.activation(lam_e[:, :], lam_s[:, :], ACT.Exp).then_inc(lam_exp, 1)
            act.sem_inc(score_used, 2)

            def softlog(i, a):
                act.wait_ge(abs_ready, i * 2 * NT + (a + 1) * NT + 2)
                act.activation(soft_log[a], soft_log[a], ACT.Exp).then_inc(act_step, steps.add())
                act.wait_ge(act_step, steps.value())
                act.activation(soft_log[a], soft_log[a], ACT.Ln, bias=one).then_inc(softlog_ready, 1)

            def stick_weights(i, a, kb):
                n = a * NT + kb
                act.wait_ge(score_ready, i * SCORES + n + 1)
                act.activation(sb_aT[a][:, OFF[kb]:OFF[kb] + WIDTH[kb]], SCORE[n % 2][:, 0:WIDTH[kb]],
                               ACT.Exp).then_inc(score_used, 1)

            def softmax_exp(i, t, j):
                n = 2 * NT + 3 * t + j
                w = (t + 1) * P if j < 2 else M
                dst = df_p[t % 2][j] if j < 2 else mx_p[t % 2]
                act.wait_ge(negmax_ready, i * 3 * NT + 3 * t + j + 1)
                c = 3 * t + j
                act.activation(dst[:, 0:w], SCORE[n % 2][:, 0:w], ACT.Exp, bias=neg_max[:, c:c + 1],
                               accum_out=expsum[:, c:c + 1]).then_inc(score_used, 1)

            with act.Fori(0, ROUNDS) as i:
                steps.enter(i, 2 + 2)
                for a in range(2):
                    softlog(i, a)
                for a in range(2):
                    for kb in range(NT):
                        stick_weights(i, a, kb)
                for t in range(NT):
                    for j in range(3):
                        softmax_exp(i, t, j)
                act.wait_ge(df_out_done, i * NT + NT)
                for t in range(NT):
                    ins = act.activation(df_sq[:, t * P:(t + 1) * P], SUM[:, t * P:(t + 1) * P], ACT.Square,
                                         accum_out=df_ss[:, t:t + 1])
                ins.then_inc(act_step, steps.add())
                act.wait_ge(act_step, steps.value())
                act.activation(df_ln[:, :], df_ss[:, :], ACT.Ln, bias=eps, scale=1.0 / P).then_inc(act_step, steps.add())
                act.wait_ge(act_step, steps.value())
                act.activation(df_rms[:, :], df_ln[:, :], ACT.Exp, scale=-0.5).then_inc(rms_ready, 1)
                steps.leave(ROUNDS)

            act.sem_inc(gate_ready, NB)
            with act.Fori(0, FT) as f:
                for b in range(NB):
                    act.wait_ge(gate_done, f * NB + b + 1)
                    act.wait_ge(branch_used, f * NB + b + 1)
                    act.activation(gate[:, b, :], GATE[b][:, :], ACT.Sigmoid,
                                   bias=b_gate[:, b, bass.ds(f, 1)]).then_inc(gate_ready, 1)

            def rough_rstd(n):
                act.wait_ge(var_ready, n + 1)
                t = n % NT
                act.activation(ln_l[:, t:t + 1], ln_v[:, t:t + 1], ACT.Ln).then_inc(act_step, steps.add())
                act.wait_ge(act_step, steps.value())
                act.activation(ln_r[:, t:t + 1], ln_l[:, t:t + 1], ACT.Exp, scale=-0.5).then_inc(rstd_ready, 1)

            def scale_rows(src, n):
                act.wait_ge(scale_ready, n + 1)
                t = n % NT
                act.activation(src, src, ACT.Identity, bias=ln_b[:, t:t + 1], scale=ln_u[:, t:t + 1]).then_inc(scaled, 1)

            def copy_x1T(t):
                for half in range(2):
                    act.wait_ge(x1_turned, 2 * t + half + 1)
                    act.activation(xT_hi[:, 4 * half:4 * half + 4, t * P:(t + 1) * P],
                                   MIX[t][half][:, :].rearrange("p (k c) -> p k c", k=4), ACT.Copy
                                   ).then_inc(x1T_rounded, 1)

            rough_rstd(0)
            for t in range(NT):
                if t < NT - 1:
                    rough_rstd(t + 1)
                if t >= 2:
                    copy_x1T(t - 2)
                scale_rows(x1[:, t, :], t)
            copy_x1T(NT - 2)
            copy_x1T(NT - 1)

            def copy_queries(h, u):
                act.wait_ge(query_done, h * 2 + u + 1)
                act.activation(peer_qT[:, u, :], QUERY[u][:, :], ACT.Copy).then_inc(query_copied, 1)

            def copy_keyscores(h, half):
                act.wait_ge(keyscore_done, h * 2 + half + 1)
                act.activation(score[:, 2 * half:2 * half + 2],
                               KEYSCORE[half][:, :].rearrange("p (t u n) -> p t u n", t=2, u=2),
                               ACT.Copy).then_inc(keyscore_copied, 1)

            def best_exp(h, t):
                act.wait_ge(negbest_ready, h * NT + t + 1)
                act.activation(best_e[:, :], best_v[:, :], ACT.Exp, bias=neg_best[:, :],
                               accum_out=best_z[:, :]).then_inc(bestexp_ready, 1)

            def gelu_group(h, t, g):
                n = (h * NT + t) * (TOPK // GROUP) + g
                act.wait_ge(hid_ready, n + 1)
                c = slice(g * GROUP, (g + 1) * GROUP)
                act.activation(gel[:, t, c], hid[:, t, c], ACT.Gelu).then_inc(gelu_ready, 1)
                act.wait_ge(actw_ready, n + 1)
                for e in range(g * GROUP, (g + 1) * GROUP):
                    if e % GROUP == 0:
                        act.wait_ge(row_used, n * GROUP + GROUP)
                    act.activation(diag[:, e % RING, :], ident, ACT.Copy,
                                   scale=act_w[:, t, e:e + 1]).then_inc(diag_ready, 1)

            def experts(h, ahead):
                for t in range(NT):
                    for g in range(TOPK // GROUP):
                        gelu_group(h, t, g)
                        if ahead and t == 0 and g in (3, 5):
                            copy_queries(h + 1, (g - 3) // 2)
                        if not ahead and t >= 1 and g == 1:
                            rough_rstd(NT + t - 1)
                        if not ahead and t >= 1 and g == 3:
                            scale_rows(acc[:, t - 1, :], NT + t - 1)
                    if ahead or t < 2:
                        best_exp(h, t + 2) if t < 2 else best_exp(h + 1, t - 2)
                    if ahead and t == 1:
                        act.wait_ge(chosen_ready, (h + 1) * NT)
                        copy_keyscores(h + 1, 0)
                        copy_keyscores(h + 1, 1)

            copy_queries(0, 0)
            copy_queries(0, 1)
            copy_keyscores(0, 0)
            copy_keyscores(0, 1)
            best_exp(0, 0)
            best_exp(0, 1)
            with act.Fori(0, HEADS - 1) as h:
                experts(h, True)
            experts(HEADS - 1, False)
            rough_rstd(2 * NT - 1)
            scale_rows(acc[:, NT - 1, :], 2 * NT - 1)

        @block.vector
        def _(dve):
            steps = Steps()

            def then(ins):
                ins.then_inc(dve_step, steps.add())
                dve.wait_ge(dve_step, steps.value())

            def unit(i, u):
                seg, src = UNITS[u], PROJ[u % 2]
                dve.wait_ge(unit_done, i * NU + u + 1)
                if seg in (SBQ, DFQ):
                    dst = sb_qT if seg == SBQ else df_raw[0]
                    dve.tensor_scalar(dst, src[:, :], QSCALE, None, ALU.mult).then_inc(unit_used, 1)
                elif seg == MXQ:
                    dve.tensor_scalar(mx_qT, src[:, :], MXSCALE, None, ALU.mult).then_inc(unit_used, 1)
                elif seg in ("swap_q", "swap_k"):
                    raw = df_raw[seg == "swap_k"]
                    dve.tensor_tensor(swapped, src[:, :], rope_sin, ALU.mult).then_inc(unit_used, 1)
                    then(dve.tensor_tensor(raw, raw, rope_cos, ALU.mult))
                    dve.wait_ge(unit_used, i * NU + u + 1 + 2)
                    then(dve.tensor_tensor(raw, raw, swapped, ALU.add))
                elif seg in (MXK, MXV):
                    dve.tensor_copy(mem_kT if seg == MXK else swapped[:, 0:M], src[:, 0:M]).then_inc(unit_used, 1)
                elif seg == "turn_mx":
                    dve.tensor_copy(mem_v, src[:, 0:M]).then_inc(unit_used, 1)
                else:
                    dst = {SBK: sb_kT, SBV: swapped, DFK: df_raw[1], DFV: swapped, "turn_sb": sb_v, "turn_df": df_v}[seg]
                    dve.tensor_copy(dst, src[:, :]).then_inc(unit_used, 1)

            dve.sem_inc(unit_used, 2)
            dve.sem_inc(abs_ready, 2)
            dve.sem_inc(mx_out_used, 1)
            for k in range(KD):
                dve.wait_ge(xT_loaded[k], 16)
                dve.tensor_copy(xT_hi[:, k, :], xT_raw[:, k, :]).then_inc(xT_rounded, 1)
                dve.wait_ge(xT_rounded, k + 1)
                dve.tensor_tensor(xT_lo[:, k, :], xT_raw[:, k, :], xT_hi[:, k, :].bitcast(F32),
                                  ALU.subtract).then_inc(xT_split, 1)
            dve.wait_ge(const_loaded, 16 * CONST_LOADS)
            pos_f, angle = df_raw[0], df_raw[1]
            then(dve.tensor_copy(pos_f, pos_i))
            then(dve.tensor_scalar(angle, pos_f, inv_freq, None, ALU.mult))
            for j in range(2):
                k, r = (rope_cos, rope_r) if j == 0 else (rope_cos, rope_k)
                then(dve.tensor_scalar(k, angle, 1.0 / TWO_PI, 0.25 * j, ALU.mult, ALU.add))
                then(dve.tensor_scalar(k, k, ROUND_MAGIC, None, ALU.add))
                then(dve.tensor_scalar(k, k, -ROUND_MAGIC, None, ALU.add))
                then(dve.scalar_tensor_tensor(r, k, -PI_A, angle, ALU.mult, ALU.add))
                then(dve.scalar_tensor_tensor(r, k, -PI_B, r, ALU.mult, ALU.add))
                then(dve.scalar_tensor_tensor(r, k, -PI_C, r, ALU.mult, ALU.add))
                if j == 1:
                    then(dve.tensor_scalar(r, r, TWO_PI / 4, None, ALU.add))
                dve.tensor_scalar(r, r, PI_TOP, -PI_TOP, ALU.min, ALU.max).then_inc(angle_ready, 1)
                unit(0, j)
            dve.wait_ge(memT_loaded, 16)
            dve.tensor_copy(memTs[0], memT_raw).then_inc(memT_rounded, 1)
            dve.wait_ge(memT_rounded, 1)
            dve.tensor_tensor(memTs[1], memT_raw, memTs[0].bitcast(F32), ALU.subtract).then_inc(memT_split, 1)
            dve.wait_ge(memT_split, 1)
            then(dve.tensor_tensor(lam_pr[:, :, :], lam_in[:, 0:4:2, :], lam_in[:, 1:4:2, :], ALU.mult))
            dve.tensor_reduce(lam_s[:, :], lam_pr[:, :, :], AX_X, ALU.add).then_inc(lam_ready, 1)
            then(dve.tensor_scalar(df_g8[:, :], df_g[:, :], 1.0 - LAMBDA_INIT, None, ALU.mult))
            dve.wait_ge(sines_ready, 2)
            then(dve.tensor_scalar(rope_sin, rope_sin, rope_sign, None, ALU.mult))
            dve.wait_ge(lam_exp, 1)
            then(dve.scalar_tensor_tensor(neg_lam[:, :], lam_e[:, 1:2], -LAMBDA_INIT, lam_e[:, 0:1],
                                          ALU.add, ALU.subtract))

            def take_abs(i, a, kb):
                n = a * NT + kb
                w = WIDTH[kb]
                dve.wait_ge(z_ready, i * 2 * NT + n + 1)
                positive = softplus[a][:, OFF[kb]:OFF[kb] + w]
                then(dve.tensor_scalar(positive, SOFT[n % 2][:, 0:w], 0.0, None, ALU.max))
                dve.scalar_tensor_tensor(soft_log[a][:, OFF[kb]:OFF[kb] + w], positive, -2.0, SOFT[n % 2][:, 0:w],
                                         ALU.mult, ALU.add).then_inc(abs_ready, 1)

            def take_softplus(i, a):
                dve.wait_ge(softlog_ready, i * 2 + a + 1)
                dve.tensor_tensor(softplus[a], softplus[a], soft_log[a], ALU.add).then_inc(softplus_ready, 1)

            def neg_maxima(i, t):
                for j in range(3):
                    n = 2 * NT + 3 * t + j
                    w = (t + 1) * P if j < 2 else M
                    dve.wait_ge(score_ready, i * SCORES + n + 1)
                    dve.tensor_reduce(neg_max[:, 3 * t + j:3 * t + j + 1], SCORE[n % 2][:, 0:w], AX_X, ALU.max,
                                      negate=True).then_inc(negmax_ready, 1)

            def probabilities(i, t):
                c = 3 * t
                dve.wait_ge(score_used, i * SCORES + 2 * NT + c + 3 + 2)
                w = (t + 1) * P
                p0, p1 = df_p[t % 2][0][:, 0:w], df_p[t % 2][1][:, 0:w]
                then(dve.reciprocal(exprec[:, c:c + 3], expsum[:, c:c + 3]))
                then(dve.tensor_scalar(p1, p1, exprec[:, c + 1:c + 2], neg_lam[:, :], ALU.mult, ALU.mult))
                dve.scalar_tensor_tensor(p0, p0, exprec[:, c:c + 1], p1, ALU.mult, ALU.add).then_inc(probs_ready, 1)
                dve.tensor_scalar(mx_p[t % 2], mx_p[t % 2], exprec[:, c + 2:c + 3], None,
                                  ALU.mult).then_inc(probs_ready, 1)

            def copy_turned(i, t):
                dve.wait_ge(turned, i * (2 * NT + 1) + 2 * t + 1)
                dve.tensor_copy(df_pT[:, 0:(t + 1) * P], TURN[0][:, 0:(t + 1) * P]).then_inc(turned_copied, 1)
                dve.wait_ge(turned, i * (2 * NT + 1) + 2 * t + 2)
                dve.tensor_copy(mx_pT, TURN[1][:, 0:M]).then_inc(turned_copied, 1)

            def stick_part(i):
                take_abs(i, 0, 2)
                unit(i, 4)
                take_abs(i, 0, 3)
                unit(i, 5)
                take_abs(i, 1, 0)
                take_abs(i, 1, 1)
                take_softplus(i, 0)
                unit(i, 6)
                take_abs(i, 1, 2)
                unit(i, 7)
                take_abs(i, 1, 3)
                unit(i, 8)
                take_softplus(i, 1)
                for u in range(9, NU):
                    unit(i, u)

            def softmax_part(i, ahead):
                def fill(u):
                    if ahead:
                        unit(i + 1, u)

                dve.wait_ge(sb_out_done, i + 1)
                dve.tensor_copy(o_branch[:, 0, at_round(i), :], SUM[:, :].rearrange("p (o t) -> p o t", o=1)
                                ).then_inc(sb_out_copied, 1)
                neg_maxima(i, 0)
                probabilities(i, 0)
                fill(0)
                neg_maxima(i, 1)
                copy_turned(i, 0)
                probabilities(i, 1)
                neg_maxima(i, 2)
                fill(1)
                copy_turned(i, 1)
                probabilities(i, 2)
                neg_maxima(i, 3)
                copy_turned(i, 2)
                probabilities(i, 3)
                fill(2)
                copy_turned(i, 3)
                dve.wait_ge(mx_out_done, i + 1)
                dve.tensor_copy(o_branch[:, 2, at_round(i), :], MXOUT[:, :].rearrange("p (o t) -> p o t", o=1)
                                ).then_inc(mx_out_used, 1)
                fill(3)
                dve.wait_ge(rms_ready, i + 1)
                dve.tensor_tensor(df_on.rearrange("p (t d) -> p t d", t=NT),
                                  SUM[:, :].rearrange("p (t d) -> p t d", t=NT),
                                  df_rms[:, :].unsqueeze(2).to_broadcast([P, NT, P]), ALU.mult).then_inc(normed_ready, 1)
                if ahead:
                    take_abs(i + 1, 0, 0)
                    take_abs(i + 1, 0, 1)
                dve.wait_ge(turned, (i + 1) * (2 * NT + 1))
                dve.tensor_scalar(o_branch[:, 1, at_round(i), :], TURN[0][:, :].rearrange("p (o t) -> p o t", o=1),
                                  df_g8[:, :], None, ALU.mult).then_inc(turned_copied, 1)

            def at_round(i):
                return slice(i, i + 1) if isinstance(i, int) else bass.ds(i, 1)

            for u in range(2, 4):
                unit(0, u)
            take_abs(0, 0, 0)
            take_abs(0, 0, 1)
            with dve.Fori(0, ROUNDS - 1) as i:
                steps.enter(i, 2 * 2 + 4 * NT)
                stick_part(i)
                softmax_part(i, True)
                steps.leave(ROUNDS - 1)
            stick_part(ROUNDS - 1)
            softmax_part(ROUNDS - 1, False)

            dve.sem_inc(branch_used, NB)
            with dve.Fori(0, FT) as f:
                steps.enter(f, 3)
                for b in range(NB):
                    dve.wait_ge(gate_ready, f * NB + b + 1 + NB)
                    dve.wait_ge(branch_done, f * NB + b + 1)
                    dve.tensor_tensor(part_sum[:, b, :], gate[:, b, :], BRANCH[b][:, :],
                                      ALU.mult).then_inc(branch_used, 1)
                    dve.wait_ge(branch_used, f * NB + b + 1 + NB)
                    if b == 1:
                        then(dve.tensor_tensor(part_sum[:, 0, :], part_sum[:, 0, :], part_sum[:, 1, :], ALU.add))
                then(dve.tensor_tensor(part_sum[:, 0:1, :], part_sum[:, 0:1, :], part_sum[:, 2:3, :], ALU.add))
                then(dve.tensor_copy(mergedT_hi[:, bass.ds(f, 1), :], part_sum[:, 0:1, :]))
                dve.tensor_tensor(mergedT_lo[:, bass.ds(f, 1), :], part_sum[:, 0:1, :],
                                  mergedT_hi[:, bass.ds(f, 1), :].bitcast(F32), ALU.subtract).then_inc(merged_ready, 1)
                dve.wait_ge(merged_ready, f + 1)
                steps.leave(FT)

            def variance(src, t):
                for n in range(2):
                    ins = dve.bn_stats(stats[:, t, n, :], src[:, n * 512:(n + 1) * 512])
                then(ins)
                then(dve.bn_aggr(mean_var[:, t, :], stats[:, t, :, :].rearrange("p n c -> p (n c)")))
                dve.tensor_scalar(ln_v[:, t:t + 1], mean_var[:, t, 1:2], LN_EPS, None, ALU.add).then_inc(var_ready, 1)

            def sharpen(t, n):
                dve.wait_ge(rstd_ready, n + 1)
                r, v, u = ln_r[:, t:t + 1], ln_v[:, t:t + 1], ln_u[:, t:t + 1]
                then(dve.tensor_scalar(ln_t[:, t:t + 1], r, r, v, ALU.mult, ALU.mult))
                then(dve.tensor_scalar(ln_t[:, t:t + 1], ln_t[:, t:t + 1], -0.5, 1.5, ALU.mult, ALU.add))
                then(dve.tensor_tensor(u, ln_t[:, t:t + 1], r, ALU.mult))
                dve.tensor_scalar(ln_b[:, t:t + 1], mean_var[:, t, 0:1], u, -1.0, ALU.mult, ALU.mult).then_inc(scale_ready, 1)

            def gain(src, n, gb):
                dve.wait_ge(scaled, n + 1)
                then(dve.tensor_tensor(src, src, gb[:, 0, :], ALU.mult))
                return dve.tensor_tensor(src, src, gb[:, 1, :], ALU.add)

            def add_mix(t):
                dve.wait_ge(mix_done, t + 1)
                for n in range(2):
                    c = slice(n * 512, (n + 1) * 512)
                    ins = dve.scalar_tensor_tensor(x1[:, t, c], x_nat[:, t, c], ALPHA, MIX[t][n][:, :],
                                                   ALU.mult, ALU.add)
                ins.then_inc(mix_used, 1)
                dve.wait_ge(mix_used, t + 1)
                variance(x1[:, t, :], t)

            def low_x1T(t):
                for half in range(2):
                    dve.wait_ge(x1T_rounded, 2 * t + half + 1)
                    c = (slice(None), slice(4 * half, 4 * half + 4), slice(t * P, (t + 1) * P))
                    dve.tensor_tensor(xT_lo[c], MIX[t][half][:, :].rearrange("p (k c) -> p k c", k=4),
                                      xT_hi[c].bitcast(F32), ALU.subtract).then_inc(x1T_split, 1)

            dve.wait_ge(xnat_loaded, 16)
            dve.wait_ge(ln1_loaded, 32)
            add_mix(0)
            for t in range(1, NT + 3):
                if t < NT:
                    add_mix(t)
                if 0 <= t - 2 < NT:
                    gain(x1[:, t - 2, :], t - 2, ln1_gb).then_inc(x1_ready, 1)
                if t - 1 < NT:
                    sharpen(t - 1, t - 1)
                if 0 <= t - 3 < NT:
                    low_x1T(t - 3)

            def choose(h, t):
                dve.sem_clear(choose_step)
                chain = Steps()

                def chosen_then(ins):
                    ins.then_inc(choose_step, chain.add())
                    dve.wait_ge(choose_step, chain.value())

                dve.wait_ge(keyscore_copied, h * 2 + t // 2 + 1)
                dve.sem_inc(choices_begun, 1)
                first, rest = slice(0, 8), slice(8, TOPK)
                s = score[:, t]
                for u in range(2):
                    ins = dve.max(top_v[:, u, first], s[:, u, :])
                chosen_then(ins)
                for u in range(2):
                    dve.max_index(top_i[:, u, first], top_v[:, u, first], s[:, u, :])
                    ins = dve.match_replace(score_cut[:, u, :], top_v[:, u, first], s[:, u, :], NEG_BIG)
                chosen_then(ins)
                for u in range(2):
                    ins = dve.max(top_v[:, u, rest], score_cut[:, u, :])
                chosen_then(ins)
                for u in range(2):
                    ins = dve.max_index(top_i[:, u, rest], top_v[:, u, rest], score_cut[:, u, :])
                ins = dve.tensor_tensor(cand.rearrange("p (i j) -> p i j", i=TOPK),
                                        top_v[:, 0, :].unsqueeze(2).to_broadcast([P, TOPK, TOPK]),
                                        top_v[:, 1, :].unsqueeze(1).to_broadcast([P, TOPK, TOPK]), ALU.add)
                chosen_then(ins)
                dve.tensor_copy(top_f[:, :, :], top_i[:, :, :])
                chosen_then(dve.max(best_v[:, first], cand))
                chosen_then(dve.tensor_scalar(neg_best[:, :], best_v[:, 0:1], -1.0, None, ALU.mult))
                dve.max_index(best_i[:, first], best_v[:, first], cand)
                chosen_then(dve.match_replace(cand_cut, best_v[:, first], cand, NEG_BIG))
                chosen_then(dve.max(best_v[:, rest], cand_cut))
                dve.sem_inc(negbest_ready, 1)
                chosen_then(dve.max_index(best_i[:, rest], best_v[:, rest], cand_cut))
                dve.tensor_scalar(best_ij[:, 0, :], best_i[:, :], 4, None, ALU.logical_shift_right)
                chosen_then(dve.tensor_scalar(best_ij[:, 1, :], best_i[:, :], TOPK - 1, None, ALU.bitwise_and))
                chosen_then(dve.tensor_copy(best_f[:, :, :], best_ij[:, :, :]))
                for u in range(2):
                    ins = dve.tensor_tensor(onehot[:, u], iota16.unsqueeze(1).to_broadcast([P, TOPK, TOPK]),
                                            best_f[:, u, :].unsqueeze(2).to_broadcast([P, TOPK, TOPK]), ALU.is_equal)
                chosen_then(ins)
                for u in range(2):
                    ins = dve.tensor_tensor(onehot[:, u], onehot[:, u],
                                            top_f[:, u, :].unsqueeze(1).to_broadcast([P, TOPK, TOPK]), ALU.mult)
                chosen_then(ins)
                chosen_then(dve.tensor_reduce(chosen[:, :, :], onehot, AX_X, ALU.add))
                dve.wait_ge(bestexp_ready, h * NT + t + 1)
                chosen_then(dve.reciprocal(best_r[:, :], best_z[:, :]))
                chosen_then(dve.tensor_scalar(weight[:, t, :], best_e[:, :], best_r[:, :], None, ALU.mult))
                dve.scalar_tensor_tensor(ids[:, t, :], chosen[:, 0, :], float(NK), chosen[:, 1, :],
                                         ALU.mult, ALU.add).then_inc(chosen_ready, 1)

            def weigh(h, t, g):
                n = (h * NT + t) * (TOPK // GROUP) + g
                dve.wait_ge(gelu_ready, n + 1)
                c = slice(g * GROUP, (g + 1) * GROUP)
                dve.tensor_tensor(act_w[:, t, c], gel[:, t, c], weight[:, t, c], ALU.mult).then_inc(actw_ready, 1)

            def add_sums(h, t):
                dve.wait_ge(row_used, (h * NT + t + 1) * TOPK + RING)
                for n in range(2):
                    c = slice(n * 512, (n + 1) * 512)
                    ins = dve.tensor_tensor(acc[:, t, c], acc[:, t, c], VSUM[t % 2][n][:, :], ALU.add)
                ins.then_inc(vsum_used, 1)

            def out_variance(t):
                dve.wait_ge(vsum_used, (HEADS - 1) * NT + t + 1 + 2)
                variance(acc[:, t, :], t)

            def out_gain(t):
                gain(acc[:, t, :], NT + t, ln2_gb).then_inc(out_ready, 1)

            def experts(h, ahead):
                for t in range(NT):
                    for g in range(TOPK // GROUP):
                        for e in range(g * GROUP, (g + 1) * GROUP):
                            dve.wait_ge(row_loaded[e % RING], ((h * NT + t) * (TOPK // RING) + e // RING) * 16 + 16)
                            ins = dve.tensor_tensor_reduce(rows[:, e % RING, 0:D], rows[:, e % RING, 0:D], x1[:, t, :],
                                                           1.0, 0.0, ALU.mult, ALU.add, hid[:, t, e:e + 1])
                        ins.then_inc(hid_ready, 1)
                        if g >= 1:
                            weigh(h, t, g - 1)
                        if t >= 1 and g == 1:
                            add_sums(h, t - 1)
                        if not ahead and t >= 1:
                            if g == 1:
                                out_variance(t - 1)
                            if g == 3:
                                sharpen(t - 1, NT + t - 1)
                            if g == 5:
                                out_gain(t - 1)
                    weigh(h, t, TOPK // GROUP - 1)
                    if t < 2:
                        choose(h, t + 2)
                    elif ahead:
                        choose(h + 1, t - 2)
                add_sums(h, NT - 1)

            dve.sem_inc(vsum_used, 2)
            choose(0, 0)
            choose(0, 1)
            dve.wait_ge(acc_ready, NT)
            dve.wait_ge(ln2_loaded, 32)
            with dve.Fori(0, HEADS - 1) as h:
                experts(h, True)
            experts(HEADS - 1, False)
            out_variance(NT - 1)
            sharpen(NT - 1, 2 * NT - 1)
            out_gain(NT - 1)


def kernel(**inputs):
    import ml_dtypes
    import numpy as np
    import concourse.bacc as bacc
    from concourse import mybir as mb
    from concourse.bass_utils import run_bass_kernel_spmd

    a = {k: np.asarray(v) for k, v in inputs.items()}
    w_in = a["w_in"][0].reshape(KD, P, 7, ROUNDS, P).transpose(3, 2, 1, 0, 4)
    w_kv = a["w_mem_kv"][0].reshape(KD, P, 2, ROUNDS, P).transpose(3, 2, 1, 0, 4)
    w_gate = a["w_gate"][0].reshape(KD, P, NB, FT, P).transpose(3, 2, 1, 0, 4)
    w_br = np.stack([a["w_br_sb"][0], a["w_br_df"][0], a["w_br_mx"][0]])
    w_br = w_br.reshape(NB, ROUNDS, P, FT, P).transpose(3, 0, 2, 1, 4)
    arrays = {
        "xT": a["x"][0].T,
        "x": a["x"][0].reshape(NT, P, D).transpose(1, 0, 2),
        "memT": a["mem"][0].T.reshape(KD, P, M).transpose(1, 0, 2),
        "pos": a["positions"][0],
        "w_mix": np.concatenate([w_in, w_kv], axis=1).reshape(ROUNDS, SEGS, P, KD * P),
        "lam": a["df_lambda"][0].reshape(-1),
        "df_g": a["df_norm_g"][0].reshape(P, 1),
        "w_gate": w_gate.reshape(FT, NB, P, KD * P),
        "b_gate": a["b_gate"][0].reshape(NB, FT, P).transpose(2, 0, 1),
        "w_br": w_br,
        "w_out": a["w_out"][0].reshape(FT, P, D),
        "ln": np.stack([a["ln1_g"][0], a["ln1_b"][0], a["ln2_g"][0], a["ln2_b"][0]]),
        "w_query": a["w_query"][0].reshape(KD, P, HEADS, 2, P).transpose(2, 1, 3, 0, 4),
        "keysT": a["sub_keys"][0].transpose(0, 3, 1, 2),
        "uv": np.concatenate([a["u_tab"][0], a["v_tab"][0]], axis=1),
    }
    row, col = np.arange(P)[:, None], np.arange(P)[None, :]
    rope, half = HD // 4, HD // 8
    c = np.zeros((P, NCONST), np.float32)
    c[:, C_IDENT:C_IDENT + P] = row == col
    c[:, C_TRI:C_TRI + P] = -1.0 * (row >= col)
    c[:, C_ONES:C_ONES + P] = -1.0
    d = np.arange(P) % HD
    partner = np.where(d < half, np.arange(P) + half, np.arange(P) - half)
    c[:, C_PERM:C_PERM + P] = (row == partner[None, :]) & (d < rope)[None, :]
    freq = (500000.0 ** (-np.arange(0, rope, 2, dtype=np.float32) / rope)).astype(np.float32)
    c[:, C_INV] = np.where(d < rope, freq[d % half], 0.0)
    c[:, C_SIGN] = np.where(d < half, -1.0, np.where(d < rope, 1.0, 0.0))
    c[:, C_EPS] = RMS_EPS
    c[:, C_ONE] = 1.0
    c[:, C_IOTA:C_IOTA + TOPK] = np.arange(TOPK)
    arrays["const"] = c
    m = np.zeros((P, 3, P), np.float32)
    m[:, 0] = row == col
    m[:, 1] = -1e30 * (row >= col)
    m[:, 2] = -1e30 * (col > row)
    arrays["masks"] = m.astype(ml_dtypes.bfloat16)
    arrays = {f"in_{k}": np.ascontiguousarray(v) for k, v in arrays.items()}

    nc = bacc.Bacc("TRN2", target_bir_lowering=False, num_devices=1)
    args = [nc.dram_tensor(k, v.shape, mb.dt.from_np(v.dtype), kind="ExternalInput").ap() for k, v in arrays.items()]
    out = nc.dram_tensor("out", (P, NT, D), F32, kind="ExternalOutput").ap()
    build_layer(nc, *args, out)
    r = run_bass_kernel_spmd(nc, [arrays], core_ids=[0])
    return r.results[0]["out"].transpose(1, 0, 2).reshape(1, T, D)
```

```python
from contextlib import ExitStack

import concourse.bass as bass
from concourse import mybir

F32 = mybir.dt.float32
F32R = mybir.dt.float32r
BF16 = mybir.dt.bfloat16
U32 = mybir.dt.uint32
I32 = mybir.dt.int32
ALU = mybir.AluOpType
ACT = mybir.ActivationFunctionType
AX_X = mybir.AxisListType.X

P = 128
T = 512
NT = T // P
D = 1024
KD = D // P
M = 256
NM = M // P
HD = 64
ROUNDS = 4
SEGS = 9
SBQ, SBK, SBV, DFQ, DFK, DFV, MXQ, MXK, MXV = range(SEGS)
UNITS = [SBQ, SBK, SBV, DFQ, "turn_sb", DFK, "swap_q", "swap_k", DFV, MXQ, "turn_df", MXK, MXV, "turn_mx"]
NU = len(UNITS)
TURNED = {"turn_sb": (SBV, 512), "turn_df": (DFV, 512), "turn_mx": (MXV, 256)}
NB = 3
FT = D // P
HEADS = 8
NK = 128
TOPK = 16
EARLY_GATES = {0: 0, 1: 1, 3: 2}
WRING = 3
WBLOCKS = ROUNDS * SEGS
RING = 8
CLEAR_OF_X = (3 * WRING * D + 6 * T) // (2 * D)
GROUP = 2
LAMBDA_INIT = 0.8 - 0.6
LN_EPS = 1e-5
RMS_EPS = 1e-5
ALPHA = 2.0 ** 0.25
QSCALE = HD ** -0.5
MXSCALE = 128 ** -0.5
SCORES = 5 * NT
CONST_LOADS = 6
REGION_B = 15104
TWO_PI = 6.283185307179586
PI_A = 6.28125
PI_B = 0.0019350051879882812
PI_C = TWO_PI - PI_A - PI_B
ROUND_MAGIC = 12582912.0
PI_TOP = 3.1415925
NEG_BIG = -3.0e38

WIDTH = [T - P * kb for kb in range(NT)]
OFF = [sum(WIDTH[:kb]) for kb in range(NT)]
CAUSAL = sum(WIDTH)

C_IDENT, C_TRI, C_ONES, C_PERM = 0, P, 2 * P, 3 * P
C_INV = 4 * P
C_SIGN = C_INV + 1
C_EPS = C_INV + 2
C_ONE = C_INV + 3
C_IOTA = C_INV + 4
NCONST = C_IOTA + TOPK


class Steps:

    def __init__(self):
        self.base, self.k = 0, 0

    def add(self):
        self.k += 1
        return 1

    def value(self):
        return self.base + self.k

    def enter(self, i, per):
        self.start, self.per = self.base + self.k, per
        self.base, self.k = i * per + self.start, 0

    def leave(self, trips):
        assert self.k == self.per, (self.k, self.per)
        self.base, self.k = self.start + trips * self.per, 0


def build_layer(nc, xT_d, x_d, memT_d, pos_d, w_mix_d, lam_d, df_g_d, w_gate_d, b_gate_d, w_br_d,
                w_out_d, ln_d, w_query_d, keysT_d, uv_d, const_d, masks_d, out_d):
    ctx = ExitStack()
    with ctx:
        def sb(name, shape, dt=F32):
            return ctx.enter_context(nc.sbuf_tensor(name, shape, dt))

        def sem(name):
            return ctx.enter_context(nc.semaphore(name))

        region_a_at = (nc.sbuf_base + 63) // 64 * 64
        region_b_at = region_a_at + 4 * RING * 2 * D
        region_c_at = region_b_at + 4 * REGION_B
        sb("slab", [P, RING * 2 * D + REGION_B + NB * ROUNDS * T + 16])

        def at_offset(name, shape, dt, offset):
            return nc.alloc_sbuf_tensor_at(name, shape, dt, offset=offset)

        region_a = at_offset("region_a", [P, RING * 2 * D], F32, region_a_at)
        rows = region_a[:, :].rearrange("p (r c) -> p r c", r=RING)
        w_raw = region_a[:, 0:WRING * D].rearrange("p (j c) -> p j c", j=WRING)
        w_hi = at_offset("w_hi", [P, WRING, D], F32R, region_a_at + 4 * WRING * D)
        w_lo = at_offset("w_lo", [P, WRING, D], F32R, region_a_at + 8 * WRING * D)
        at = 3 * WRING * D
        rope_cos = region_a[:, at:at + T]
        rope_sin = region_a[:, at + T:at + 2 * T]
        rope_k = region_a[:, at + 2 * T:at + 3 * T]
        rope_r = region_a[:, at + 3 * T:at + 4 * T]
        wo_raw = region_a[:, at:at + D]
        wo_hi = at_offset("wo_hi", [P, D], F32R, region_a_at + 4 * (at + D))
        wo_lo = at_offset("wo_lo", [P, D], F32R, region_a_at + 4 * (at + 2 * D))
        assert 3 * D <= 6 * T
        at += 4 * T
        df_raw = [region_a[:, at + j * T:at + (j + 1) * T] for j in range(2)]
        at += 2 * T
        x_nat = region_a[:, at:at + NT * D].rearrange("p (t d) -> p t d", t=NT)
        o_mx_hi = at_offset("o_mx_hi", [P, ROUNDS, T], F32R, region_a_at + 4 * (at + (NT - 2) * D))
        assert ROUNDS * T == 2 * D
        assert at + NT * D <= RING * 2 * D

        region_b = at_offset("region_b", [P, REGION_B], F32, region_b_at)
        at = 0

        def part(n):
            nonlocal at
            at += n
            assert at <= REGION_B
            return region_b[:, at - n:at]

        xT_raw = part(KD * T).rearrange("p (k t) -> p k t", k=KD)
        memT_raw = part(KD * M).rearrange("p (k m) -> p k m", k=KD)
        at = 0
        sb_qT, sb_kT, sb_v, df_v, mx_qT = part(T), part(T), part(T), part(T), part(T)
        mem_kT, mem_v = part(M), part(M)
        softplus = [part(CAUSAL) for _ in range(2)]
        softplus_lo = [at_offset(f"softplus_lo{a}", [P, CAUSAL], F32R, region_b_at + 4 * (at - (2 - a) * CAUSAL))
                       for a in range(2)]
        sb_aT = [part(CAUSAL) for _ in range(2)]
        df_p = [[part(T) for _ in range(2)] for _ in range(2)]
        df_pT = part(T)
        mx_pT = part(M)
        df_on = part(T)
        df_sq = df_pT
        mx_p = [part(M) for _ in range(2)]
        swapped = part(T)
        pos_i = swapped.bitcast(I32)
        soft_log = [part(CAUSAL) for _ in range(2)]
        soft_log_at = at - 2 * CAUSAL
        softplus_hi = [at_offset(f"softplus_hi{a}", [P, CAUSAL], F32R, region_b_at + 4 * (soft_log_at + a * CAUSAL))
                       for a in range(2)]
        mergedT_hi = at_offset("mergedT_hi", [P, FT, T], F32R, region_b_at)
        mergedT_lo = at_offset("mergedT_lo", [P, FT, T], F32R, region_b_at + 4 * FT * T)
        at = 2 * FT * T
        ln1_gb = part(2 * D).rearrange("p (j d) -> p j d", j=2)
        gate = part(NB * T).rearrange("p (b t) -> p b t", b=NB)
        merged0 = [at_offset(f"merged0_{name}", [P, P], F32R, region_b_at + 4 * (at + j * P))
                   for j, name in enumerate(("hi", "lo"))]
        at += 2 * P
        WBR = ROUNDS * P
        assert soft_log_at == at + WBR
        w_br_hi_all = at_offset("w_br_hi", [P, NB, WBR], F32R, region_b_at + 4 * at)
        at += NB * WBR
        w_br_lo_all = at_offset("w_br_lo", [P, NB, WBR], F32R, region_b_at + 4 * at)
        w_br = part(NB * WBR).rearrange("p (b c) -> p b c", b=NB)
        w_br_hi = [w_br_hi_all[:, (b + 1) % NB, :] for b in range(NB)]
        w_br_lo = [w_br_lo_all[:, b, :] for b in range(NB)]
        at = 0
        acc = part(NT * D).rearrange("p (t d) -> p t d", t=NT)
        assert at <= 2 * FT * T
        at = 2 * FT * T
        ln2_gb = part(2 * D).rearrange("p (j d) -> p j d", j=2)
        score = part(NT * 2 * NK).rearrange("p (t u n) -> p t u n", t=NT, u=2)
        onehot = part(2 * TOPK * TOPK).rearrange("p (u e i) -> p u e i", u=2, e=TOPK)
        diag = part(RING * P).rearrange("p (e c) -> p e c", e=RING)
        w_q = part(2 * D).rearrange("p (u k c) -> p u k c", u=2, k=KD)
        keysT = part(2 * NK).rearrange("p (u n) -> p u n", u=2)

        xT_hi = sb("xT_hi", [P, KD, T], F32R)
        xT_lo = sb("xT_lo", [P, KD, T], F32R)
        memT_hi = sb("memT_hi", [P, KD * M], F32R)
        memT_lo = sb("memT_lo", [P, KD * M], F32R)
        memTs = [m[:, :].rearrange("p (k m) -> p k m", k=KD) for m in (memT_hi, memT_lo)]
        wqs = [m[:, :].rearrange("p (u k c) -> p u k c", u=2, k=KD) for m in (memT_hi, memT_lo)]
        oT = at_offset("oT", [P, NB * ROUNDS * T], F32, region_c_at)
        o_lo_all = at_offset("o_lo", [P, NB, ROUNDS, T], F32R, region_c_at)
        o_hi = [memT_hi[:, :].rearrange("p (i t) -> p i t", i=ROUNDS),
                memT_lo[:, :].rearrange("p (i t) -> p i t", i=ROUNDS), o_mx_hi[:, :, :]]
        o_lo = [o_lo_all[:, b] for b in range(NB)]
        o_branch = oT[:, :].rearrange("p (b i t) -> p b i t", b=NB, i=ROUNDS)
        x1 = oT[:, 0:NT * D].rearrange("p (t d) -> p t d", t=NT)
        at = NT * D
        peer_qT = oT[:, at:at + 2 * T].rearrange("p (u t) -> p u t", u=2)
        at += 2 * T
        score_cut = oT[:, at:at + 2 * NK].rearrange("p (u n) -> p u n", u=2)
        at += 2 * NK
        cand, cand_cut = (oT[:, at + j * TOPK * TOPK:at + (j + 1) * TOPK * TOPK] for j in range(2))
        assert at + 2 * TOPK * TOPK <= NB * ROUNDS * T
        b_gate = sb("b_gate", [P, NB, FT])
        const = sb("const", [P, NCONST])
        neg_sums = sb("neg_sums", [P, 2 * P], F32R)
        masks = sb("masks", [P, 3, P], BF16)
        df_g = sb("df_g", [P, 1])
        df_g8 = sb("df_g8", [P, 1])
        lam_in = sb("lam_in", [P, 4, HD])
        lam_pr = sb("lam_pr", [P, 2, HD])
        lam_s = sb("lam_s", [P, 2])
        lam_e = sb("lam_e", [P, 2])
        neg_lam = sb("neg_lam", [P, 1])
        neg_max = sb("neg_max", [P, 3 * NT])
        expsum = sb("expsum", [P, 3 * NT])
        exprec = sb("exprec", [P, 3 * NT])
        df_ss = sb("df_ss", [P, NT])
        df_ln = sb("df_ln", [P, NT])
        df_rms = sb("df_rms", [P, NT])
        stats = sb("stats", [P, NT, 2, 6])
        mean_var = sb("mean_var", [P, NT, 2])
        ln_v = sb("ln_v", [P, NT])
        ln_l = sb("ln_l", [P, NT])
        ln_r = sb("ln_r", [P, NT])
        ln_t = sb("ln_t", [P, NT])
        ln_u = sb("ln_u", [P, NT])
        top_v = sb("top_v", [P, 2, TOPK])
        top_i = sb("top_i", [P, 2, TOPK], U32)
        top_f = sb("top_f", [P, 2, TOPK])
        best_v = sb("best_v", [P, TOPK])
        best_i = sb("best_i", [P, TOPK], U32)
        best_ij = sb("best_ij", [P, 2, TOPK], U32)
        best_f = sb("best_f", [P, 2, TOPK])
        chosen = sb("chosen", [P, 2, TOPK])
        neg_best = sb("neg_best", [P, 1])
        best_e = sb("best_e", [P, TOPK])
        best_z = sb("best_z", [P, 1])
        best_r = sb("best_r", [P, 1])
        ids = sb("ids", [P, NT, TOPK], U32)
        weight = sb("weight", [P, NT, TOPK])
        hid = sb("hid", [P, NT, TOPK])
        gel = sb("gel", [P, NT, TOPK])
        act_w = sb("act_w", [P, NT, TOPK])

        ident = const[:, C_IDENT:C_IDENT + P]
        neg_tri = neg_sums[:, 0:P]
        neg_ones = neg_sums[:, P:2 * P]
        swap_perm = const[:, C_PERM:C_PERM + P]
        eps = const[:, C_EPS:C_EPS + 1]
        one = const[:, C_ONE:C_ONE + 1]
        iota16 = const[:, C_IOTA:C_IOTA + TOPK]
        inv_freq = const[:, C_INV:C_INV + 1]
        rope_sign = const[:, C_SIGN:C_SIGN + 1]

        bank = [ctx.enter_context(nc.psum_tensor(f"bank{b}", [P, 512], F32)) for b in range(8)]
        PROJ, SOFT, SCORE = bank[0:2], bank[2:4], bank[4:6]
        TURN = [bank[6], bank[3]]
        SUM, MXOUT = bank[7], bank[2]
        GATE, BRANCH = [bank[0], bank[1], bank[4]], [bank[5], bank[2], bank[3]]
        MIX = [[bank[6], bank[7]], [bank[0], bank[1]], [bank[4], bank[5]], [bank[2], bank[3]]]
        VSUM = [[bank[0], bank[1]], [bank[4], bank[5]]]
        QUERY = [bank[2], bank[3]]
        KEYSCORE = [bank[6], bank[7]]
        QUERY0, KEYSCORE0 = bank[6][:, 0:2 * P], bank[7][:, 0:2 * NK]

        def tokens_of(h):
            return P if isinstance(h, int) and h == 0 else 0

        const_loaded, memT_loaded = sem("const_loaded"), sem("memT_loaded")
        xT_loaded = [sem(f"xT_loaded{k}") for k in range(KD)]
        w_loaded = [sem(f"w_loaded{j}") for j in range(WRING)]
        w_rounded, w_split = sem("w_rounded"), sem("w_split")
        wq_rounded, wq_split = sem("wq_rounded"), sem("wq_split")
        xT_rounded, xT_split, memT_rounded, memT_split = (sem("xT_rounded"), sem("xT_split"),
                                                          sem("memT_rounded"), sem("memT_split"))
        unit_done, unit_used = sem("unit_done"), sem("unit_used")
        z_ready, relu_ready = sem("z_ready"), sem("relu_ready")
        abs_ready, softlog_ready, softplus_ready = sem("abs_ready"), sem("softlog_ready"), sem("softplus_ready")
        score_ready, score_used = sem("score_ready"), sem("score_used")
        negmax_ready, probs_ready = sem("negmax_ready"), sem("probs_ready")
        turned, turned_copied = sem("turned"), sem("turned_copied")
        sb_out_done, sb_out_copied = sem("sb_out_done"), sem("sb_out_copied")
        df_out_done, rms_ready, normed_ready = sem("df_out_done"), sem("rms_ready"), sem("normed_ready")
        mx_out_done, mx_out_used = sem("mx_out_done"), sem("mx_out_used")
        dve_step, act_step, choose_step = sem("dve_step"), sem("act_step"), sem("choose_step")
        angle_ready, sines_ready, lam_ready, lam_exp = (sem("angle_ready"), sem("sines_ready"),
                                                        sem("lam_ready"), sem("lam_exp"))
        wb_loaded = [sem(f"wb_loaded{b}") for b in range(NB)]
        gate_done, gate_ready = sem("gate_done"), sem("gate_ready")
        branch_done, branch_used = sem("branch_done"), sem("branch_used")
        o_rounded, o_split, o_last_rounded, o_last_split = (sem("o_rounded"), sem("o_split"),
                                                            sem("o_last_rounded"), sem("o_last_split"))
        sums_ready = sem("sums_ready")
        wb_rounded, wb_split = sem("wb_rounded"), sem("wb_split")
        merged_ready = sem("merged_ready")
        mix_block_done, xnat_loaded, ln1_loaded, ln2_loaded = (sem("mix_block_done"), sem("xnat_loaded"),
                                                            sem("ln1_loaded"), sem("ln2_loaded"))
        wo_loaded, wo_rounded, wo_split, mix0_done = (sem("wo_loaded"), sem("wo_rounded"),
                                                      sem("wo_split"), sem("mix0_done"))
        query0_done, query0_copied, keyscore0_done, keyscore0_copied = (sem("query0_done"), sem("query0_copied"),
                                                                        sem("keyscore0_done"), sem("keyscore0_copied"))
        mix_done, mix_used = sem("mix_done"), sem("mix_used")
        var_ready, rstd_ready, x1_ready = sem("var_ready"), sem("rstd_ready"), sem("x1_ready")
        x1_turned, x1T_rounded, x1T_split, acc_ready = (sem("x1_turned"), sem("x1T_rounded"),
                                                        sem("x1T_split"), sem("acc_ready"))
        wq_loaded, keys_loaded = sem("wq_loaded"), sem("keys_loaded")
        query_done, query_copied = sem("query_done"), sem("query_copied")
        keyscore_done, keyscore_copied = sem("keyscore_done"), sem("keyscore_copied")
        negbest_ready, bestexp_ready, chosen_ready = sem("negbest_ready"), sem("bestexp_ready"), sem("chosen_ready")
        row_loaded = [sem(f"row_loaded{r}") for r in range(RING)]
        row_used = sem("row_used")
        hid_ready, gelu_ready, actw_ready, diag_ready = (sem("hid_ready"), sem("gelu_ready"),
                                                         sem("actw_ready"), sem("diag_ready"))
        vsum_used = sem("vsum_used")
        pool_begun, choices_begun = sem("pool_begun"), sem("choices_begun")
        out_ready, out_stored = sem("out_ready"), sem("out_stored")

        block = ctx.enter_context(nc.Block())

        @block.sync
        def _(sp):
            def load_block(n, slot, src):
                sp.dma_start(w_raw[:, slot, :], src).then_inc(w_loaded[slot], 16)

            load_block(0, 0, w_mix_d[0, 0])
            for k in range(KD):
                sp.dma_start(xT_raw[:, k, :], xT_d[k * P:(k + 1) * P, :]).then_inc(xT_loaded[k], 16)
            sp.dma_start(const[:, :], const_d).then_inc(const_loaded, 16)
            sp.dma_start(pos_i, pos_d.partition_broadcast(P)).then_inc(const_loaded, 16)
            load_block(1, 1, w_mix_d[0, 1])
            sp.dma_start(masks[:, :, :], masks_d).then_inc(const_loaded, 16)
            load_block(2, 2, w_mix_d[0, 2])
            sp.dma_start(lam_in[:, :, :].rearrange("p a b -> p (a b)"),
                         lam_d.partition_broadcast(P)).then_inc(const_loaded, 16)
            sp.dma_start(df_g[:, :], df_g_d).then_inc(const_loaded, 16)
            sp.dma_start(b_gate[:, :, :], b_gate_d).then_inc(const_loaded, 16)
            sp.dma_start(memT_raw, memT_d).then_inc(memT_loaded, 16)
            for s in range(WRING, SEGS):
                sp.wait_ge(w_split, s - WRING + 1)
                load_block(s, s % WRING, w_mix_d[0, s])
            sp.dma_start(x_nat[:, 0:NT - 2], x_d[:, 0:NT - 2]).then_inc(xnat_loaded, 16)
            with sp.Fori(1, ROUNDS) as i:
                for s in range(SEGS):
                    sp.wait_ge(w_split, i * SEGS + s - WRING + 1)
                    load_block(i * SEGS + s, s % WRING, w_mix_d[i, s])

            def load_gate(f, b):
                sp.wait_ge(w_split, f * NB + b + WBLOCKS - WRING + 1)
                load_block(0, b, w_gate_d[f, b])

            for b in range(NB):
                load_gate(0, b)
            sp.wait_ge(sb_out_done, ROUNDS)
            for b in range(NB):
                sp.dma_start(w_br[:, b], w_br_d[0, b].rearrange("p k c -> p (k c)")).then_inc(wb_loaded[b], 16)
            for b in range(NB):
                load_gate(1, b)
            sp.wait_ge(turned_copied, ROUNDS * (2 * NT + 1))
            sp.dma_start(wo_raw, w_out_d[0]).then_inc(wo_loaded, 16)
            for j in range(2):
                sp.dma_start(ln1_gb[:, j, :], ln_d[j].partition_broadcast(P)).then_inc(ln1_loaded, 16)

            def load_branch(f, b):
                sp.wait_ge(branch_done, f * NB - NB + b + 1)
                sp.dma_start(w_br[:, b], w_br_d[f, b].rearrange("p k c -> p (k c)")).then_inc(wb_loaded[b], 16)

            def load_out0(f):
                sp.wait_ge(wo_split, f)
                sp.dma_start(wo_raw, w_out_d[f]).then_inc(wo_loaded, 16)

            def load_out(f):
                n = WBLOCKS + FT * NB + f
                sp.wait_ge(w_split, n - WRING + 1)
                load_block(n, n % WRING, w_out_d[f])

            with sp.Fori(1, FT - 1) as f:
                for b in range(NB):
                    load_branch(f, b)
                load_out0(f)
                for b in range(NB):
                    load_gate(f + 1, b)
            for b in range(NB):
                load_branch(FT - 1, b)
                if b == NB - 1:
                    load_out0(FT - 1)
                load_out(b)
            load_out(NB)
            sp.wait_ge(mix0_done, FT)
            sp.dma_start(w_q, w_query_d[0]).then_inc(wq_loaded, 16)
            sp.dma_start(keysT, keysT_d[0]).then_inc(keys_loaded, 16)
            for f in range(NB + 1, FT):
                load_out(f)
                if f == FT - 3:
                    sp.dma_start(x_nat[:, NT - 2:NT], x_d[:, NT - 2:NT]).then_inc(xnat_loaded, 16)
            sp.wait_ge(x1_ready, NT)
            for j in range(2):
                sp.dma_start(ln2_gb[:, j, :], ln_d[2 + j].partition_broadcast(P)).then_inc(ln2_loaded, 16)
            with sp.Fori(1, HEADS) as h:
                sp.wait_ge(wq_split, h * 2)
                sp.dma_start(w_q, w_query_d[h]).then_inc(wq_loaded, 16)
                sp.wait_ge(keyscore_done, h * 2)
                sp.dma_start(keysT, keysT_d[h]).then_inc(keys_loaded, 16)
            for t in range(NT):
                sp.wait_ge(out_ready, t + 1)
                sp.dma_start(out_d[:, t, :], acc[:, t, :]).then_inc(out_stored, 16)
            sp.wait_ge(out_stored, 16 * NT)

        @block.gpsimd
        def _(pool):
            def split_block(n, slot, uses):
                pool.wait_ge(w_loaded[slot], uses * 16)
                pool.sem_inc(pool_begun, 1)
                pool.tensor_scalar(w_hi[:, slot, :], w_raw[:, slot, :], 1.0, 0.0, ALU.mult,
                                   ALU.add).then_inc(w_rounded, 1)
                pool.wait_ge(w_rounded, n + 1)
                pool.tensor_tensor(w_lo[:, slot, :], w_raw[:, slot, :], w_hi[:, slot, :].bitcast(F32),
                                   ALU.subtract).then_inc(w_split, 1)

            def split_query(h, u):
                hi, lo = (m[:, u].rearrange("p k c -> p (k c)") for m in wqs)
                raw = w_q[:, u].rearrange("p k c -> p (k c)")
                pool.wait_ge(wq_loaded, h * 16 + 16)
                pool.sem_inc(pool_begun, 1)
                pool.tensor_scalar(hi, raw, 1.0, 0.0, ALU.mult, ALU.add).then_inc(wq_rounded, 1)
                pool.wait_ge(wq_rounded, h * 2 + u + 1)
                pool.tensor_tensor(lo, raw, hi.bitcast(F32), ALU.subtract).then_inc(wq_split, 1)

            def split_out(f):
                pool.wait_ge(wo_loaded, f * 16 + 16)
                pool.sem_inc(pool_begun, 1)
                pool.tensor_scalar(wo_hi[:, :], wo_raw, 1.0, 0.0, ALU.mult, ALU.add).then_inc(wo_rounded, 1)
                pool.wait_ge(wo_rounded, f + 1)
                pool.tensor_tensor(wo_lo[:, :], wo_raw, wo_hi[:, :].bitcast(F32), ALU.subtract).then_inc(wo_split, 1)

            def split_gate(f, b):
                pool.wait_ge(gate_done, f * NB - NB + b + 1)
                split_block(f * NB + WBLOCKS + b, b, f + WBLOCKS // WRING + 1)

            def split_branch(f, b):
                pool.wait_ge(wb_loaded[b], f * 16 + 16)
                pool.sem_inc(pool_begun, 1)
                pool.tensor_scalar(w_br_hi[b], w_br[:, b, :], 1.0, 0.0, ALU.mult, ALU.add).then_inc(wb_rounded, 1)
                pool.wait_ge(wb_rounded, f * NB + b + 1)
                pool.tensor_tensor(w_br_lo[b], w_br[:, b, :], w_br_hi[b].bitcast(F32), ALU.subtract).then_inc(wb_split, 1)

            def split_outputs(n, b, rounds):
                c = slice(0, rounds)
                pool.tensor_scalar(o_hi[b][:, c], o_branch[:, b, c], 1.0, 0.0, ALU.mult, ALU.add).then_inc(o_rounded, 1)
                pool.wait_ge(o_rounded, n + 1)
                pool.tensor_tensor(o_lo[b][:, c], o_branch[:, b, c], o_hi[b][:, c].bitcast(F32),
                                   ALU.subtract).then_inc(o_split, 1)

            def gather_tile(h, t, ahead, first=False):
                pool.wait_ge(chosen_ready, h * NT + t + 1)
                for e in range(TOPK):
                    if first and e == RING:
                        for i in range(NT):
                            pool.wait_ge(x1_ready, i + 1)
                            pool.tensor_scalar(acc[:, i, :], x1[:, i, :], ALPHA, 0.0, ALU.mult,
                                               ALU.add).then_inc(acc_ready, 1)
                    n = (h * NT + t) * TOPK + e
                    pool.wait_ge(row_used, n + 1)
                    if first and e == CLEAR_OF_X:
                        pool.wait_ge(mix_used, NT)
                    pool.sem_inc(pool_begun, 1)
                    pool.indirect_dma_start(rows[:, e % RING, :], None, uv_d,
                                            bass.IndirectOffsetOnAxis(ap=ids[:, t, e:e + 1], axis=0)
                                            ).then_inc(row_loaded[e % RING], 16)
                    after = 11 if first else 3
                    if ahead and t == 0 and e in (after, after + 2):
                        u = (e - after) // 2
                        pool.wait_ge(query_done, h * 2 + u + 1)
                        split_query(h + 1, u)

            for s in range(SEGS):
                if s >= WRING:
                    pool.wait_ge(unit_done, UNITS.index(s - WRING) + 1)
                split_block(s, s % WRING, s // WRING + 1)
            with pool.Fori(1, ROUNDS) as i:
                for s in range(SEGS):
                    before = UNITS.index(s - WRING) if s >= WRING else UNITS.index(s - WRING + SEGS) - NU
                    pool.wait_ge(unit_done, i * NU + before + 1)
                    split_block(i * SEGS + s, s % WRING, i * (SEGS // WRING) + s // WRING + 1)
            for b in range(NB):
                pool.wait_ge(unit_done, (ROUNDS - 1) * NU + UNITS.index(MXQ + b) + 1)
                split_block(WBLOCKS + b, b, WBLOCKS // WRING + 1)
            pool.wait_ge(turned_copied, (ROUNDS - 1) * (2 * NT + 1))
            split_outputs(0, 1, ROUNDS - 1)
            pool.wait_ge(mx_out_used, ROUNDS)
            split_outputs(1, 2, ROUNDS - 1)
            pool.wait_ge(sb_out_copied, ROUNDS)
            split_outputs(2, 0, ROUNDS)
            split_branch(0, 0)
            split_branch(0, 1)
            split_gate(1, 0)
            split_gate(1, 1)
            pool.wait_ge(turned_copied, ROUNDS * (2 * NT + 1))
            split_branch(0, 2)
            split_gate(1, 2)
            split_out(0)
            for b in range(NB):
                split_branch(1, b)
            with pool.Fori(2, FT) as f:
                for b in range(NB):
                    split_gate(f, b)
                    if b == NB - 1:
                        pool.wait_ge(mix0_done, f - 1)
                        split_out(f - 1)
                    split_branch(f, b)
            for f in range(FT):
                n = WBLOCKS + FT * NB + f
                if f == 1:
                    pool.wait_ge(mix0_done, FT - 1)
                    split_out(FT - 1)
                if f < WRING:
                    pool.wait_ge(gate_done, FT * NB - WRING + f + 1)
                else:
                    pool.wait_ge(mix_block_done, f - WRING + 1)
                split_block(n, n % WRING, n // WRING + 1)
            pool.wait_ge(mix_done, NT - 1)
            gather_tile(0, 0, True, first=True)
            for t in range(1, NT):
                gather_tile(0, t, True)
            with pool.Fori(1, HEADS - 1) as h:
                for t in range(NT):
                    gather_tile(h, t, True)
            for t in range(NT):
                gather_tile(HEADS - 1, t, False)

        @block.tensor
        def _(pe):
            xTs = (xT_hi, xT_lo)

            def triple(out, left, right, start, stop):
                pe.matmul(out, left[0], right[0], start=start, stop=False)
                pe.matmul(out, left[0], right[1], start=False, stop=False)
                return pe.matmul(out, left[1], right[0], start=False, stop=stop)

            def w_parts(slot, k, n=P):
                return [w[:, slot, k * n:(k + 1) * n] for w in (w_hi, w_lo)]

            def project(i, u, half=None):
                seg = UNITS[u]
                out = PROJ[u % 2]
                ks = range(KD) if half is None else range(half * KD // 2, (half + 1) * KD // 2)
                pe.wait_ge(unit_used, i * NU + u + 1)
                if seg in ("swap_q", "swap_k"):
                    raw = UNITS.index(DFQ if seg == "swap_q" else DFK)
                    pe.wait_ge(unit_used, i * NU + raw + 1 + 2)
                    mm = pe.matmul(out[:, :], swap_perm, df_raw[seg == "swap_k"], start=True, stop=True)
                    mm.then_inc(unit_done, 1)
                    return
                if seg in TURNED:
                    v, n = TURNED[seg]
                    pe.wait_ge(unit_used, i * NU + UNITS.index(v) + 1 + 2)
                    for t in range(n // P):
                        mm = pe.transpose(out[:, t * P:(t + 1) * P], swapped[:, t * P:(t + 1) * P], ident)
                    mm.then_inc(unit_done, 1)
                    return
                pe.wait_ge(w_split, i * SEGS + seg + 1)
                slot = seg % WRING
                n = M if seg in (MXK, MXV) else T
                if seg == MXK:
                    pe.wait_ge(memT_split, 1)
                for k in ks:
                    if isinstance(i, int) and i == 0 and u == 0:
                        pe.wait_ge(xT_split, k + 1)
                    mm = triple(out[:, 0:n], w_parts(slot, k), [x[:, k, :] for x in (memTs if n == M else xTs)],
                                start=(k == 0), stop=(k == KD - 1))
                if KD - 1 in ks:
                    mm.then_inc(unit_done, 1)

            def head_scores(out, a, kb, stop):
                r = slice(a * HD, (a + 1) * HD)
                pe.matmul(out[:, 0:WIDTH[kb]], sb_kT[r, kb * P:(kb + 1) * P], sb_qT[r, kb * P:T],
                          start=True, stop=False)
                return pe.matmul(out[:, 0:P], masks[:, 0, :], masks[:, 1, :], start=False, stop=stop)

            def z_block(i, a, kb):
                n = a * NT + kb
                if n == 0:
                    pe.wait_ge(unit_used, i * NU + 2 + 2)
                    pe.wait_ge(mx_out_used, i + 1)
                pe.wait_ge(abs_ready, i * 2 * NT + n + 1)
                head_scores(SOFT[n % 2], a, kb, True).then_inc(z_ready, 1)

            def stick_block(i, a, kb):
                n = a * NT + kb
                pe.wait_ge(softplus_ready, i * 2 + a + 1)
                pe.wait_ge(score_used, i * SCORES + n + 1)
                out = SCORE[n % 2]
                head_scores(out, a, kb, False)
                for block in range(kb, NT):
                    for j, softplus_part in enumerate((softplus_hi, softplus_lo)):
                        mm = pe.matmul(out[:, (block - kb) * P:WIDTH[kb]], neg_tri if block == kb else neg_ones,
                                       softplus_part[a][:, OFF[block]:OFF[block] + WIDTH[block]],
                                       start=False, stop=(block == NT - 1 and j == 1))
                mm.then_inc(score_ready, 1)

            def stick_sum(i):
                pe.wait_ge(score_used, i * SCORES + 2 * NT + 2)
                for a in range(2):
                    for kb in range(NT):
                        mm = pe.matmul(SUM[a * HD:(a + 1) * HD, kb * P:T], sb_v[:, kb * P + a * HD:kb * P + (a + 1) * HD],
                                       sb_aT[a][:, OFF[kb]:OFF[kb] + WIDTH[kb]], start=(kb == 0), stop=(kb == NT - 1))
                mm.then_inc(sb_out_done, 1)

            def df_scores(i, t, m):
                n = 2 * NT + 3 * t + m
                pe.wait_ge(score_used, i * SCORES + n + 1)
                r = slice(m * HD, (m + 1) * HD)
                w = (t + 1) * P
                pe.matmul(SCORE[n % 2][:, 0:w], df_raw[0][r, t * P:w], df_raw[1][r, 0:w], start=True, stop=False)
                pe.matmul(SCORE[n % 2][:, t * P:w], masks[:, 0, :], masks[:, 2, :],
                          start=False, stop=True).then_inc(score_ready, 1)

            def mx_scores(i, t):
                n = 2 * NT + 3 * t + 2
                pe.wait_ge(score_used, i * SCORES + n + 1)
                pe.matmul(SCORE[n % 2][:, 0:M], mx_qT[:, t * P:(t + 1) * P], mem_kT, start=True,
                          stop=True).then_inc(score_ready, 1)

            def turn(i, t):
                pe.wait_ge(probs_ready, i * 2 * NT + 2 * t + 1)
                for kb in range(t + 1):
                    mm = pe.transpose(TURN[0][:, kb * P:(kb + 1) * P], df_p[t % 2][0][:, kb * P:(kb + 1) * P], ident)
                mm.then_inc(turned, 1)
                pe.wait_ge(probs_ready, i * 2 * NT + 2 * t + 2)
                for kb in range(NM):
                    mm = pe.transpose(TURN[1][:, kb * P:(kb + 1) * P], mx_p[t % 2][:, kb * P:(kb + 1) * P], ident)
                mm.then_inc(turned, 1)

            def weigh_values(i, t):
                if t == 0:
                    pe.wait_ge(sb_out_copied, i + 1)
                pe.wait_ge(turned_copied, i * (2 * NT + 1) + 2 * t + 1)
                for kb in range(t + 1):
                    mm = pe.matmul(SUM[:, t * P:(t + 1) * P], df_pT[:, kb * P:(kb + 1) * P],
                                   df_v[:, kb * P:(kb + 1) * P], start=(kb == 0), stop=(kb == t))
                mm.then_inc(df_out_done, 1)
                pe.wait_ge(turned_copied, i * (2 * NT + 1) + 2 * t + 2)
                for kb in range(NM):
                    mm = pe.matmul(MXOUT[:, t * P:(t + 1) * P], mem_v[:, kb * P:(kb + 1) * P],
                                   mx_pT[:, kb * P:(kb + 1) * P], start=(kb == 0), stop=(kb == NM - 1))
                if t == NT - 1:
                    mm.then_inc(mx_out_done, 1)

            def gate_matmuls(f, b, half=None):
                ks = range(KD) if half is None else range(half * KD // 2, (half + 1) * KD // 2)
                if half != 1:
                    pe.wait_ge(w_split, f * NB + b + WBLOCKS + 1)
                    if isinstance(f, int) and f == 0:
                        pe.wait_ge(unit_used, ROUNDS * NU + 2)
                    else:
                        pe.wait_ge(gate_ready, f * NB + b + 1)
                for k in ks:
                    mm = triple(GATE[b][:, :], w_parts(b, k), [xT_hi[:, k, :], xT_lo[:, k, :]],
                                start=(k == 0), stop=(k == KD - 1))
                if KD - 1 in ks:
                    mm.then_inc(gate_done, 1)

            def branch_matmuls(f, b):
                pe.wait_ge(wb_split, f * NB + b + 1)
                pe.wait_ge(branch_used, f * NB + b + 1)
                for k in range(ROUNDS):
                    c = slice(k * P, (k + 1) * P)
                    mm = triple(BRANCH[b][:, :], [w_br_hi[b][:, c], w_br_lo[b][:, c]],
                                [o_hi[b][:, k], o_lo[b][:, k]], start=(k == 0), stop=(k == ROUNDS - 1))
                mm.then_inc(branch_done, 1)

            def first_scores(i):
                z_block(i, 0, 0)
                z_block(i, 0, 1)
                project(i, 4)
                z_block(i, 0, 2)
                z_block(i, 0, 3)
                project(i, 5, 0)

            def softmax_part(i, ahead):
                def fill(u, half=None):
                    if ahead:
                        project(i + 1, u, half)
                    elif u in EARLY_GATES:
                        gate_matmuls(0, EARLY_GATES[u], half)

                for t in range(NT):
                    df_scores(i, t, 0)
                    df_scores(i, t, 1)
                    if t >= 1:
                        fill(t - 1, 1)
                        turn(i, t - 1)
                    if t == 0:
                        fill(t, 0)
                    mx_scores(i, t)
                    if 0 < t < NT - 1 or t == NT - 1 and ahead:
                        fill(t, 0)
                    if t >= 1:
                        weigh_values(i, t - 1)
                turn(i, NT - 1)
                fill(NT - 1, 1 if ahead else 0)
                weigh_values(i, NT - 1)
                if ahead:
                    first_scores(i + 1)
                else:
                    fill(NT - 1, 1)
                    pe.wait_ge(o_split, NB)
                    branch_matmuls(0, 0)
                pe.wait_ge(normed_ready, i + 1)
                for t in range(NT):
                    mm = pe.transpose(TURN[0][:, t * P:(t + 1) * P], df_on[:, t * P:(t + 1) * P], ident)
                mm.then_inc(turned, 1)

            def stick_part(i):
                project(i, 5, 1)
                z_block(i, 1, 0)
                z_block(i, 1, 1)
                project(i, 6)
                z_block(i, 1, 2)
                project(i, 7)
                z_block(i, 1, 3)
                project(i, 8)
                stick_block(i, 0, 0)
                stick_block(i, 0, 1)
                project(i, 9)
                project(i, 10)
                stick_block(i, 0, 2)
                stick_block(i, 0, 3)
                project(i, 11)
                stick_block(i, 1, 0)
                project(i, 12)
                stick_block(i, 1, 1)
                stick_block(i, 1, 2)
                project(i, 13)
                stick_block(i, 1, 3)
                stick_sum(i)

            for u in range(4):
                project(0, u)
            pe.wait_ge(const_loaded, 16 * CONST_LOADS)
            pe.wait_ge(sums_ready, 1)
            first_scores(0)
            with pe.Fori(0, ROUNDS - 1) as i:
                stick_part(i)
                softmax_part(i, True)
            stick_part(ROUNDS - 1)
            softmax_part(ROUNDS - 1, False)

            pe.wait_ge(o_last_split, 2)
            def mix_first(f, start, stop):
                pe.wait_ge(wo_split, f + 1)
                pe.wait_ge(merged_ready, f + 1)
                for c in range(2):
                    d = slice(c * 512, (c + 1) * 512)
                    mm = triple(MIX[0][c][:, :], [m[:, :] for m in merged0], [wo_hi[:, d], wo_lo[:, d]],
                                start=start, stop=stop)
                mm.then_inc(mix0_done, 1)

            def merge(f, mixed):
                for b in range(NB):
                    if mixed:
                        gate_matmuls(f, b)
                    if mixed or b > 0:
                        branch_matmuls(f, b)
                    if mixed and b == 0:
                        mix_first(f - 1, start=(mixed == "first"), stop=False)

            merge(0, None)
            merge(1, "first")
            with pe.Fori(2, FT) as f:
                merge(f, "later")
            def turn_x1(t):
                pe.wait_ge(x1_ready, t + 1)
                for k in range(KD):
                    mm = pe.transpose(MIX[t][k // 4][:, (k % 4) * P:(k % 4 + 1) * P], x1[:, t, k * P:(k + 1) * P], ident)
                    if k % 4 == 3:
                        mm.then_inc(x1_turned, 1)

            pe.sem_inc(row_used, RING)
            for f in range(FT):
                n = WBLOCKS + FT * NB + f
                pe.wait_ge(w_split, n + 1)
                for t in range(1, NT):
                    if f == 0:
                        pe.wait_ge(gate_ready, FT * NB + (2 if t == 1 else NB))
                        pe.wait_ge(branch_used, FT * NB + 1)
                        if t == NT - 1:
                            mix_first(FT - 1, start=False, stop=True)
                            pe.wait_ge(branch_used, FT * NB + NB)
                    for c in range(2):
                        mm = triple(MIX[t][c][:, :], [m[:, f, t * P:(t + 1) * P] for m in (mergedT_hi, mergedT_lo)],
                                    w_parts(n % WRING, c, 512), start=(f == 0), stop=(f == FT - 1))
                    if f == FT - 1:
                        mm.then_inc(mix_done, 1)
                if f < FT - 1:
                    mm.then_inc(mix_block_done, 1)
                if f == 2:
                    turn_x1(0)
                if f == 3:
                    pe.wait_ge(wq_split, 2)
                    pe.wait_ge(x1T_split, 2)
                    for u in range(2):
                        for k in range(KD):
                            mm = triple(QUERY0[:, u * P:(u + 1) * P], [w[:, u, k, :] for w in wqs],
                                        [xT_hi[:, k, 0:P], xT_lo[:, k, 0:P]], start=(k == 0), stop=(k == KD - 1))
                    mm.then_inc(query0_done, 1)
                if f == 4:
                    pe.wait_ge(keys_loaded, 16)
                    pe.wait_ge(query0_copied, 1)
                    for u in range(2):
                        mm = pe.matmul(KEYSCORE0[:, u * NK:(u + 1) * NK], peer_qT[:, u, 0:P], keysT[:, u, :],
                                       start=True, stop=True)
                    mm.then_inc(keyscore0_done, 1)
            for t in range(1, NT):
                turn_x1(t)

            def query_matmuls(h, first, n):
                at = tokens_of(h)
                for j in range(first, first + n):
                    u, k = j // KD, j % KD
                    if k == 0:
                        pe.wait_ge(wq_split, h * 2 + u + 1)
                    mm = triple(QUERY[u][:, at:T], [w[:, u, k, :] for w in wqs], [xT_hi[:, k, at:T], xT_lo[:, k, at:T]],
                                start=(k == 0), stop=(k == KD - 1))
                    if k == KD - 1:
                        mm.then_inc(query_done, 1)

            def key_scores(h, half, first=False):
                if half == 0:
                    pe.wait_ge(keys_loaded, h * 16 + 16)
                    pe.wait_ge(query_copied, h * 2 + 2)
                    if first:
                        pe.wait_ge(keyscore0_copied, 1)
                    else:
                        pe.wait_ge(keyscore_copied, h * 2)
                for t in (2 * half, 2 * half + 1):
                    if first and t == 0:
                        continue
                    for u in range(2):
                        c = (t % 2) * 2 * NK + u * NK
                        mm = pe.matmul(KEYSCORE[half][:, c:c + NK], peer_qT[:, u, t * P:(t + 1) * P], keysT[:, u, :],
                                       start=True, stop=True)
                mm.then_inc(keyscore_done, 1)

            def sum_rows(h, t, e):
                pe.wait_ge(diag_ready, (h * NT + t) * TOPK + e + 1)
                if e == 0:
                    pe.wait_ge(vsum_used, h * NT + t + 1)
                for n in range(2):
                    mm = pe.matmul(VSUM[t % 2][n][:, :], diag[:, e % RING, :],
                                   rows[:, e % RING, D + n * 512:D + (n + 1) * 512],
                                   start=(e == 0), stop=(e == TOPK - 1))
                mm.then_inc(row_used, 1)

            def experts(h, ahead, first=False):
                for t in range(NT):
                    for e in range(TOPK):
                        sum_rows(h, t, e)
                        if ahead and t == first and 2 <= e < 10:
                            query_matmuls(h + 1, 2 * (e - 2), 2)
                        if ahead and t == first and e in (12, 13):
                            key_scores(h + 1, e - 12)

            pe.wait_ge(x1T_split, 2 * NT)
            query_matmuls(0, 0, 2 * KD)
            key_scores(0, 0, first=True)
            key_scores(0, 1, first=True)
            experts(0, True, first=True)
            with pe.Fori(1, HEADS - 1) as h:
                experts(h, True)
            experts(HEADS - 1, False)

        @block.scalar
        def _(act):
            steps = Steps()
            act.wait_ge(const_loaded, 16 * CONST_LOADS)
            act.wait_ge(angle_ready, 1)
            act.activation(rope_sin, rope_r, ACT.Sin).then_inc(sines_ready, 1)
            act.wait_ge(angle_ready, 2)
            act.activation(rope_cos, rope_k, ACT.Sin).then_inc(sines_ready, 1)
            act.wait_ge(lam_ready, 1)
            act.activation(lam_e[:, :], lam_s[:, :], ACT.Exp).then_inc(lam_exp, 1)
            act.sem_inc(score_used, 2)

            def positive_part(i, a, kb):
                n = a * NT + kb
                act.wait_ge(z_ready, i * 2 * NT + n + 1)
                act.activation(softplus[a][:, OFF[kb]:OFF[kb] + WIDTH[kb]], SOFT[n % 2][:, 0:WIDTH[kb]],
                               ACT.Relu).then_inc(relu_ready, 1)

            def softlog(i, a):
                act.wait_ge(abs_ready, i * 2 * NT + (a + 1) * NT + 2)
                act.activation(soft_log[a], soft_log[a], ACT.Exp).then_inc(act_step, steps.add())
                act.wait_ge(act_step, steps.value())
                act.activation(soft_log[a], soft_log[a], ACT.Ln, bias=one).then_inc(softlog_ready, 1)

            def stick_weights(i, a, kb):
                n = a * NT + kb
                act.wait_ge(score_ready, i * SCORES + n + 1)
                act.activation(sb_aT[a][:, OFF[kb]:OFF[kb] + WIDTH[kb]], SCORE[n % 2][:, 0:WIDTH[kb]],
                               ACT.Exp).then_inc(score_used, 1)

            def softmax_exp(i, t, j):
                n = 2 * NT + 3 * t + j
                w = (t + 1) * P if j < 2 else M
                dst = df_p[t % 2][j] if j < 2 else mx_p[t % 2]
                act.wait_ge(negmax_ready, i * 3 * NT + 3 * t + j + 1)
                c = 3 * t + j
                act.activation(dst[:, 0:w], SCORE[n % 2][:, 0:w], ACT.Exp, bias=neg_max[:, c:c + 1],
                               accum_out=expsum[:, c:c + 1]).then_inc(score_used, 1)

            def round_(i, ahead):
                for a in range(2):
                    for kb in range(2 * (1 - a), NT):
                        positive_part(i, a, kb)
                    softlog(i, a)
                for a in range(2):
                    for kb in range(NT):
                        stick_weights(i, a, kb)
                for t in range(NT):
                    for j in range(3):
                        softmax_exp(i, t, j)
                if ahead:
                    positive_part(i + 1, 0, 0)
                    positive_part(i + 1, 0, 1)
                act.wait_ge(df_out_done, i * NT + NT)
                for t in range(NT):
                    ins = act.activation(df_sq[:, t * P:(t + 1) * P], SUM[:, t * P:(t + 1) * P], ACT.Square,
                                         accum_out=df_ss[:, t:t + 1])
                ins.then_inc(act_step, steps.add())
                act.wait_ge(act_step, steps.value())
                act.activation(df_ln[:, :], df_ss[:, :], ACT.Ln, bias=eps, scale=1.0 / P).then_inc(act_step, steps.add())
                act.wait_ge(act_step, steps.value())
                act.activation(df_rms[:, :], df_ln[:, :], ACT.Exp, scale=-0.5).then_inc(rms_ready, 1)

            positive_part(0, 0, 0)
            positive_part(0, 0, 1)
            with act.Fori(0, ROUNDS - 1) as i:
                steps.enter(i, 2 + 2)
                round_(i, True)
                steps.leave(ROUNDS - 1)
            round_(ROUNDS - 1, False)

            act.sem_inc(gate_ready, NB)
            act.wait_ge(turned_copied, ROUNDS * (2 * NT + 1))
            with act.Fori(0, FT) as f:
                for b in range(NB):
                    act.wait_ge(gate_done, f * NB + b + 1)
                    act.wait_ge(merged_ready, f)
                    act.activation(gate[:, b, :], GATE[b][:, :], ACT.Sigmoid,
                                   bias=b_gate[:, b, bass.ds(f, 1)]).then_inc(gate_ready, 1)

            def rough_rstd(n):
                act.wait_ge(var_ready, n + 1)
                t = n % NT
                act.activation(ln_l[:, t:t + 1], ln_v[:, t:t + 1], ACT.Ln).then_inc(act_step, steps.add())
                act.wait_ge(act_step, steps.value())
                act.activation(ln_r[:, t:t + 1], ln_l[:, t:t + 1], ACT.Exp, scale=-0.5).then_inc(rstd_ready, 1)

            def copy_x1T(t):
                for half in range(2):
                    act.wait_ge(x1_turned, 2 * t + half + 1)
                    act.activation(xT_hi[:, 4 * half:4 * half + 4, t * P:(t + 1) * P],
                                   MIX[t][half][:, :].rearrange("p (k c) -> p k c", k=4), ACT.Copy
                                   ).then_inc(x1T_rounded, 1)

            def copy_queries(h, u):
                act.wait_ge(query_done, h * 2 + u + 1)
                at = tokens_of(h)
                act.activation(peer_qT[:, u, at:T], QUERY[u][:, at:T], ACT.Copy).then_inc(query_copied, 1)

            def copy_keyscores(h, half):
                act.wait_ge(keyscore_done, h * 2 + half + 1)
                tiles = KEYSCORE[half][:, :].rearrange("p (t u n) -> p t u n", t=2, u=2)
                at = tokens_of(h) // P if half == 0 else 0
                act.activation(score[:, 2 * half + at:2 * half + 2], tiles[:, at:2], ACT.Copy).then_inc(keyscore_copied, 1)

            def best_exp(h, t):
                act.wait_ge(negbest_ready, h * NT + t + 1)
                act.activation(best_e[:, :], best_v[:, :], ACT.Exp, bias=neg_best[:, :],
                               accum_out=best_z[:, :]).then_inc(bestexp_ready, 1)

            def gelu_group(h, t, g):
                n = (h * NT + t) * (TOPK // GROUP) + g
                act.wait_ge(hid_ready, n + 1)
                c = slice(g * GROUP, (g + 1) * GROUP)
                act.activation(gel[:, t, c], hid[:, t, c], ACT.Gelu).then_inc(gelu_ready, 1)
                act.wait_ge(actw_ready, n + 1)
                for e in range(g * GROUP, (g + 1) * GROUP):
                    if e % GROUP == 0:
                        act.wait_ge(row_used, n * GROUP + GROUP)
                    act.activation(diag[:, e % RING, :], ident, ACT.Copy,
                                   scale=act_w[:, t, e:e + 1]).then_inc(diag_ready, 1)

            def experts(h, ahead, first=False):
                for t in range(NT):
                    for g in range(TOPK // GROUP):
                        gelu_group(h, t, g)
                        if ahead and t == first and g in (3, 5):
                            copy_queries(h + 1, (g - 3) // 2)
                        if first and t == 0 and g == 2:
                            best_exp(0, 1)
                        if not ahead and t >= 1 and g == 1:
                            rough_rstd(NT + t - 1)
                    if ahead or t < 2:
                        best_exp(h, t + 2) if t < 2 else best_exp(h + 1, t - 2)
                    if ahead and t == 1:
                        act.wait_ge(chosen_ready, (h + 1) * NT)
                        copy_keyscores(h + 1, 0)
                        copy_keyscores(h + 1, 1)

            rough_rstd(0)
            copy_x1T(0)
            act.wait_ge(wq_loaded, 16)
            for u in range(2):
                act.activation(wqs[0][:, u], w_q[:, u], ACT.Copy).then_inc(wq_rounded, 1)
            act.wait_ge(query0_done, 1)
            act.activation(peer_qT[:, :, 0:P], QUERY0.rearrange("p (u t) -> p u t", u=2), ACT.Copy).then_inc(query0_copied, 1)
            act.wait_ge(keyscore0_done, 1)
            act.activation(score[:, 0], KEYSCORE0.rearrange("p (u n) -> p u n", u=2), ACT.Copy).then_inc(keyscore0_copied, 1)
            best_exp(0, 0)
            rough_rstd(1)
            rough_rstd(2)
            rough_rstd(3)
            for t in range(1, NT):
                copy_x1T(t)

            copy_queries(0, 0)
            copy_queries(0, 1)
            copy_keyscores(0, 0)
            copy_keyscores(0, 1)
            experts(0, True, first=True)
            with act.Fori(1, HEADS - 1) as h:
                experts(h, True)
            experts(HEADS - 1, False)
            rough_rstd(2 * NT - 1)

        @block.vector
        def _(dve):
            steps = Steps()

            def then(ins):
                ins.then_inc(dve_step, steps.add())
                dve.wait_ge(dve_step, steps.value())

            def unit(i, u):
                seg, src = UNITS[u], PROJ[u % 2]
                dve.wait_ge(unit_done, i * NU + u + 1)
                if seg in (SBQ, DFQ):
                    dst = sb_qT if seg == SBQ else df_raw[0]
                    dve.tensor_scalar(dst, src[:, :], QSCALE, None, ALU.mult).then_inc(unit_used, 1)
                elif seg == MXQ:
                    dve.tensor_scalar(mx_qT, src[:, :], MXSCALE, None, ALU.mult).then_inc(unit_used, 1)
                elif seg in ("swap_q", "swap_k"):
                    raw = df_raw[seg == "swap_k"]
                    dve.tensor_tensor(swapped, src[:, :], rope_sin, ALU.mult).then_inc(unit_used, 1)
                    then(dve.tensor_tensor(raw, raw, rope_cos, ALU.mult))
                    dve.wait_ge(unit_used, i * NU + u + 1 + 2)
                    then(dve.tensor_tensor(raw, raw, swapped, ALU.add))
                elif seg in (MXK, MXV):
                    dve.tensor_copy(mem_kT if seg == MXK else swapped[:, 0:M], src[:, 0:M]).then_inc(unit_used, 1)
                elif seg == "turn_mx":
                    dve.tensor_copy(mem_v, src[:, 0:M]).then_inc(unit_used, 1)
                else:
                    dst = {SBK: sb_kT, SBV: swapped, DFK: df_raw[1], DFV: swapped, "turn_sb": sb_v, "turn_df": df_v}[seg]
                    dve.tensor_copy(dst, src[:, :]).then_inc(unit_used, 1)

            dve.sem_inc(unit_used, 2)
            dve.sem_inc(abs_ready, 2)
            dve.sem_inc(mx_out_used, 1)
            for k in range(KD):
                dve.wait_ge(xT_loaded[k], 16)
                dve.tensor_copy(xT_hi[:, k, :], xT_raw[:, k, :]).then_inc(xT_rounded, 1)
                dve.wait_ge(xT_rounded, k + 1)
                dve.tensor_tensor(xT_lo[:, k, :], xT_raw[:, k, :], xT_hi[:, k, :].bitcast(F32),
                                  ALU.subtract).then_inc(xT_split, 1)
            dve.wait_ge(const_loaded, 16 * CONST_LOADS)
            dve.tensor_copy(neg_sums[:, :], const[:, C_TRI:C_TRI + 2 * P]).then_inc(sums_ready, 1)
            pos_f, angle = df_raw[0], df_raw[1]
            then(dve.tensor_copy(pos_f, pos_i))
            then(dve.tensor_scalar(angle, pos_f, inv_freq, None, ALU.mult))
            for j in range(2):
                k, r = (rope_cos, rope_r) if j == 0 else (rope_cos, rope_k)
                then(dve.tensor_scalar(k, angle, 1.0 / TWO_PI, 0.25 * j, ALU.mult, ALU.add))
                then(dve.tensor_scalar(k, k, ROUND_MAGIC, None, ALU.add))
                then(dve.tensor_scalar(k, k, -ROUND_MAGIC, None, ALU.add))
                then(dve.scalar_tensor_tensor(r, k, -PI_A, angle, ALU.mult, ALU.add))
                then(dve.scalar_tensor_tensor(r, k, -PI_B, r, ALU.mult, ALU.add))
                then(dve.scalar_tensor_tensor(r, k, -PI_C, r, ALU.mult, ALU.add))
                if j == 1:
                    then(dve.tensor_scalar(r, r, TWO_PI / 4, None, ALU.add))
                dve.tensor_scalar(r, r, PI_TOP, -PI_TOP, ALU.min, ALU.max).then_inc(angle_ready, 1)
                unit(0, j)
            dve.wait_ge(memT_loaded, 16)
            dve.tensor_copy(memTs[0], memT_raw).then_inc(memT_rounded, 1)
            dve.wait_ge(memT_rounded, 1)
            dve.tensor_tensor(memTs[1], memT_raw, memTs[0].bitcast(F32), ALU.subtract).then_inc(memT_split, 1)
            dve.wait_ge(memT_split, 1)
            then(dve.tensor_tensor(lam_pr[:, :, :], lam_in[:, 0:4:2, :], lam_in[:, 1:4:2, :], ALU.mult))
            dve.tensor_reduce(lam_s[:, :], lam_pr[:, :, :], AX_X, ALU.add).then_inc(lam_ready, 1)
            then(dve.tensor_scalar(df_g8[:, :], df_g[:, :], 1.0 - LAMBDA_INIT, None, ALU.mult))
            dve.wait_ge(sines_ready, 2)
            then(dve.tensor_scalar(rope_sin, rope_sin, rope_sign, None, ALU.mult))
            dve.wait_ge(lam_exp, 1)
            then(dve.scalar_tensor_tensor(neg_lam[:, :], lam_e[:, 1:2], -LAMBDA_INIT, lam_e[:, 0:1],
                                          ALU.add, ALU.subtract))

            def take_abs(i, a, kb):
                n = a * NT + kb
                w = WIDTH[kb]
                dve.wait_ge(relu_ready, i * 2 * NT + n + 1)
                positive = softplus[a][:, OFF[kb]:OFF[kb] + w]
                dve.scalar_tensor_tensor(soft_log[a][:, OFF[kb]:OFF[kb] + w], positive, -2.0, SOFT[n % 2][:, 0:w],
                                         ALU.mult, ALU.add).then_inc(abs_ready, 1)

            def first_scores(i):
                unit(i, 4)
                take_abs(i, 0, 2)
                take_abs(i, 0, 3)

            def take_softplus(i, a):
                dve.wait_ge(softlog_ready, i * 2 + a + 1)
                then(dve.tensor_tensor(softplus[a], softplus[a], soft_log[a], ALU.add))
                then(dve.tensor_copy(softplus_hi[a][:, :], softplus[a]))
                dve.tensor_tensor(softplus_lo[a][:, :], softplus[a], softplus_hi[a][:, :].bitcast(F32),
                                  ALU.subtract).then_inc(softplus_ready, 1)

            def neg_maxima(i, t, maps):
                for j in maps:
                    n = 2 * NT + 3 * t + j
                    w = (t + 1) * P if j < 2 else M
                    dve.wait_ge(score_ready, i * SCORES + n + 1)
                    dve.tensor_reduce(neg_max[:, 3 * t + j:3 * t + j + 1], SCORE[n % 2][:, 0:w], AX_X, ALU.max,
                                      negate=True).then_inc(negmax_ready, 1)

            def probabilities(i, t):
                c = 3 * t
                dve.wait_ge(score_used, i * SCORES + 2 * NT + c + 3 + 2)
                w = (t + 1) * P
                p0, p1 = df_p[t % 2][0][:, 0:w], df_p[t % 2][1][:, 0:w]
                then(dve.reciprocal(exprec[:, c:c + 3], expsum[:, c:c + 3]))
                then(dve.tensor_scalar(p1, p1, exprec[:, c + 1:c + 2], neg_lam[:, :], ALU.mult, ALU.mult))
                dve.scalar_tensor_tensor(p0, p0, exprec[:, c:c + 1], p1, ALU.mult, ALU.add).then_inc(probs_ready, 1)
                dve.tensor_scalar(mx_p[t % 2], mx_p[t % 2], exprec[:, c + 2:c + 3], None,
                                  ALU.mult).then_inc(probs_ready, 1)

            def copy_turned(i, t):
                dve.wait_ge(turned, i * (2 * NT + 1) + 2 * t + 1)
                dve.tensor_copy(df_pT[:, 0:(t + 1) * P], TURN[0][:, 0:(t + 1) * P]).then_inc(turned_copied, 1)
                dve.wait_ge(turned, i * (2 * NT + 1) + 2 * t + 2)
                dve.tensor_copy(mx_pT, TURN[1][:, 0:M]).then_inc(turned_copied, 1)

            def stick_part(i):
                unit(i, 5)
                take_abs(i, 1, 0)
                take_abs(i, 1, 1)
                unit(i, 6)
                take_abs(i, 1, 2)
                take_softplus(i, 0)
                unit(i, 7)
                take_abs(i, 1, 3)
                unit(i, 8)
                take_softplus(i, 1)
                for u in range(9, NU):
                    unit(i, u)

            def softmax_part(i, ahead):
                def fill(u):
                    if ahead:
                        unit(i + 1, u)

                dve.wait_ge(sb_out_done, i + 1)
                dve.tensor_copy(o_branch[:, 0, at_round(i), :], SUM[:, :].rearrange("p (o t) -> p o t", o=1)
                                ).then_inc(sb_out_copied, 1)
                for t in range(NT):
                    neg_maxima(i, t, (0, 1))
                    if t >= 1:
                        fill(t - 1)
                        copy_turned(i, t - 1)
                    neg_maxima(i, t, (2,))
                    probabilities(i, t)
                copy_turned(i, NT - 1)
                dve.wait_ge(mx_out_done, i + 1)
                dve.tensor_copy(o_branch[:, 2, at_round(i), :], MXOUT[:, :].rearrange("p (o t) -> p o t", o=1)
                                ).then_inc(mx_out_used, 1)
                if not ahead:
                    dve.wait_ge(mx_out_used, ROUNDS + 1)
                    split_last(0, 2)
                fill(3)
                if ahead:
                    take_abs(i + 1, 0, 0)
                    take_abs(i + 1, 0, 1)
                dve.wait_ge(rms_ready, i + 1)
                dve.tensor_tensor(df_on.rearrange("p (t d) -> p t d", t=NT),
                                  SUM[:, :].rearrange("p (t d) -> p t d", t=NT),
                                  df_rms[:, :].unsqueeze(2).to_broadcast([P, NT, P]), ALU.mult).then_inc(normed_ready, 1)
                if ahead:
                    first_scores(i + 1)
                dve.wait_ge(turned, (i + 1) * (2 * NT + 1))
                dve.tensor_scalar(o_branch[:, 1, at_round(i), :], TURN[0][:, :].rearrange("p (o t) -> p o t", o=1),
                                  df_g8[:, :], None, ALU.mult).then_inc(turned_copied, 1)
                if not ahead:
                    dve.wait_ge(turned_copied, ROUNDS * (2 * NT + 1))
                    split_last(1, 1)

            def split_last(n, b):
                k = ROUNDS - 1
                dve.tensor_copy(o_hi[b][:, k], o_branch[:, b, k]).then_inc(o_last_rounded, 1)
                dve.wait_ge(o_last_rounded, n + 1)
                dve.tensor_tensor(o_lo[b][:, k], o_branch[:, b, k], o_hi[b][:, k].bitcast(F32),
                                  ALU.subtract).then_inc(o_last_split, 1)

            def at_round(i):
                return slice(i, i + 1) if isinstance(i, int) else bass.ds(i, 1)

            for u in range(2, 4):
                unit(0, u)
            take_abs(0, 0, 0)
            take_abs(0, 0, 1)
            first_scores(0)
            with dve.Fori(0, ROUNDS - 1) as i:
                steps.enter(i, 2 * 2 + 2 * NT + 4)
                stick_part(i)
                softmax_part(i, True)
                steps.leave(ROUNDS - 1)
            dve.sem_inc(branch_used, NB)
            stick_part(ROUNDS - 1)
            softmax_part(ROUNDS - 1, False)

            with dve.Fori(0, FT) as f:
                steps.enter(f, 3)
                for b in range(NB):
                    dve.wait_ge(gate_ready, f * NB + b + 1 + NB)
                    dve.wait_ge(branch_done, f * NB + b + 1)
                    dve.tensor_tensor(gate[:, b, :], gate[:, b, :], BRANCH[b][:, :], ALU.mult).then_inc(branch_used, 1)
                    dve.wait_ge(branch_used, f * NB + b + 1 + NB)
                    if b >= 1:
                        then(dve.tensor_tensor(gate[:, 0, :], gate[:, 0, :], gate[:, b, :], ALU.add))
                dve.wait_ge(mix0_done, f)
                for dst, src in ((merged0[0][:, :].rearrange("p (o t) -> p o t", o=1), gate[:, 0:1, 0:P]),
                                 (mergedT_hi[:, bass.ds(f, 1), P:T], gate[:, 0:1, P:T])):
                    ins = dve.tensor_copy(dst, src)
                then(ins)
                dve.tensor_tensor(merged0[1][:, :], gate[:, 0, 0:P], merged0[0][:, :].bitcast(F32), ALU.subtract)
                dve.tensor_tensor(mergedT_lo[:, bass.ds(f, 1), P:T], gate[:, 0:1, P:T],
                                  mergedT_hi[:, bass.ds(f, 1), P:T].bitcast(F32), ALU.subtract).then_inc(merged_ready, 1)
                dve.wait_ge(merged_ready, f + 1)
                steps.leave(FT)

            def variance(src, t, gb):
                for n in range(2):
                    ins = dve.bn_stats(stats[:, t, n, :], src[:, n * 512:(n + 1) * 512])
                then(ins)
                then(dve.bn_aggr(mean_var[:, t, :], stats[:, t, :, :].rearrange("p n c -> p (n c)")))
                dve.tensor_scalar(ln_v[:, t:t + 1], mean_var[:, t, 1:2], LN_EPS, None, ALU.add).then_inc(var_ready, 1)
                then(dve.scalar_tensor_tensor(src, src, mean_var[:, t, 0:1], gb[:, 0, :], ALU.subtract, ALU.mult))

            def normalise(src, t, n, gb):
                dve.wait_ge(rstd_ready, n + 1)
                r, v, u = ln_r[:, t:t + 1], ln_v[:, t:t + 1], ln_u[:, t:t + 1]
                then(dve.tensor_scalar(ln_t[:, t:t + 1], r, r, v, ALU.mult, ALU.mult))
                then(dve.tensor_scalar(ln_t[:, t:t + 1], ln_t[:, t:t + 1], -0.5, 1.5, ALU.mult, ALU.add))
                then(dve.tensor_tensor(u, ln_t[:, t:t + 1], r, ALU.mult))
                return dve.scalar_tensor_tensor(src, src, u, gb[:, 1, :], ALU.mult, ALU.add)

            def add_mix(t):
                dve.wait_ge(xnat_loaded, 16 if t < NT - 2 else 32)
                if t == 0:
                    dve.wait_ge(mix0_done, FT)
                else:
                    dve.wait_ge(mix_done, t)
                for n in range(2):
                    c = slice(n * 512, (n + 1) * 512)
                    ins = dve.scalar_tensor_tensor(x1[:, t, c], x_nat[:, t, c], ALPHA, MIX[t][n][:, :],
                                                   ALU.mult, ALU.add)
                ins.then_inc(mix_used, 1)
                dve.wait_ge(mix_used, t + 1)
                variance(x1[:, t, :], t, ln1_gb)

            def norm_x1(t):
                normalise(x1[:, t, :], t, t, ln1_gb).then_inc(x1_ready, 1)

            def low_x1T(t):
                for half in range(2):
                    dve.wait_ge(x1T_rounded, 2 * t + half + 1)
                    c = (slice(None), slice(4 * half, 4 * half + 4), slice(t * P, (t + 1) * P))
                    dve.tensor_tensor(xT_lo[c], MIX[t][half][:, :].rearrange("p (k c) -> p k c", k=4),
                                      xT_hi[c].bitcast(F32), ALU.subtract).then_inc(x1T_split, 1)

            dve.wait_ge(ln1_loaded, 32)
            def choose(h, t, first=False):
                dve.sem_clear(choose_step)
                chain = Steps()

                def chosen_then(ins):
                    ins.then_inc(choose_step, chain.add())
                    dve.wait_ge(choose_step, chain.value())

                if first:
                    dve.wait_ge(keyscore0_copied, 1)
                else:
                    dve.wait_ge(keyscore_copied, h * 2 + t // 2 + 1)
                dve.sem_inc(choices_begun, 1)
                top, rest = slice(0, 8), slice(8, TOPK)
                s = score[:, t]
                for u in range(2):
                    ins = dve.max(top_v[:, u, top], s[:, u, :])
                chosen_then(ins)
                for u in range(2):
                    dve.max_index(top_i[:, u, top], top_v[:, u, top], s[:, u, :])
                    ins = dve.match_replace(score_cut[:, u, :], top_v[:, u, top], s[:, u, :], NEG_BIG)
                chosen_then(ins)
                for u in range(2):
                    ins = dve.max(top_v[:, u, rest], score_cut[:, u, :])
                chosen_then(ins)
                for u in range(2):
                    ins = dve.max_index(top_i[:, u, rest], top_v[:, u, rest], score_cut[:, u, :])
                ins = dve.tensor_tensor(cand.rearrange("p (i j) -> p i j", i=TOPK),
                                        top_v[:, 0, :].unsqueeze(2).to_broadcast([P, TOPK, TOPK]),
                                        top_v[:, 1, :].unsqueeze(1).to_broadcast([P, TOPK, TOPK]), ALU.add)
                chosen_then(ins)
                dve.tensor_copy(top_f[:, :, :], top_i[:, :, :])
                chosen_then(dve.max(best_v[:, top], cand))
                chosen_then(dve.tensor_scalar(neg_best[:, :], best_v[:, 0:1], -1.0, None, ALU.mult))
                dve.max_index(best_i[:, top], best_v[:, top], cand)
                chosen_then(dve.match_replace(cand_cut, best_v[:, top], cand, NEG_BIG))
                chosen_then(dve.max(best_v[:, rest], cand_cut))
                dve.sem_inc(negbest_ready, 1)
                chosen_then(dve.max_index(best_i[:, rest], best_v[:, rest], cand_cut))
                dve.tensor_scalar(best_ij[:, 0, :], best_i[:, :], 4, None, ALU.logical_shift_right)
                chosen_then(dve.tensor_scalar(best_ij[:, 1, :], best_i[:, :], TOPK - 1, None, ALU.bitwise_and))
                chosen_then(dve.tensor_copy(best_f[:, :, :], best_ij[:, :, :]))
                for u in range(2):
                    ins = dve.tensor_tensor(onehot[:, u], iota16.unsqueeze(1).to_broadcast([P, TOPK, TOPK]),
                                            best_f[:, u, :].unsqueeze(2).to_broadcast([P, TOPK, TOPK]), ALU.is_equal)
                chosen_then(ins)
                for u in range(2):
                    ins = dve.tensor_tensor(onehot[:, u], onehot[:, u],
                                            top_f[:, u, :].unsqueeze(1).to_broadcast([P, TOPK, TOPK]), ALU.mult)
                chosen_then(ins)
                chosen_then(dve.tensor_reduce(chosen[:, :, :], onehot, AX_X, ALU.add))
                dve.wait_ge(bestexp_ready, h * NT + t + 1)
                chosen_then(dve.reciprocal(best_r[:, :], best_z[:, :]))
                chosen_then(dve.tensor_scalar(weight[:, t, :], best_e[:, :], best_r[:, :], None, ALU.mult))
                dve.scalar_tensor_tensor(ids[:, t, :], chosen[:, 0, :], float(NK), chosen[:, 1, :],
                                         ALU.mult, ALU.add).then_inc(chosen_ready, 1)

            def weigh(h, t, g):
                n = (h * NT + t) * (TOPK // GROUP) + g
                dve.wait_ge(gelu_ready, n + 1)
                c = slice(g * GROUP, (g + 1) * GROUP)
                dve.tensor_tensor(act_w[:, t, c], gel[:, t, c], weight[:, t, c], ALU.mult).then_inc(actw_ready, 1)

            def add_sums(h, t):
                dve.wait_ge(row_used, (h * NT + t + 1) * TOPK + RING)
                if isinstance(h, int) and h == 0:
                    dve.wait_ge(acc_ready, t + 1)
                for n in range(2):
                    c = slice(n * 512, (n + 1) * 512)
                    ins = dve.tensor_tensor(acc[:, t, c], acc[:, t, c], VSUM[t % 2][n][:, :], ALU.add)
                ins.then_inc(vsum_used, 1)

            def out_variance(t):
                dve.wait_ge(vsum_used, (HEADS - 1) * NT + t + 1 + 2)
                variance(acc[:, t, :], t, ln2_gb)

            def out_normalise(t):
                normalise(acc[:, t, :], t, NT + t, ln2_gb).then_inc(out_ready, 1)

            def experts(h, ahead, first=False):
                for t in range(NT):
                    for g in range(TOPK // GROUP):
                        for e in range(g * GROUP, (g + 1) * GROUP):
                            dve.wait_ge(row_loaded[e % RING], ((h * NT + t) * (TOPK // RING) + e // RING) * 16 + 16)
                            ins = dve.tensor_tensor_reduce(rows[:, e % RING, 0:D], rows[:, e % RING, 0:D], x1[:, t, :],
                                                           1.0, 0.0, ALU.mult, ALU.add, hid[:, t, e:e + 1])
                        ins.then_inc(hid_ready, 1)
                        if g >= 1:
                            weigh(h, t, g - 1)
                        if first and t == 0 and g == 3:
                            choose(0, 1)
                        if t >= 1 and g == 1:
                            add_sums(h, t - 1)
                        if not ahead and t >= 1:
                            if g == 1:
                                out_variance(t - 1)
                            if g == 3:
                                out_normalise(t - 1)
                    weigh(h, t, TOPK // GROUP - 1)
                    if t < 2:
                        choose(h, t + 2)
                    elif ahead:
                        choose(h + 1, t - 2)
                add_sums(h, NT - 1)

            dve.sem_inc(vsum_used, 2)
            add_mix(0)
            norm_x1(0)
            low_x1T(0)
            for u in range(2):
                dve.wait_ge(wq_rounded, u + 1)
                dve.tensor_tensor(wqs[1][:, u], w_q[:, u], wqs[0][:, u].bitcast(F32), ALU.subtract).then_inc(wq_split, 1)
            choose(0, 0, first=True)
            for t in range(1, NT + 2):
                if t < NT:
                    add_mix(t)
                if 1 <= t - 1 < NT:
                    norm_x1(t - 1)
                if 1 <= t - 2 < NT:
                    low_x1T(t - 2)
            dve.wait_ge(ln2_loaded, 32)
            experts(0, True, first=True)
            with dve.Fori(1, HEADS - 1) as h:
                experts(h, True)
            experts(HEADS - 1, False)
            out_variance(NT - 1)
            out_normalise(NT - 1)


def kernel(**inputs):
    import ml_dtypes
    import numpy as np
    import concourse.bacc as bacc
    from concourse import mybir as mb
    from concourse.bass_utils import run_bass_kernel_spmd

    a = {k: np.asarray(v) for k, v in inputs.items()}
    w_in = a["w_in"][0].reshape(KD, P, 7, ROUNDS, P).transpose(3, 2, 1, 0, 4)
    w_kv = a["w_mem_kv"][0].reshape(KD, P, 2, ROUNDS, P).transpose(3, 2, 1, 0, 4)
    w_gate = a["w_gate"][0].reshape(KD, P, NB, FT, P).transpose(3, 2, 1, 0, 4)
    w_br = np.stack([a["w_br_sb"][0], a["w_br_df"][0], a["w_br_mx"][0]])
    w_br = w_br.reshape(NB, ROUNDS, P, FT, P).transpose(3, 0, 2, 1, 4)
    arrays = {
        "xT": a["x"][0].T,
        "x": a["x"][0].reshape(NT, P, D).transpose(1, 0, 2),
        "memT": a["mem"][0].T.reshape(KD, P, M).transpose(1, 0, 2),
        "pos": a["positions"][0],
        "w_mix": np.concatenate([w_in, w_kv], axis=1).reshape(ROUNDS, SEGS, P, KD * P),
        "lam": a["df_lambda"][0].reshape(-1),
        "df_g": a["df_norm_g"][0].reshape(P, 1),
        "w_gate": w_gate.reshape(FT, NB, P, KD * P),
        "b_gate": a["b_gate"][0].reshape(NB, FT, P).transpose(2, 0, 1),
        "w_br": w_br,
        "w_out": a["w_out"][0].reshape(FT, P, D),
        "ln": np.stack([a["ln1_g"][0], a["ln1_b"][0], a["ln2_g"][0], a["ln2_b"][0]]),
        "w_query": a["w_query"][0].reshape(KD, P, HEADS, 2, P).transpose(2, 1, 3, 0, 4),
        "keysT": a["sub_keys"][0].transpose(0, 3, 1, 2),
        "uv": np.concatenate([a["u_tab"][0], a["v_tab"][0]], axis=1),
    }
    row, col = np.arange(P)[:, None], np.arange(P)[None, :]
    rope, half = HD // 4, HD // 8
    c = np.zeros((P, NCONST), np.float32)
    c[:, C_IDENT:C_IDENT + P] = row == col
    c[:, C_TRI:C_TRI + P] = -1.0 * (row >= col)
    c[:, C_ONES:C_ONES + P] = -1.0
    d = np.arange(P) % HD
    partner = np.where(d < half, np.arange(P) + half, np.arange(P) - half)
    c[:, C_PERM:C_PERM + P] = (row == partner[None, :]) & (d < rope)[None, :]
    freq = (500000.0 ** (-np.arange(0, rope, 2, dtype=np.float32) / rope)).astype(np.float32)
    c[:, C_INV] = np.where(d < rope, freq[d % half], 0.0)
    c[:, C_SIGN] = np.where(d < half, -1.0, np.where(d < rope, 1.0, 0.0))
    c[:, C_EPS] = RMS_EPS
    c[:, C_ONE] = 1.0
    c[:, C_IOTA:C_IOTA + TOPK] = np.arange(TOPK)
    arrays["const"] = c
    m = np.zeros((P, 3, P), np.float32)
    m[:, 0] = row == col
    m[:, 1] = -1e30 * (row >= col)
    m[:, 2] = -1e30 * (col > row)
    arrays["masks"] = m.astype(ml_dtypes.bfloat16)
    arrays = {f"in_{k}": np.ascontiguousarray(v) for k, v in arrays.items()}

    nc = bacc.Bacc("TRN2", target_bir_lowering=False, num_devices=1)
    args = [nc.dram_tensor(k, v.shape, mb.dt.from_np(v.dtype), kind="ExternalInput").ap() for k, v in arrays.items()]
    out = nc.dram_tensor("out", (P, NT, D), F32, kind="ExternalOutput").ap()
    build_layer(nc, *args, out)
    r = run_bass_kernel_spmd(nc, [arrays], core_ids=[0])
    return r.results[0]["out"].transpose(1, 0, 2).reshape(1, T, D)
```
